# Optimizing a Trainium2 kernel written in Bass

```python
import jax, jax.numpy as jnp
from jax import lax
import numpy as np

D_MODEL = 1024
BATCH = 1
SEQ = 2048
DEPTH = 1

CHUNK = 64
HEAD_DIM = 64
FOX_HEADS = 8
SWA_HEADS = 8
SWA_KV_HEADS = 2
WINDOW = 128
WINDOW_CHUNKS = WINDOW // CHUNK
Q_BLOCK = 128
FOX_WIDTH = FOX_HEADS * HEAD_DIM
SWA_WIDTH = SWA_HEADS * HEAD_DIM
SWA_KV_WIDTH = SWA_KV_HEADS * HEAD_DIM
SPLIT_SIZES = (FOX_WIDTH, FOX_WIDTH, FOX_WIDTH, FOX_HEADS, FOX_WIDTH,
               SWA_WIDTH, SWA_KV_WIDTH, SWA_KV_WIDTH, SWA_WIDTH,
               D_MODEL, D_MODEL)
D_IN = sum(SPLIT_SIZES)
EPS = 1e-6
NEG_INF = -1e30

kernel_name = "hybrid_fox_swa_gated_block"

def _rms_norm(x, g):
    xf = x.astype(jnp.float32)
    y = xf * lax.rsqrt(jnp.mean(xf * xf, axis=-1, keepdims=True) + EPS)
    return (y * g.astype(jnp.float32)).astype(x.dtype)

def _fox_attention(q, k, v, log_f):
    B, S, H, Dh = q.shape
    F = jnp.transpose(jnp.cumsum(log_f, axis=1), (0, 2, 1))
    scale = Dh ** -0.5
    outs = []
    for blk in range(S // Q_BLOCK):
        qs = blk * Q_BLOCK
        qe = qs + Q_BLOCK
        logits = jnp.einsum('bqhd,bkhd->bhqk', q[:, qs:qe], k[:, :qe]).astype(jnp.float32) * scale
        logits = logits + F[:, :, qs:qe, None] - F[:, :, None, :qe]
        causal = (qs + jnp.arange(Q_BLOCK))[:, None] >= jnp.arange(qe)[None, :]
        logits = jnp.where(causal, logits, NEG_INF)
        p = jax.nn.softmax(logits, axis=-1).astype(v.dtype)
        outs.append(jnp.einsum('bhqk,bkhd->bqhd', p, v[:, :qe]))
    return jnp.concatenate(outs, axis=1)

def _swa_attention(q, k, v, sinks):
    B, S, H, Dh = q.shape
    KVH = k.shape[2]
    G = H // KVH
    NC = S // CHUNK
    WK = WINDOW_CHUNKS * CHUNK
    qc = q.reshape(B, NC, CHUNK, KVH, G, Dh)

    def band(t):
        tc = t.reshape(B, NC, CHUNK, KVH, Dh)
        tp = jnp.pad(tc, ((0, 0), (WINDOW_CHUNKS - 1, 0), (0, 0), (0, 0), (0, 0)))
        return jnp.concatenate([tp[:, w:w + NC] for w in range(WINDOW_CHUNKS)], axis=2)

    kb, vb = band(k), band(v)
    logits = jnp.einsum('bcqhgd,bcshd->bchgqs', qc, kb).astype(jnp.float32) * (Dh ** -0.5)
    slopes = (2.0 ** (-8.0 * jnp.arange(1, H + 1, dtype=jnp.float32) / H)).reshape(KVH, G)
    qi = jnp.arange(CHUNK)[:, None]
    kj = jnp.arange(WK)[None, :]
    dist = jnp.abs((WINDOW_CHUNKS - 1) * CHUNK + qi - kj).astype(jnp.float32)
    logits = logits - slopes[:, :, None, None] * dist
    key_chunk = jnp.arange(NC)[:, None] - (WINDOW_CHUNKS - 1) + (jnp.arange(WK) // CHUNK)[None, :]
    valid = key_chunk >= 0
    logits = jnp.where(valid[None, :, None, None, None, :], logits, NEG_INF)
    sink = jnp.broadcast_to(sinks.astype(jnp.float32).reshape(KVH, G)[None, None, :, :, None, None],
                            logits.shape[:-1] + (1,))
    p = jax.nn.softmax(jnp.concatenate([logits, sink], axis=-1), axis=-1)[..., :WK]
    out = jnp.einsum('bchgqs,bcshd->bcqhgd', p.astype(v.dtype), vb)
    return out.reshape(B, S, H * Dh)

def setup_inputs(seed: int = 0) -> dict:
    key = jax.random.key(seed)
    ks = jax.random.split(key, 16)
    f32 = jnp.float32
    nrm = lambda k, shape, s: jax.random.normal(k, shape, f32) * s
    return {
        "x": nrm(ks[0], (BATCH, SEQ, D_MODEL), 1.0),
        "c": nrm(ks[1], (BATCH, D_MODEL), 1.0),
        "w_ada": nrm(ks[2], (DEPTH, D_MODEL, 3 * D_MODEL), 0.5 * D_MODEL ** -0.5),
        "b_ada": nrm(ks[3], (DEPTH, 3 * D_MODEL), 0.01),
        "norm_g": 1.0 + nrm(ks[4], (DEPTH, D_MODEL), 0.02),
        "w_in": nrm(ks[5], (DEPTH, D_MODEL, D_IN), D_MODEL ** -0.5),
        "b_forget": jax.random.uniform(ks[6], (DEPTH, FOX_HEADS), f32, 1.0, 4.0),
        "fox_q_g": 1.0 + nrm(ks[7], (DEPTH, HEAD_DIM), 0.02),
        "fox_k_g": 1.0 + nrm(ks[8], (DEPTH, HEAD_DIM), 0.02),
        "w_o_fox": nrm(ks[9], (DEPTH, FOX_WIDTH, D_MODEL), FOX_WIDTH ** -0.5),
        "swa_q_g": 1.0 + nrm(ks[10], (DEPTH, HEAD_DIM), 0.02),
        "swa_k_g": 1.0 + nrm(ks[11], (DEPTH, HEAD_DIM), 0.02),
        "swa_sinks": nrm(ks[12], (DEPTH, SWA_HEADS), 0.5),
        "w_o_swa": nrm(ks[13], (DEPTH, SWA_WIDTH, D_MODEL), SWA_WIDTH ** -0.5),
        "w_out": nrm(ks[14], (DEPTH, D_MODEL, D_MODEL), D_MODEL ** -0.5),
    }

def reference(x, c, w_ada, b_ada, norm_g, w_in, b_forget, fox_q_g, fox_k_g, w_o_fox,
              swa_q_g, swa_k_g, swa_sinks, w_o_swa, w_out):
    B, S, D = x.shape
    offsets = [int(o) for o in np.cumsum(SPLIT_SIZES)[:-1]]
    for layer in range(DEPTH):
        ada = jax.nn.silu(c) @ w_ada[layer] + b_ada[layer]
        shift, scale, gate = jnp.split(ada, 3, axis=-1)
        h = _rms_norm(x, norm_g[layer]) * (1.0 + scale[:, None, :]) + shift[:, None, :]
        proj = h @ w_in[layer]
        (qa, ka, va, fa, za, qb, kb, vb, zb, ga, gb) = jnp.split(proj, offsets, axis=-1)

        qa = _rms_norm(qa.reshape(B, S, FOX_HEADS, HEAD_DIM), fox_q_g[layer])
        ka = _rms_norm(ka.reshape(B, S, FOX_HEADS, HEAD_DIM), fox_k_g[layer])
        va = va.reshape(B, S, FOX_HEADS, HEAD_DIM)
        log_f = jax.nn.log_sigmoid(fa.astype(jnp.float32) + b_forget[layer].astype(jnp.float32))
        ya = _fox_attention(qa, ka, va, log_f).reshape(B, S, FOX_WIDTH)
        ya = (ya * jax.nn.silu(za)) @ w_o_fox[layer]

        qb = _rms_norm(qb.reshape(B, S, SWA_HEADS, HEAD_DIM), swa_q_g[layer])
        kb = _rms_norm(kb.reshape(B, S, SWA_KV_HEADS, HEAD_DIM), swa_k_g[layer])
        vb = vb.reshape(B, S, SWA_KV_HEADS, HEAD_DIM)
        yb = _swa_attention(qb, kb, vb, swa_sinks[layer])
        yb = (yb * jax.nn.silu(zb)) @ w_o_swa[layer]

        merged = jax.nn.sigmoid(ga) * ya + jax.nn.sigmoid(gb) * yb
        x = x + gate[:, None, :] * (merged @ w_out[layer])
    return x


_drawn_inputs = setup_inputs


def setup_inputs(seed=0):
    import zlib

    import numpy as np

    out = dict(_drawn_inputs(seed))
    spreads = {}
    factors = {'b_ada': 8.0,
     'norm_g': 8.0,
     'fox_q_g': 8.0,
     'fox_k_g': 8.0,
     'swa_q_g': 8.0,
     'swa_k_g': 8.0,
     'swa_sinks': 8.0}
    for name, (base, spread) in spreads.items():
        noise = np.random.default_rng([zlib.crc32(name.encode()), seed]).standard_normal(out[name].shape)
        drawn = base * np.exp(spread * noise) if base else spread * noise
        out[name] = __import__('jax').numpy.asarray(drawn.astype(out[name].dtype))
    for name, factor in factors.items():
        out[name] = (out[name] * factor).astype(out[name].dtype)
    return out
```

```python
from contextlib import ExitStack

import numpy as np
import concourse.bass as bass
from concourse import mybir
from concourse.alu_op_type import AluOpType as ALU

F32 = mybir.dt.float32
F32R = mybir.dt.float32r
ACT = mybir.ActivationFunctionType
AX = mybir.AxisListType

P = 128
D = 1024
S = 2048
KT = D // P
TT = S // P
HD = 64
FOX_H, SWA_H, KV_H = 8, 8, 2
FW, SW, KW = FOX_H * HD, SWA_H * HD, KV_H * HD
CHUNK = 64
COLS = 512
EPS = 1e-6
NEG = -1e30
QK_SCALE = HD ** -0.5

C_Q, C_K, C_V, C_F = 0, FW, 2 * FW, 3 * FW
C_ZA = C_F + FOX_H
C_QB = C_ZA + FW
C_KB = C_QB + SW
C_VB = C_KB + KW
C_ZB = C_VB + KW
C_GA = C_ZB + SW
C_GB = C_GA + D
D_IN = C_GB + D

R_Q, R_K, R_QB, R_KB = 0, FW, 2 * FW, 2 * FW + SW

class Steps:

    def __init__(self, eng, sem):
        self.eng, self.sem, self.n, self.local = eng, sem, 0, 0

    def did(self, ins):
        ins.then_inc(self.sem, 1)
        self.n = self.n + 1
        self.local += 1
        return ins

    def settle(self, ins):
        self.did(ins)
        self.eng.wait_ge(self.sem, self.n)

    def loop(self, i, per_iteration):
        self.base, self.per, self.local = self.n, per_iteration, 0
        self.n = self.n + i * per_iteration

    def end(self, iterations):
        assert self.local == self.per, (self.local, self.per)
        self.n = self.base + iterations * self.per

def identity(pool, tile, done):
    pool.memset(tile, 0.0).then_inc(done, 1)
    pool.wait_ge(done, 1)
    pool.affine_select(out=tile, in_=tile, compare_op=ALU.not_equal, fill=1.0, base=0,
                       pattern=[[-1, P]], channel_multiplier=1).then_inc(done, 1)

def condition_and_norm(nc, io, keep):
    ctx = ExitStack()
    sb = lambda name, shape, dt=F32: ctx.enter_context(nc.sbuf_tensor(name, shape, dt))
    sem = lambda name: ctx.enter_context(nc.semaphore(name))
    NADA = 2 * KT
    WR, XR = 3, 4
    with ctx:
        wada = [sb(f"wada{k}", [P, 2 * D]) for k in range(WR)]
        xin = [sb(f"xin{k}", [P, D]) for k in range(XR)]
        xn = [sb(f"xn{k}", [P, D]) for k in range(2)]
        hf = [sb(f"hf{k}", [P, KT, P]) for k in range(2)]
        c_raw, bias, ng = sb("c_raw", [P, KT]), sb("bias", [P, NADA]), sb("ng", [P, KT])
        acc, mulA = sb("acc", [P, NADA]), sb("mulA", [P, KT])
        ss, sd, rstd = sb("ss", [P, 2]), sb("sd", [P, 2]), sb("rstd", [P, 2])
        ps_ada = [ctx.enter_context(nc.psum_tensor(f"ps_ada{k}", [P, 512], F32)) for k in range(2)]
        ps_x = [ctx.enter_context(nc.psum_tensor(f"ps_x{k}", [P, KT, P], F32)) for k in range(2)]
        small_in, id_done, siluc_done = sem("p_small"), sem("p_id"), sem("p_siluc")
        wada_in = [sem(f"p_wada{k}") for k in range(WR)]
        x_in = [sem(f"p_x{k}") for k in range(XR)]
        ada_mm, ada_acc = sem("p_ada_mm"), sem("p_ada_acc")
        ab_ready = sem("p_ab")
        ss_done, var_done, sd_done, rstd_done, xn_done = (sem("p_" + n) for n in ("ss", "var", "sd", "rstd", "xn"))
        xt_done, mul_done, full_done, hi_done, lo_done = (sem("p_" + n) for n in ("xt", "mul", "full", "hi", "lo"))
        dve_steps = sem("p_dve")
        block = ctx.enter_context(nc.Block())

        @block.sync
        def _(sp):
            with nc.allow_non_contiguous_dma(reason="columns of small vectors"):
                sp.dma_start(c_raw[:], io["c"].rearrange("a (k p) -> p (a k)", p=P)).then_inc(small_in, 16)
                sp.dma_start(bias[:], io["b_ada"][:, 0:2 * D].rearrange("a (k p) -> p (a k)", p=P)).then_inc(small_in, 16)
                sp.dma_start(ng[:], io["norm_g"].rearrange("a (k p) -> p (a k)", p=P)).then_inc(small_in, 16)
            for k in range(KT):
                if k >= WR:
                    sp.wait_ge(ada_mm, k - WR + 1)
                sp.dma_start(wada[k % WR][:], io["w_ada"][0, k * P:(k + 1) * P, 0:2 * D]).then_inc(wada_in[k % WR], 16)
            for t in range(TT):
                if t >= XR:
                    sp.wait_ge(xn_done, t - XR + 1)
                sp.dma_start(xin[t % XR][:], io["x"][0, t * P:(t + 1) * P, :]).then_inc(x_in[t % XR], 16)

        @block.gpsimd
        def _(pool):
            identity(pool, keep["ident"][:], id_done)
            pool.wait_ge(ab_ready, 1)
            for t in range(TT):
                pool.wait_ge(mul_done, t + 1)
                pool.tensor_tensor(hf[t % 2][:], hf[t % 2][:], acc[:, 0:KT].unsqueeze(2).to_broadcast([P, KT, P]),
                                   ALU.add).then_inc(full_done, 1)

        @block.tensor
        def _(pe):
            pe.wait_ge(siluc_done, 1)
            for k in range(KT):
                pe.wait_ge(wada_in[k % WR], 16 * (k // WR + 1))
                if k >= 2:
                    pe.wait_ge(ada_acc, k - 1)
                for m in range(NADA):
                    mm = nc.tensor.matmul(ps_ada[k % 2][:, m:m + 1], wada[k % WR][:, m * P:(m + 1) * P],
                                          keep["siluc"][:, k:k + 1], start=True, stop=True)
                mm.then_inc(ada_mm, 1)
            pe.wait_ge(id_done, 2)
            for t in range(TT):
                pe.wait_ge(xn_done, t + 1)
                if t >= 2:
                    pe.wait_ge(mul_done, t - 1)
                for k in range(KT):
                    mm = nc.tensor.transpose(ps_x[t % 2][:, k, :], xn[t % 2][:, k * P:(k + 1) * P], keep["ident"][:])
                mm.then_inc(xt_done, 1)

        @block.scalar
        def _(act):
            act.wait_ge(small_in, 48)
            nc.scalar.activation(keep["siluc"][:], c_raw[:], ACT.Silu).then_inc(siluc_done, 1)

            def high(t):
                act.wait_ge(full_done, t + 1)
                nc.scalar.activation(keep["hTh"][:, :, t * P:(t + 1) * P], hf[t % 2][:], ACT.Copy).then_inc(hi_done, 1)

            for t in range(TT):
                act.wait_ge(x_in[t % XR], 16 * (t // XR + 1))
                if t >= 2:
                    act.wait_ge(xt_done, t - 1)
                    act.wait_ge(var_done, t - 1)
                nc.scalar.activation(xn[t % 2][:], xin[t % XR][:], ACT.Square,
                                     accum_out=ss[:, t % 2:t % 2 + 1]).then_inc(ss_done, 1)
                act.wait_ge(var_done, t + 1)
                nc.scalar.activation(sd[:, t % 2:t % 2 + 1], rstd[:, t % 2:t % 2 + 1], ACT.Sqrt).then_inc(sd_done, 1)
                act.wait_ge(rstd_done, t + 1)
                nc.scalar.activation(xn[t % 2][:], xin[t % XR][:], ACT.Copy,
                                     scale=rstd[:, t % 2:t % 2 + 1]).then_inc(xn_done, 1)
                if t >= 1:
                    high(t - 1)
            high(TT - 1)

        @block.vector
        def _(dve):
            st = Steps(dve, dve_steps)
            for k in range(KT):
                dve.wait_ge(ada_mm, k + 1)
                if k == 0:
                    nc.vector.tensor_tensor(acc[:], ps_ada[0][:, 0:NADA], bias[:], ALU.add).then_inc(ada_acc, 1)
                else:
                    dve.wait_ge(ada_acc, k)
                    nc.vector.tensor_tensor(acc[:], ps_ada[k % 2][:, 0:NADA], acc[:], ALU.add).then_inc(ada_acc, 1)
            dve.wait_ge(ada_acc, KT)
            st.settle(nc.vector.tensor_scalar(mulA[:], acc[:, KT:NADA], 1.0, None, ALU.add))
            st.settle(nc.vector.tensor_tensor(mulA[:], mulA[:], ng[:], ALU.mult))
            nc.vector.engine_nop().then_inc(ab_ready, 1)

            def low(t):
                dve.wait_ge(hi_done, t + 1)
                high = keep["hTh"][:, :, t * P:(t + 1) * P]
                nc.vector.tensor_tensor(keep["hTl"][:, :, t * P:(t + 1) * P], hf[t % 2][:], high.bitcast(F32),
                                        ALU.subtract).then_inc(lo_done, 1)

            for t in range(TT):
                v = rstd[:, t % 2:t % 2 + 1]
                dve.wait_ge(ss_done, t + 1)
                if t >= 2:
                    dve.wait_ge(xn_done, t - 1)
                nc.vector.tensor_scalar(v, ss[:, t % 2:t % 2 + 1], 1.0 / D, EPS, ALU.mult, ALU.add).then_inc(var_done, 1)
                dve.wait_ge(sd_done, t + 1)
                nc.vector.reciprocal(v, sd[:, t % 2:t % 2 + 1]).then_inc(rstd_done, 1)
                dve.wait_ge(xt_done, t + 1)
                if t >= 2:
                    dve.wait_ge(lo_done, t - 1)
                nc.vector.tensor_tensor(hf[t % 2][:], ps_x[t % 2][:], mulA[:].unsqueeze(2).to_broadcast([P, KT, P]),
                                        ALU.mult).then_inc(mul_done, 1)
                if t >= 1:
                    low(t - 1)
            low(TT - 1)

def project(nc, io, keep, dram):
    ctx = ExitStack()
    sb = lambda name, shape, dt=F32: ctx.enter_context(nc.sbuf_tensor(name, shape, dt))
    sem = lambda name: ctx.enter_context(nc.semaphore(name))
    hTh, hTl = keep["hTh"], keep["hTl"]
    RAW, BANKS, ST = 4, 4, 4
    NT = S // COLS
    N_NORM, N_Z, N_G = 3, 2, 2 * D // COLS
    G_NORM = 0
    G_KV = G_NORM + N_NORM
    G_V = G_KV + 1
    G_Z = G_V + 1
    G_G = G_Z + N_Z
    G_F = G_G + N_G
    DVE_TILES = TT * G_G
    with ctx:
        wraw = [sb(f"wraw{k}", [P, COLS]) for k in range(RAW)]
        Wh, Wl = sb("Wh", [P, KT, COLS], F32R), sb("Wl", [P, KT, COLS], F32R)
        st = [sb(f"st{k}", [P, COLS]) for k in range(ST)]
        qn = [sb(f"qn{k}", [P, COLS]) for k in range(2)]
        qT = [sb(f"qT{k}", [P, COLS]) for k in range(2)]
        sq = sb("sq", [P, COLS])
        var, sd, rs = sb("var", [P, 2, FOX_H]), sb("nsd", [P, 2, FOX_H]), sb("nrs", [P, 2, FOX_H])
        gains = sb("gains", [P, 4, HD])
        bf, one = sb("bf", [FOX_H, 1]), sb("one", [FOX_H, 1])
        fu, fl = sb("fu", [FOX_H, COLS]), sb("fl", [FOX_H, COLS])
        fc = [t[0:FOX_H, :] for t in (*qn, *qT)]
        wg = [sb(f"wg{k}", [P, D]) for k in range(4)]
        bg, gacc = sb("bg", [P, KT]), sb("gacc", [P, KT])
        bank = [ctx.enter_context(nc.psum_tensor(f"pj{k}", [P, COLS], F32)) for k in range(BANKS)]
        tbank = [ctx.enter_context(nc.psum_tensor(f"pt{k}", [P, 4, P], F32)) for k in range(2)]
        gbank = [ctx.enter_context(nc.psum_tensor(f"pg{k}", [P, 512], F32)) for k in range(2)]
        small_in, credits = sem("j_small"), sem("j_credits")
        w_in = [sem(f"j_w{k}") for k in range(RAW)]
        w_hi, w_split, w_free = sem("j_whi"), sem("j_wsplit"), sem("j_wfree")
        mm_done, dve_free, act_free = sem("j_mm"), sem("j_dfree"), sem("j_afree")
        sq_done, var_done, sd_done, qn_done = sem("j_sq"), sem("j_var"), sem("j_sd"), sem("j_qn")
        qt_done, qT_done = sem("j_qt"), sem("j_qTd")
        qT_stored = [sem(f"j_qs{k}") for k in range(2)]
        st_dve, st_act = sem("j_std"), sem("j_sta")
        stored = [sem(f"j_st{k}") for k in range(ST)]
        sig_done, ln_done, f_done, f_stored = sem("j_sig"), sem("j_ln"), sem("j_f"), sem("j_fs")
        wg_in = [sem(f"j_wg{k}") for k in range(4)]
        g_mm, g_acc, g_stored = sem("j_gmm"), sem("j_gacc"), sem("j_gs")
        gains_ready = sem("j_gains")
        act_steps, dve_steps = sem("j_act"), sem("j_dve")
        block = ctx.enter_context(nc.Block())

        def norm_loop(eng, body):
            with eng.Fori(0, N_NORM) as i:
                body(i)

        @block.gpsimd
        def _(pool):
            pool.sem_inc(w_split, RAW)

            def load(g, col0):
                for k in range(KT):
                    n = g * KT + k
                    pool.wait_ge(w_split, n + 1)
                    pool.dma_start(wraw[k % RAW][:], io["w_in"][0, k * P:(k + 1) * P, bass.ds(col0, COLS)]
                                   ).then_inc(w_in[k % RAW], 16)

            with pool.Fori(0, N_NORM) as i:
                load(i + G_NORM, i * COLS + i // 2 * (C_QB - 2 * COLS))
            load(G_KV, C_KB)
            load(G_V, C_V)
            with pool.Fori(0, N_Z) as i:
                load(i + G_Z, i * (C_ZB - C_ZA) + C_ZA)
            with pool.Fori(0, N_G) as i:
                load(i + G_G, i * COLS + C_GA)
            load(G_F, C_F)

        @block.sync
        def _(sp):
            for n, name in enumerate(("fox_q_g", "fox_k_g", "swa_q_g", "swa_k_g")):
                sp.dma_start(gains[:, n, :], io[name].to_broadcast([P, HD])).then_inc(small_in, 16)
            with nc.allow_non_contiguous_dma(reason="columns of small vectors"):
                sp.dma_start(bf[:], io["b_forget"].rearrange("a h -> h a")).then_inc(small_in, 16)
                sp.dma_start(bg[:], io["b_ada"][:, 2 * D:3 * D].rearrange("a (k p) -> p (a k)", p=P)).then_inc(small_in, 16)

            def store_norm(g, row0, heads):
                for t in range(TT):
                    sp.wait_ge(qT_done, g * TT + t + 2 + 1)
                    sp.dma_start(dram["qk"][bass.ds(row0, heads * HD), t * P:(t + 1) * P]
                                 .rearrange("(b p) n -> p b n", p=P),
                                 qT[t % 2][:, 0:heads * HD].rearrange("p (b n) -> p b n", n=P)
                                 ).then_inc(qT_stored[t % 2], 16)
            with sp.Fori(0, N_NORM) as i:
                store_norm(i, i * COLS + R_Q, FOX_H)
            for t in range(TT):
                sp.wait_ge(qT_done, N_NORM * TT + t + 2 + 1)
                sp.dma_start(dram["qk"][R_KB:R_KB + KW, t * P:(t + 1) * P], qT[t % 2][:, 0:P]).then_inc(qT_stored[t % 2], 16)
                sp.wait_ge(st_dve, t + 1)
                sp.dma_start(dram["v"][t * P:(t + 1) * P, FW:FW + KW], st[t % ST][:, 0:KW]).then_inc(stored[t % ST], 16)
            for t in range(TT):
                sp.wait_ge(st_dve, TT + t + 1)
                sp.dma_start(dram["v"][t * P:(t + 1) * P, 0:FW], st[t % ST][:]).then_inc(stored[t % ST], 16)
            with sp.Fori(0, N_Z) as i:
                for t in range(TT):
                    sp.wait_ge(st_dve, i * TT + (2 * TT + t + 1))
                    sp.dma_start(dram["z"][t * P:(t + 1) * P, bass.ds(i * COLS, COLS)], st[t % ST][:]).then_inc(stored[t % ST], 16)
            with sp.Fori(0, N_G) as i:
                for t in range(TT):
                    m, b = t // NT, t % NT
                    sp.wait_ge(st_act, i * TT + (t + 1))
                    sp.dma_start(dram["g"][bass.ds(i * COLS + m * P, P), b * COLS:(b + 1) * COLS], st[t % ST][:]).then_inc(stored[t % ST], 16)
            for k in range(KT):
                if k >= 4:
                    sp.wait_ge(g_mm, k - 3)
                sp.dma_start(wg[k % 4][:], io["w_ada"][0, k * P:(k + 1) * P, 2 * D:3 * D]).then_inc(wg_in[k % 4], 16)
                if k == 3:
                    for b in range(NT):
                        sp.wait_ge(f_done, b + 1)
                        sp.dma_start(dram["f"][:, b * COLS:(b + 1) * COLS], fc[b]).then_inc(f_stored, 16)
            sp.wait_ge(g_acc, KT)
            with nc.allow_non_contiguous_dma(reason="column to row of a small vector"):
                sp.dma_start(dram["gate"].rearrange("a (k p) -> p (a k)", p=P), gacc[:]).then_inc(g_stored, 16)
            sp.wait_ge(g_stored, 16)
            sp.wait_ge(f_stored, 16 * NT)
            for k in range(2):
                sp.wait_ge(qT_stored[k], 16 * (N_NORM + 1) * TT // 2 + 16)
            for k in range(ST):
                sp.wait_ge(stored[k], 16 * (2 + N_Z + N_G) * TT // ST)

        @block.tensor
        def _(pe):
            pe.sem_inc(w_free, KT - 1)
            pe.sem_inc(qt_done, 2)

            def three(out, a_hi, a_lo, b_hi, b_lo, first, last):
                nc.tensor.matmul(out, a_hi, b_hi, start=first, stop=False)
                nc.tensor.matmul(out, a_hi, b_lo, start=False, stop=False)
                return nc.tensor.matmul(out, a_lo, b_hi, start=False, stop=last)

            def tile(g, t, tiles, free_sem, free_at, operands, width):
                pe.wait_ge(free_sem, free_at)
                for k in range(KT):
                    if t == 0:
                        pe.wait_ge(w_split, g * KT + k + 1 + RAW)
                    mm = three(bank[t % BANKS][:, 0:width], *operands(k), k == 0, k == KT - 1)
                    if t == tiles - 1 and k < KT - 1:
                        mm.then_inc(w_free, 1)
                mm.then_inc(mm_done, 1)

            def tokens_by_cols(t, width):
                tok = slice(t * P, (t + 1) * P)
                return lambda k: (hTh[:, k, tok], hTl[:, k, tok], Wh[:, k, 0:width], Wl[:, k, 0:width])

            def cols_by_tokens(m, b):
                c, tok = slice(m * P, (m + 1) * P), slice(b * COLS, (b + 1) * COLS)
                return lambda k: (Wh[:, k, c], Wl[:, k, c], hTh[:, k, tok], hTl[:, k, tok])

            def flip(g, t, heads):
                pe.wait_ge(qn_done, g * TT + t + 1)
                pe.wait_ge(qT_done, g * TT + t + 1)
                for b in range(heads * HD // P):
                    mm = nc.tensor.transpose(tbank[t % 2][:, b, :], qn[t % 2][:, b * P:(b + 1) * P], keep["ident"][:])
                mm.then_inc(qt_done, 1)

            def norm_group(g, heads):
                for t in range(TT):
                    tile(g, t, TT, dve_free, g * TT + t + 1, tokens_by_cols(t, heads * HD if heads == FOX_H else 2 * KW),
                         heads * HD if heads == FOX_H else 2 * KW)
                    if t >= 2:
                        flip(g, t - 2, heads)
                flip(g, TT - 2, heads)
                flip(g, TT - 1, heads)

            def plain_group(g):
                for t in range(TT):
                    tile(g, t, TT, dve_free, g * TT + t + 1, tokens_by_cols(t, COLS), COLS)

            with pe.Fori(0, N_NORM) as i:
                norm_group(i, FOX_H)
            norm_group(G_KV, KV_H)
            plain_group(G_V)
            with pe.Fori(0, N_Z) as i:
                plain_group(i + G_Z)
            pe.wait_ge(dve_free, DVE_TILES + BANKS)
            with pe.Fori(0, N_G) as i:
                for t in range(TT):
                    tile(i + G_G, t, TT, act_free, i * TT + (t + 1), cols_by_tokens(t // NT, t % NT), COLS)
            for t in range(NT):
                tile(G_F, t, NT, act_free, N_G * TT + t + 1, cols_by_tokens(0, t), COLS)
            for k in range(KT):
                pe.wait_ge(wg_in[k % 4], 16 * (k // 4 + 1))
                if k >= 2:
                    pe.wait_ge(g_acc, k - 1)
                for m in range(KT):
                    mm = nc.tensor.matmul(gbank[k % 2][:, m:m + 1], wg[k % 4][:, m * P:(m + 1) * P],
                                          keep["siluc"][:, k:k + 1], start=True, stop=True)
                mm.then_inc(g_mm, 1)

        @block.scalar
        def _(act):
            act.sem_inc(qT_done, 2)
            act.sem_inc(act_free, BANKS)
            act.sem_inc(qT_stored[0], 16)
            act.sem_inc(qT_stored[1], 16)

            def split_high(g, first=False):
                for k in range(KT):
                    act.wait_ge(w_in[k % RAW], g * (16 * KT // RAW) + 16 * (k // RAW + 1))
                    if k < KT - 1:
                        act.wait_ge(w_free, g * (KT - 1) + (k + 1))
                    elif not first:
                        act.wait_ge(mm_done, g * TT)
                    nc.scalar.activation(Wh[:, k, :], wraw[k % RAW][:], ACT.Copy).then_inc(w_hi, 1)

            def squares(g, t, heads):
                w = heads * HD
                n = g * TT + t
                act.wait_ge(mm_done, n + 1)
                act.wait_ge(var_done, n + 1)
                nc.scalar.activation(sq[:, 0:w], bank[t % BANKS][:, 0:w], ACT.Square).then_inc(sq_done, 1)
                act.wait_ge(var_done, n + 2)
                nc.scalar.activation(sd[:, t % 2, 0:heads], var[:, t % 2, 0:heads], ACT.Sqrt).then_inc(sd_done, 1)

            def copy_out(g, t, heads):
                w = heads * HD
                act.wait_ge(qt_done, g * TT + t + 2 + 1)
                act.wait_ge(qT_stored[t % 2], g * (8 * TT) + 16 * (t // 2 + 1))
                nc.scalar.activation(qT[t % 2][:, 0:w], tbank[t % 2][:, 0:w // P, :].rearrange("p b n -> p (b n)"),
                                     ACT.Copy).then_inc(qT_done, 1)

            def norm_group(g, heads):
                for t in range(TT):
                    if t == TT - 1:
                        split_high(g + 1)
                    squares(g, t, heads)
                    if t >= 2:
                        copy_out(g, t - 2, heads)
                copy_out(g, TT - 2, heads)
                copy_out(g, TT - 1, heads)

            split_high(0, first=True)
            with act.Fori(0, N_NORM) as i:
                norm_group(i, FOX_H)
            norm_group(G_KV, KV_H)
            split_high(G_Z)
            with act.Fori(0, N_Z) as i:
                for t in range(TT):
                    if t == TT - 1:
                        split_high(i + (G_Z + 1))
                    act.wait_ge(mm_done, i * TT + (G_Z * TT + t + 1))
                    act.wait_ge(stored[t % ST], i * (16 * TT // ST) + 16 * (2 * TT // ST + t // ST))
                    nc.scalar.activation(st[t % ST][:], bank[t % BANKS][:], ACT.Sigmoid).then_inc(sig_done, 1)
            with act.Fori(0, N_G) as i:
                for t in range(TT):
                    if t == TT - 1:
                        split_high(i + (G_G + 1))
                    act.wait_ge(mm_done, i * TT + (G_G * TT + t + 1))
                    act.wait_ge(stored[t % ST], i * (16 * TT // ST) + 16 * ((2 + N_Z) * TT // ST + t // ST))
                    nc.scalar.activation(st[t % ST][:], bank[t % BANKS][:], ACT.Sigmoid).then_inc(st_act, 1)
                    act.wait_ge(st_act, i * TT + (t + 1))
                    act.sem_inc(act_free, 1)
            steps = Steps(act, act_steps)
            act.wait_ge(small_in, 96)
            for b in range(NT):
                act.wait_ge(mm_done, (G_F * TT) + b + 1)
                if b >= 1:
                    act.wait_ge(f_done, b)
                steps.did(nc.scalar.activation(fu[:], bank[b % BANKS][0:FOX_H, :], ACT.Identity, bias=bf[:, 0:1]))
                steps.settle(nc.scalar.activation(fl[:], bank[b % BANKS][0:FOX_H, :], ACT.Abs, bias=bf[:, 0:1]))
                act.sem_inc(act_free, 1)
                steps.settle(nc.scalar.activation(fl[:], fl[:], ACT.Exp, scale=-1.0))
                nc.scalar.activation(fl[:], fl[:], ACT.Ln, bias=1.0).then_inc(ln_done, 1)

        @block.vector
        def _(dve):
            dve.sem_inc(dve_free, BANKS)
            dve.sem_inc(var_done, 1)
            steps = Steps(dve, dve_steps)

            def split_low(g):
                for k in range(KT):
                    n = g * KT + k
                    dve.wait_ge(w_hi, n + 1)
                    nc.vector.tensor_tensor(Wl[:, k, :], wraw[k % RAW][:], Wh[:, k, :].bitcast(F32),
                                            ALU.subtract).then_inc(w_split, 1)

            def normalise(g, t, heads, gain, copy_v):
                w, u = heads * HD, t % 2
                n = g * TT + t
                by_head = lambda ap: ap[:, 0:w].rearrange("p (h d) -> p h d", d=HD)
                dve.wait_ge(sq_done, n + 1)
                steps.settle(nc.vector.tensor_reduce(var[:, u, 0:heads], by_head(sq), AX.X, ALU.add))
                nc.vector.tensor_scalar(var[:, u, 0:heads], var[:, u, 0:heads], 1.0 / HD, EPS, ALU.mult, ALU.add
                                        ).then_inc(var_done, 1)
                if copy_v:
                    if t >= ST:
                        dve.wait_ge(stored[t % ST], 16 * (t // ST))
                    nc.vector.tensor_copy(st[t % ST][:, 0:KW], bank[t % BANKS][:, KW:2 * KW]).then_inc(st_dve, 1)
                dve.wait_ge(sd_done, n + 1)
                steps.settle(nc.vector.reciprocal(rs[:, u, 0:heads], sd[:, u, 0:heads]))
                dve.wait_ge(qt_done, n + 1)
                nc.vector.tensor_tensor(by_head(qn[u]), by_head(bank[t % BANKS]),
                                        rs[:, u, 0:heads].unsqueeze(2).to_broadcast([P, heads, HD]), ALU.mult
                                        ).then_inc(dve_free, 1)
                dve.wait_ge(dve_free, n + 1 + BANKS)
                nc.vector.tensor_tensor(by_head(qn[u]), by_head(qn[u]),
                                        gains[:, bass.ds(gain, 1), :].to_broadcast([P, heads, HD]), ALU.mult
                                        ).then_inc(qn_done, 1)

            split_low(0)
            dve.wait_ge(small_in, 96)
            for n in (0, 2):
                nc.vector.tensor_scalar(gains[:, n, :], gains[:, n, :], QK_SCALE, None, ALU.mult).then_inc(gains_ready, 1)
            dve.wait_ge(gains_ready, 2)
            with dve.Fori(0, N_NORM) as i:
                steps.loop(i, 2 * TT)
                for t in range(TT):
                    if t == TT - 1:
                        split_low(i + 1)
                    normalise(i, t, FOX_H, i, False)
            steps.end(N_NORM)
            for t in range(TT):
                if t == TT - 1:
                    split_low(G_V)
                normalise(G_KV, t, KV_H, 3, True)
            for t in range(TT):
                if t == TT - 1:
                    split_low(G_Z)
                dve.wait_ge(mm_done, G_V * TT + t + 1)
                dve.wait_ge(stored[t % ST], 16 * (TT // ST + t // ST))
                nc.vector.tensor_copy(st[t % ST][:], bank[t % BANKS][:]).then_inc(dve_free, 1)
                dve.wait_ge(dve_free, G_V * TT + t + 1 + BANKS)
                dve.sem_inc(st_dve, 1)
            with dve.Fori(0, N_Z) as i:
                for t in range(TT):
                    if t == TT - 1:
                        split_low(i + (G_Z + 1))
                    dve.wait_ge(sig_done, i * TT + (t + 1))
                    nc.vector.tensor_tensor(st[t % ST][:], st[t % ST][:], bank[t % BANKS][:], ALU.mult).then_inc(dve_free, 1)
                    dve.wait_ge(dve_free, i * TT + (G_Z * TT + t + 1 + BANKS))
                    dve.sem_inc(st_dve, 1)
            with dve.Fori(0, N_G) as i:
                split_low(i + (G_G + 1))
            steps.settle(nc.vector.memset(one[:], 1.0))
            dve.wait_ge(qt_done, G_V * TT + 2)
            for k in range(2):
                dve.wait_ge(qT_stored[k], 16 * (G_V * TT // 2) + 16)
            for b in range(NT):
                dve.wait_ge(ln_done, b + 1)
                steps.settle(nc.vector.tensor_scalar(fu[:], fu[:], 0.0, None, ALU.min))
                steps.settle(nc.vector.tensor_tensor(fu[:], fl[:], fu[:], ALU.subtract))
                nc.vector.tensor_tensor_scan(fc[b], one[:].to_broadcast([FOX_H, COLS]), fu[:],
                                             fc[b - 1][:, COLS - 1:COLS] if b else 0.0,
                                             ALU.mult, ALU.add).then_inc(f_done, 1)
                dve.wait_ge(f_done, b + 1)
            for k in range(KT):
                dve.wait_ge(g_mm, k + 1)
                if k >= 1:
                    dve.wait_ge(g_acc, k)
                nc.vector.tensor_tensor(gacc[:], gbank[k % 2][:, 0:KT], gacc[:] if k else bg[:], ALU.add).then_inc(g_acc, 1)

_INS = ["x", "c", "w_ada", "b_ada", "norm_g", "w_in", "b_forget", "fox_q_g", "fox_k_g", "w_o_fox",
        "swa_q_g", "swa_k_g", "swa_sinks", "w_o_swa", "w_out"]

def attend(nc, io, keep, dram):
    ctx = ExitStack()
    sb = lambda name, shape, dt=F32: ctx.enter_context(nc.sbuf_tensor(name, shape, dt))
    sem = lambda name: ctx.enter_context(nc.semaphore(name))
    yT = keep["yT"]
    QUAD = 4
    HALF = 1024
    with ctx:
        raw = {"q": sb("raw_q", [P, S]), "k": sb("raw_k", [P, S])}
        Q = [sb(f"Q{k}", [P, S], F32R) for k in range(2)]
        Kh = [sb(f"Kh{k}", [P, S], F32R) for k in range(2)]
        Kl = [sb(f"Kl{k}", [P, S], F32R) for k in range(2)]
        V = [sb(f"V{k}", [P, TT, 2 * HD]) for k in range(2)]
        ZY = [sb(f"ZY{k}", [P, TT, 2 * HD]) for k in range(2)]
        Sn = [sb(f"Sn{k}", [P, S]) for k in range(2)]
        PT = [sb(f"PT{k}", [P, 4 * P]) for k in range(4)]
        nF = [sb(f"nF{k}", [P, S]) for k in range(2)]
        identr, maskr = sb("identr", [P, P], F32R), sb("maskr", [P, P], F32R)
        mask0 = sb("mask0", [P, P])
        nmax, rsum, rinv = sb("nmax", [P, 4]), sb("rsum", [P, 2]), sb("rinv", [P, 2])
        sinks = sb("sinks", [P, SWA_H])
        alibi = [nF[0][:, 0:QUAD * 2 * P].rearrange("p (h n) -> p h n", h=QUAD),
                 nF[1][:, 0:2 * P]]
        logits = [ctx.enter_context(nc.psum_tensor(f"lg{k}", [P, HALF], F32)) for k in range(2)]
        flips = [ctx.enter_context(nc.psum_tensor(f"fl{k}", [P, 4 * P], F32)) for k in range(2)]
        outs = [ctx.enter_context(nc.psum_tensor(f"ot{k}", [P, 512], F32)) for k in range(2)]

        def part(tag, swa):
            s = lambda name: sem(f"{tag}_{name}")
            raw_in, split_done = {x: s("raw" + x) for x in "qk"}, {x: s("split" + x) for x in "qk"}
            hi_done = s("hi")
            bias_in, vz_in = [s("bias0"), s("bias1")], [s("vz0"), s("vz1")]
            row_scored, chunk_ready, chunk_read = s("scored"), s("cready"), s("cread")
            exp_done, flip_done, copy_act, copy_dve = s("exp"), s("flip"), s("cact"), s("cdve")
            pv_group, y_done, yt_flip, yt_done = s("pvg"), s("y"), s("ytf"), s("yt")
            bias_used, init = s("bused"), s("init")
            act_steps, dve_steps, pool_steps = s("act"), s("dve"), s("pool")
            ITER = (SWA_H if swa else FOX_H) // QUAD

            rows, chunks, groups = [], [], []
            for hh in range(QUAD):
                for qb in range(TT):
                    first = max(0, qb - 1) if swa else 0
                    rows.append((hh, qb, first))
            n_act = n_dve = n_pt = 0
            row_chunks, row_groups, yt_at = [], [], {}
            for r, (hh, qb, first) in enumerate(rows):
                width = (qb + 1 - first) * P
                row_chunks.append([(len(chunks) + j, c, min(HALF, width - c)) for j, c in enumerate(range(0, width, HALF))])
                chunks += row_chunks[-1]
                mine = []
                blocks = list(range(first, qb + 1))
                for b in range(0, len(blocks), 4):
                    on_dve = (n_pt % 4 == 3) if not swa else (n_pt % 2 == 1)
                    mine.append((len(groups), blocks[b:b + 4], on_dve, n_dve if on_dve else n_act, n_pt))
                    groups.append((on_dve, n_dve if on_dve else n_act))
                    n_dve, n_act, n_pt = n_dve + on_dve, n_act + (not on_dve), n_pt + 1
                row_groups.append(mine)
                if r > 0 and rows[r - 1][0] % 2 == 1:
                    yt_at[r - 1] = (len(groups), n_act)
                    groups.append((False, n_act))
                    n_act += 1
            yt_at[len(rows) - 1] = (len(groups), n_act)
            groups.append((False, n_act))
            n_act += 1
            NR, NCH, NG = len(rows), len(chunks), len(groups)
            NYT = len(yt_at)
            yt_order = {r: n for n, r in enumerate(sorted(yt_at))}
            assert NCH % 2 == 0 and n_pt % 4 == 0

            def until(eng, sm, i, per, count):
                assert count > -per
                eng.wait_ge(sm, i * per + (per + count))

            def flip_bank_free(pe, i, order):
                on_dve, n = groups[order - 2]
                sm, per = (copy_dve, n_dve) if on_dve else (copy_act, n_act)
                until(pe, sm, i, per, n + 1 - (per if order < 2 else 0))

            block = ctx2.enter_context(nc.Block())

            @block.sync
            def _(sp):
                if swa:
                    sp.dma_start(sinks[:], io["swa_sinks"].to_broadcast([P, SWA_H])).then_inc(bias_in[0], 16)
                for i in range(ITER):
                    for hh in range(QUAD):
                        pair = hh // 2
                        for x in "qk":
                            if x == "k" and swa and hh:
                                continue
                            per = QUAD if x == "q" or not swa else 1
                            until(sp, split_done[x], i, per, hh)
                            row0 = (i * (QUAD * HD) + (hh * HD + (R_QB if swa else R_Q)) if x == "q" else
                                    i * HD + R_KB if swa else i * (QUAD * HD) + (hh * HD + R_K))
                            for half in range(2):
                                sp.dma_start(raw[x][half * HD:(half + 1) * HD, :], dram["qk"][bass.ds(row0, HD), :]
                                             ).then_inc(raw_in[x], 16)
                        if not swa:
                            until(sp, bias_used, i, QUAD, hh - 1)
                            sp.dma_start(nF[hh % 2][:], dram["f"][bass.ds(i * QUAD + hh, 1), :].to_broadcast([P, S])
                                         ).then_inc(bias_in[hh % 2], 16)
                        if hh % 2 == 0:
                            vcol = i * HD + FW if swa else i * (QUAD * HD) + pair * 2 * HD
                            zcol = i * (QUAD * HD) + ((FW if swa else 0) + pair * 2 * HD)
                            until(sp, pv_group, i, n_pt, (pair - 1) * n_pt // 2 if not swa or pair else 0)
                            until(sp, yt_done, i, NYT, (pair - 1) * NYT // 2)
                            if swa:
                                if hh == 0:
                                    sp.dma_start(V[0][:, :, 0:HD], dram["v"][:, bass.ds(vcol, HD)]
                                                 .rearrange("(t p) n -> p t n", p=P)).then_inc(vz_in[0], 16)
                            else:
                                sp.dma_start(V[pair][:], dram["v"][:, bass.ds(vcol, 2 * HD)]
                                             .rearrange("(t p) n -> p t n", p=P)).then_inc(vz_in[pair], 16)
                            sp.dma_start(ZY[pair][:], dram["z"][:, bass.ds(zcol, 2 * HD)]
                                         .rearrange("(t p) n -> p t n", p=P)).then_inc(vz_in[pair], 16)

            @block.gpsimd
            def _(pool):
                pool.sem_inc(split_done["q"], QUAD)
                pool.sem_inc(split_done["k"], 1 if swa else QUAD)
                if not swa:
                    pool.memset(mask0[:], 0.0).then_inc(init, 1)
                    pool.wait_ge(init, 1)
                    pool.affine_select(out=mask0[:], in_=mask0[:], compare_op=ALU.is_ge, fill=NEG, base=0,
                                       pattern=[[-1, P]], channel_multiplier=1).then_inc(init, 1)
                else:
                    dist = alibi[1]
                    pool.iota(dist.bitcast(mybir.dt.int32), pattern=[[-1, 2 * P]], base=P, channel_multiplier=1).then_inc(init, 1)
                    pool.wait_ge(init, 1)
                with pool.Fori(0, ITER) as i:
                    for hh in range(QUAD):
                        u = hh % 2
                        pool.wait_ge(hi_done, i * (QUAD + (1 if swa else QUAD)) + (hh + (1 if swa else hh) + 1 if hh or not swa else 1))
                        pool.tensor_tensor(Q[u][HD:P, :], raw["q"][HD:P, :], Q[u][HD:P, :].bitcast(F32), ALU.subtract
                                           ).then_inc(split_done["q"], 1)
                        until(pool, split_done["q"], i, QUAD, hh + 1)
                        if swa and hh:
                            continue
                        pool.wait_ge(hi_done, i * (QUAD + (1 if swa else QUAD)) + (2 * hh + 2))
                        pool.tensor_tensor(Kl[u][:], raw["k"][:], Kh[u][:].bitcast(F32), ALU.subtract
                                           ).then_inc(split_done["k"], 1)
                        until(pool, split_done["k"], i, *((1, 1) if swa else (QUAD, hh + 1)))

            @block.scalar
            def _(act):
                act.sem_inc(copy_act, n_act)
                act.sem_inc(yt_done, NYT)
                if not swa:
                    act.wait_ge(init, 2)
                    nc.scalar.activation(maskr[:], mask0[:], ACT.Copy).then_inc(init, 1)
                    nc.scalar.activation(identr[:], keep["ident"][:], ACT.Copy).then_inc(init, 1)

                def high(i, hh):
                    u = hh % 2
                    NH = NCH // QUAD
                    until(act, chunk_ready, i, NCH, (hh - 1) * NH)
                    act.wait_ge(raw_in["q"], i * (32 * QUAD) + 32 * (hh + 1))
                    nc.scalar.activation(Q[u][:], raw["q"][:], ACT.Copy).then_inc(hi_done, 1)
                    if swa and hh:
                        return
                    if swa:
                        until(act, chunk_ready, i, NCH, 0)
                    act.wait_ge(raw_in["k"], i * (32 * (1 if swa else QUAD)) + 32 * (hh + 1))
                    nc.scalar.activation(Kh[u][:], raw["k"][:], ACT.Copy).then_inc(hi_done, 1)

                def exps(i, r):
                    last = row_chunks[r][-1]
                    width = last[1] + last[2] + (1 if swa else 0)
                    until(act, chunk_read, i, NCH, last[0] + 1)
                    until(act, y_done, i, NR, r - 1)
                    nc.scalar.activation(Sn[r % 2][:, 0:width], Sn[r % 2][:, 0:width], ACT.Exp, scale=-1.0,
                                         bias=nmax[:, r % 4:r % 4 + 1], accum_out=rsum[:, r % 2:r % 2 + 1]).then_inc(exp_done, 1)

                def copy(i, g):
                    order, blocks, on_dve, n, pt = g
                    if on_dve:
                        return
                    until(act, flip_done, i, NG, order + 1)
                    until(act, pv_group, i, n_pt, pt - 3)
                    nc.scalar.activation(PT[pt % 4][:, 0:len(blocks) * P], flips[order % 2][:, 0:len(blocks) * P], ACT.Copy
                                         ).then_inc(copy_act, 1)

                def keep_yt(i, r):
                    order, n = yt_at[r]
                    hh, qb, _ = rows[r]
                    until(act, flip_done, i, NG, order + 1)
                    tile = i * 2 + ((4 if swa else 0) + hh // 2)
                    nc.scalar.activation(yT[:, bass.ds(tile, 1), qb * P:(qb + 1) * P].rearrange("p a n -> p (a n)"),
                                         flips[order % 2][:, 0:P], ACT.Copy).then_inc(copy_act, 1)
                    until(act, copy_act, i, n_act, n + 1)
                    act.sem_inc(yt_done, 1)

                with act.Fori(0, ITER) as i:
                    high(i, 0)
                    exps(i, 0)
                    for r, (hh, qb, first) in enumerate(rows):
                        gs = row_groups[r]
                        half = (len(gs) + 1) // 2
                        for g in gs[:half]:
                            copy(i, g)
                        if r + 1 < NR:
                            exps(i, r + 1)
                        for g in gs[half:]:
                            copy(i, g)
                        if r - 1 in yt_at:
                            keep_yt(i, r - 1)
                        if qb == 6 and hh + 1 < QUAD:
                            high(i, hh + 1)
                    keep_yt(i, NR - 1)

            @block.tensor
            def _(pe):
                pe.sem_inc(pv_group, n_pt)
                pe.sem_inc(chunk_ready, NCH)
                pe.sem_inc(flip_done, NG)
                if not swa:
                    pe.wait_ge(init, 4)

                def score(i, r):
                    hh, qb, first = rows[r]
                    u, ku = hh % 2, 0 if swa else hh % 2
                    if qb == 0:
                        until(pe, split_done["q"], i, QUAD, hh + 1)
                        until(pe, split_done["k"], i, *((1, 1) if swa else (QUAD, hh + 1)))
                    q = Q[u][:, qb * P:(qb + 1) * P]
                    for n, c0, width in row_chunks[r]:
                        until(pe, chunk_read, i, NCH, n - 1)
                        for c in range(c0, c0 + width, 512):
                            w = min(512, c0 + width - c)
                            diagonal = not swa and c + w == (qb + 1) * P
                            out = logits[n % 2][:, c - c0:c - c0 + w]
                            k = slice(first * P + c, first * P + c + w)
                            nc.tensor.matmul(out, q, Kh[ku][:, k], start=True, stop=False)
                            mm = nc.tensor.matmul(out, q, Kl[ku][:, k], start=False, stop=not diagonal)
                            if diagonal:
                                mm = nc.tensor.matmul(logits[n % 2][:, c - c0 + w - P:c - c0 + w], identr[:], maskr[:],
                                                      start=False, stop=True)
                        mm.then_inc(chunk_ready, 1)

                def flip(i, r, g):
                    order, blocks, on_dve, n, pt = g
                    hh, qb, first = rows[r]
                    flip_bank_free(pe, i, order)
                    for j, b in enumerate(blocks):
                        mm = nc.tensor.transpose(flips[order % 2][:, j * P:(j + 1) * P],
                                                 Sn[r % 2][:, (b - first) * P:(b - first + 1) * P], keep["ident"][:])
                    mm.then_inc(flip_done, 1)

                def gather(i, r, g):
                    order, blocks, on_dve, n, pt = g
                    hh, qb, first = rows[r]
                    vslot, vcol = (0, 0) if swa else (hh // 2, hh % 2 * HD)
                    if on_dve:
                        until(pe, copy_dve, i, n_dve, n + 1)
                    else:
                        until(pe, copy_act, i, n_act, n + 1)
                    for j, b in enumerate(blocks):
                        mm = nc.tensor.matmul(outs[r % 2][:, 0:HD], PT[pt % 4][:, j * P:(j + 1) * P],
                                              V[vslot][:, b, vcol:vcol + HD], start=b == first, stop=b == qb)
                    mm.then_inc(pv_group, 1)

                def flip_y(i, r):
                    order, n = yt_at[r]
                    hh, qb, first = rows[r]
                    flip_bank_free(pe, i, order)
                    until(pe, y_done, i, NR, r + 1)
                    nc.tensor.transpose(flips[order % 2][:, 0:P], ZY[hh // 2][:, qb, :], keep["ident"][:]).then_inc(flip_done, 1)

                with pe.Fori(0, ITER) as i:
                    score(i, 0)
                    for r, (hh, qb, first) in enumerate(rows):
                        if r + 1 < NR:
                            score(i, r + 1)
                        if qb == 0 and hh % 2 == 0:
                            if not swa:
                                pe.wait_ge(vz_in[hh // 2], i * 32 + 32)
                            elif hh == 0:
                                pe.wait_ge(vz_in[0], i * 32 + 32)
                        pe.wait_ge(exp_done, i * NR + (r + 1))
                        until(pe, y_done, i, NR, r - 1)
                        gs = row_groups[r]
                        flip(i, r, gs[0])
                        for j in range(1, len(gs)):
                            flip(i, r, gs[j])
                            gather(i, r, gs[j - 1])
                        gather(i, r, gs[-1])
                        if r - 1 in yt_at:
                            flip_y(i, r - 1)
                    flip_y(i, NR - 1)

            @block.vector
            def _(dve):
                for sm, credits in ((copy_dve, n_dve), (chunk_read, NCH), (y_done, NR), (bias_used, QUAD)):
                    dve.sem_inc(sm, credits)
                steps = Steps(dve, dve_steps)
                if swa:
                    dist, bias = alibi[1], alibi[0]
                    dve.wait_ge(init, 1)
                    dve.wait_ge(bias_in[0], 16)
                    steps.settle(nc.vector.tensor_copy(dist, dist.bitcast(mybir.dt.int32)))
                    steps.settle(nc.vector.tensor_scalar(Sn[0][:, 0:2 * P], dist, -1.0, None, ALU.mult))
                    steps.settle(nc.vector.tensor_tensor(dist, dist, Sn[0][:, 0:2 * P], ALU.max))
                    for hh in range(QUAD):
                        steps.settle(nc.vector.tensor_scalar(bias[:, hh, :], dist, -(2.0 ** -(8.0 * (hh + 1) / SWA_H)), None, ALU.mult))
                        steps.settle(nc.vector.memset(bias[0:HD, hh, 0:CHUNK], NEG))
                        steps.settle(nc.vector.memset(bias[0:HD, hh, 3 * CHUNK:4 * CHUNK], NEG))
                        steps.settle(nc.vector.memset(bias[HD:P, hh, 0:2 * CHUNK], NEG))
                    steps.settle(nc.vector.tensor_scalar(sinks[:], sinks[:], -1.0, None, ALU.mult))

                def bias_of(hh, qb, first, c, w):
                    if swa:
                        off = 2 * P - w
                        return alibi[0][:, hh, off:off + w]
                    return nF[hh % 2][:, c:c + w]

                def take(i, r):
                    hh, qb, first = rows[r]
                    if qb == 0 and not swa:
                        dve.wait_ge(bias_in[hh % 2], i * 32 + 16 * (hh // 2 + 1))
                    until(dve, flip_done, i, NG, row_groups[r - 2][-1][0] + 1 - (NG if r < 2 else 0))
                    start = snk[:, hh:hh + 1] if swa else -NEG
                    if swa:
                        w = row_chunks[r][-1][2]
                        steps.did(nc.vector.tensor_copy(Sn[r % 2][:, w:w + 1], start))
                    for n, c, w in row_chunks[r]:
                        until(dve, chunk_ready, i, NCH, n + 1)
                        m = nmax[:, r % 4:r % 4 + 1]
                        if c:
                            until(dve, chunk_read, i, NCH, n)
                            start = m
                        nc.vector.tensor_tensor_reduce(out=Sn[r % 2][:, c:c + w], in0=logits[n % 2][:, 0:w],
                                                       in1=bias_of(hh, qb, first, c, w), scale=-1.0, scalar=start,
                                                       op0=ALU.add, op1=ALU.min, accum_out=m).then_inc(chunk_read, 1)
                    if qb == TT - 1:
                        until(dve, chunk_read, i, NCH, row_chunks[r][-1][0] + 1)
                        dve.sem_inc(bias_used, 1)

                def copy(i, g):
                    order, blocks, on_dve, n, pt = g
                    if not on_dve:
                        return
                    until(dve, flip_done, i, NG, order + 1)
                    until(dve, pv_group, i, n_pt, pt - 3)
                    nc.vector.tensor_copy(PT[pt % 4][:, 0:len(blocks) * P], flips[order % 2][:, 0:len(blocks) * P]
                                          ).then_inc(copy_dve, 1)

                def finish(i, r):
                    hh, qb, first = rows[r]
                    dve.wait_ge(exp_done, i * NR + (r + 1))
                    steps.settle(nc.vector.reciprocal(rinv[:, r % 2:r % 2 + 1], rsum[:, r % 2:r % 2 + 1]))
                    if qb == 0 and hh % 2 == 0:
                        dve.wait_ge(vz_in[hh // 2], (i * 32 + 32) if not (swa and hh == 2) else (i * 16 + 16))
                    until(dve, pv_group, i, n_pt, row_groups[r][-1][4] + 1)
                    y = ZY[hh // 2][:, qb, hh % 2 * HD:(hh % 2 + 1) * HD]
                    nc.vector.scalar_tensor_tensor(out=y, in0=outs[r % 2][:, 0:HD], scalar=rinv[:, r % 2:r % 2 + 1],
                                                   in1=y, op0=ALU.mult, op1=ALU.mult).then_inc(y_done, 1)

                snk = sinks[:, 0:QUAD]
                for i in range(ITER):
                    take(i, 0)
                    for r in range(NR):
                        if r + 1 < NR:
                            take(i, r + 1)
                        for g in row_groups[r]:
                            copy(i, g)
                        finish(i, r)
                    if swa:
                        for hh in range(QUAD):
                            steps.settle(nc.vector.tensor_scalar(alibi[0][:, hh, :], alibi[0][:, hh, :],
                                                                 2.0 ** -(8.0 * QUAD / SWA_H), None, ALU.mult))
                        steps.settle(nc.vector.tensor_copy(sinks[:, 0:QUAD], sinks[:, QUAD:2 * QUAD]))

            return bias_in

        for tag, swa in (("a", False), ("b", True)):
            with ExitStack() as ctx2:
                part(tag, swa)

def split_rows(nc, ctx, tag, sources, Wh, Wl):
    RING = 2
    ring = [ctx.enter_context(nc.sbuf_tensor(f"{tag}_raw{k}", [P, D], F32)) for k in range(RING)]
    w_in = [ctx.enter_context(nc.semaphore(f"{tag}_win{k}")) for k in range(RING)]
    w_hi, w_split = (ctx.enter_context(nc.semaphore(f"{tag}_{n}")) for n in ("whi", "wsplit"))

    def load(sp):
        for k, src in enumerate(sources):
            if k >= RING:
                sp.wait_ge(w_split, k - RING + 1)
            sp.dma_start(ring[k % RING][:], src).then_inc(w_in[k % RING], 16)

    def high(act, k):
        act.wait_ge(w_in[k % RING], 16 * (k // RING + 1))
        nc.scalar.activation(Wh[:, k, :], ring[k % RING][:], ACT.Copy).then_inc(w_hi, 1)

    def low(dve, k):
        dve.wait_ge(w_hi, k + 1)
        nc.vector.tensor_tensor(Wl[:, k, :], ring[k % RING][:], Wh[:, k, :].bitcast(F32), ALU.subtract).then_inc(w_split, 1)

    return load, high, low, w_split

def merge(nc, io, keep, dram):
    ctx = ExitStack()
    sb = lambda name, shape, dt=F32: ctx.enter_context(nc.sbuf_tensor(name, shape, dt))
    sem = lambda name: ctx.enter_context(nc.semaphore(name))
    yT = keep["yT"]
    TB = 256
    NB, BK = S // TB, FW // P
    with ctx:
        Wh, Wl = sb("woh", [P, KT, D], F32R), sb("wol", [P, KT, D], F32R)
        yh, yl = ([sb(f"{n}{k}", [P, KT, TB], F32R) for k in range(2)] for n in ("yh", "yl"))
        gates = [sb(f"gt{k}", [P, 2, KT, TB]) for k in range(2)]
        ta, tb_ = [sb(f"ta{k}", [P, TB]) for k in range(2)], [sb(f"tb{k}", [P, TB]) for k in range(2)]
        pa = [ctx.enter_context(nc.psum_tensor(f"pa{k}", [P, 512], F32)) for k in range(4)]
        pb = [ctx.enter_context(nc.psum_tensor(f"pb{k}", [P, 512], F32)) for k in range(4)]
        sources = [io["w_o_fox"][0, k * P:(k + 1) * P, :] for k in range(BK)] + \
                  [io["w_o_swa"][0, k * P:(k + 1) * P, :] for k in range(BK)]
        load, high, low, w_split = split_rows(nc, ctx, "m", sources, Wh, Wl)
        gate_in = [sem(f"m_g{k}") for k in range(2)]
        y_hi, y_split, mm_done, gated, merged = sem("m_yhi"), sem("m_ysplit"), sem("m_mm"), sem("m_gated"), sem("m_merged")
        block = ctx.enter_context(nc.Block())

        PER = 2 * KT

        @block.sync
        def _(sp):
            load(sp)
            with sp.Fori(0, NB // 2) as i:
                for u in range(2):
                    sp.wait_ge(merged, i * PER + (u + 1) * KT)
                    for half in range(2):
                        sp.dma_start(gates[u][:, half, :, :],
                                     dram["g"][half * D:(half + 1) * D, bass.ds(i * 2 * TB + u * TB, TB)]
                                     .rearrange("(k p) n -> p k n", p=P)).then_inc(gate_in[u], 16)

        @block.gpsimd
        def _(pool):
            with pool.Fori(0, NB // 2) as i:
                for u in range(2):
                    pool.wait_ge(y_hi, i * 2 + (u + 1))
                    pool.tensor_tensor(yl[u][:], yT[:, :, bass.ds(i * 2 * TB + u * TB, TB)], yh[u][:].bitcast(F32),
                                       ALU.subtract).then_inc(y_split, 1)

        @block.tensor
        def _(pe):
            def branch(bank, u, m, k0):
                for k in range(k0, k0 + BK):
                    c = slice(m * P, (m + 1) * P)
                    nc.tensor.matmul(bank, Wh[:, k, c], yh[u][:, k, :], start=k == k0, stop=False)
                    nc.tensor.matmul(bank, Wh[:, k, c], yl[u][:, k, :], start=False, stop=False)
                    mm = nc.tensor.matmul(bank, Wl[:, k, c], yh[u][:, k, :], start=False, stop=k == k0 + BK - 1)
                return mm

            pe.wait_ge(w_split, KT)
            with pe.Fori(0, NB // 2) as i:
                for u in range(2):
                    pe.wait_ge(y_split, i * 2 + (u + 1))
                    for m in range(KT):
                        n = u * KT + m
                        pe.wait_ge(merged, i * PER + (PER + n - 3))
                        branch(pa[n % 4][:, 0:TB], u, m, 0)
                        branch(pb[n % 4][:, 0:TB], u, m, BK).then_inc(mm_done, 1)

        @block.scalar
        def _(act):
            for k in range(KT):
                high(act, k)
            with act.Fori(0, NB // 2) as i:
                for u in range(2):
                    act.wait_ge(merged, i * PER + (u + 1) * KT)
                    nc.scalar.activation(yh[u][:], yT[:, :, bass.ds(i * 2 * TB + u * TB, TB)], ACT.Copy).then_inc(y_hi, 1)

        @block.vector
        def _(dve):
            dve.sem_inc(merged, PER)
            for k in range(KT):
                low(dve, k)
            with dve.Fori(0, NB // 2) as i:
                for u in range(2):
                    dve.wait_ge(gate_in[u], i * 32 + 32)
                    for m in range(KT):
                        n = u * KT + m
                        dve.wait_ge(mm_done, i * 2 * KT + (n + 1))
                        dve.wait_ge(merged, i * PER + (PER + n - 1))
                        nc.vector.tensor_tensor(ta[n % 2][:], pa[n % 4][:, 0:TB], gates[u][:, 0, m, :], ALU.mult)
                        nc.vector.tensor_tensor(tb_[n % 2][:], pb[n % 4][:, 0:TB], gates[u][:, 1, m, :], ALU.mult).then_inc(gated, 1)
                        dve.wait_ge(gated, i * PER + (n + 1))
                        nc.vector.tensor_tensor(yT[:, m, bass.ds(i * 2 * TB + u * TB, TB)], ta[n % 2][:], tb_[n % 2][:],
                                                ALU.add).then_inc(merged, 1)

def output(nc, io, keep, dram, out):
    ctx = ExitStack()
    sb = lambda name, shape, dt=F32: ctx.enter_context(nc.sbuf_tensor(name, shape, dt))
    sem = lambda name: ctx.enter_context(nc.semaphore(name))
    yT = keep["yT"]
    N = 512
    with ctx:
        Wh, Wl = sb("wuh", [P, KT, D], F32R), sb("wul", [P, KT, D], F32R)
        mh, ml = ([sb(f"{n}{k}", [P, KT, P], F32R) for k in range(2)] for n in ("mh", "ml"))
        x_in = [sb(f"xo{k}", [P, D]) for k in range(3)]
        o = [sb(f"o{k}", [P, D]) for k in range(2)]
        gate = sb("gate", [P, D])
        po = [ctx.enter_context(nc.psum_tensor(f"po{k}", [P, D], F32)) for k in range(2)]
        load, high, low, w_split = split_rows(nc, ctx, "o", [io["w_out"][0, k * P:(k + 1) * P, :] for k in range(KT)], Wh, Wl)
        gate_in, x_sem = sem("o_gate"), [sem(f"o_x{k}") for k in range(3)]
        m_hi, m_split, mm_done, scaled, added = sem("o_mhi"), sem("o_msplit"), sem("o_mm"), sem("o_scaled"), sem("o_added")
        stored = [sem(f"o_st{k}") for k in range(2)]
        block = ctx.enter_context(nc.Block())

        @block.sync
        def _(sp):
            sp.dma_start(gate[:], dram["gate"].to_broadcast([P, D])).then_inc(gate_in, 16)
            load(sp)
            for t in range(TT):
                sp.wait_ge(added, t + 1)
                sp.dma_start(out[0, t * P:(t + 1) * P, :], o[t % 2][:]).then_inc(stored[t % 2], 16)
            for k in range(2):
                sp.wait_ge(stored[k], 16 * TT // 2)

        @block.gpsimd
        def _(pool):
            for t in range(TT):
                if t >= 3:
                    pool.wait_ge(added, t - 2)
                pool.dma_start(x_in[t % 3][:], io["x"][0, t * P:(t + 1) * P, :]).then_inc(x_sem[t % 3], 16)

        @block.tensor
        def _(pe):
            for t in range(TT):
                pe.wait_ge(m_split, t + 1)
                if t >= 2:
                    pe.wait_ge(scaled, t - 1)
                u = t % 2
                for h in range(D // N):
                    bank = po[u][:, h * N:(h + 1) * N]
                    for k in range(KT):
                        if t == 0 and h == 0:
                            pe.wait_ge(w_split, k + 1)
                        c = slice(h * N, (h + 1) * N)
                        nc.tensor.matmul(bank, mh[u][:, k, :], Wh[:, k, c], start=k == 0, stop=False)
                        nc.tensor.matmul(bank, mh[u][:, k, :], Wl[:, k, c], start=False, stop=False)
                        mm = nc.tensor.matmul(bank, ml[u][:, k, :], Wh[:, k, c], start=False, stop=k == KT - 1)
                mm.then_inc(mm_done, 1)

        def tile_of(t):
            return yT[:, :, t * P:(t + 1) * P]

        @block.scalar
        def _(act):
            def high_m(t):
                if t >= 2:
                    act.wait_ge(mm_done, t - 1)
                nc.scalar.activation(mh[t % 2][:], tile_of(t), ACT.Copy).then_inc(m_hi, 1)

            high_m(0)
            high_m(1)
            for k in range(KT):
                high(act, k)
            for t in range(2, TT):
                high_m(t)

        @block.vector
        def _(dve):
            def low_m(t):
                dve.wait_ge(m_hi, t + 1)
                nc.vector.tensor_tensor(ml[t % 2][:], tile_of(t), mh[t % 2][:].bitcast(F32), ALU.subtract).then_inc(m_split, 1)

            low_m(0)
            low_m(1)
            for k in range(KT):
                low(dve, k)
            dve.wait_ge(gate_in, 16)
            for t in range(TT):
                dve.wait_ge(mm_done, t + 1)
                if t >= 2:
                    dve.wait_ge(stored[t % 2], 16 * (t // 2))
                nc.vector.tensor_tensor(o[t % 2][:], po[t % 2][:], gate[:], ALU.mult).then_inc(scaled, 1)
                if t + 2 < TT:
                    low_m(t + 2)
                dve.wait_ge(scaled, t + 1)
                dve.wait_ge(x_sem[t % 3], 16 * (t // 3 + 1))
                nc.vector.tensor_tensor(o[t % 2][:], o[t % 2][:], x_in[t % 3][:], ALU.add).then_inc(added, 1)

def build(nc, io, out):
    scratch = lambda name, shape: nc.dram_tensor(name, shape, F32).ap()
    dram = {
        "qk": scratch("qk_scratch", [2 * FW + SW + KW, S]),
        "v": scratch("v_scratch", [S, FW + KW]),
        "z": scratch("z_scratch", [S, FW + SW]),
        "g": scratch("g_scratch", [2 * D, S]),
        "f": scratch("f_scratch", [FOX_H, S]),
        "gate": scratch("gate_scratch", [1, D]),
    }
    with ExitStack() as ctx:
        keep = {"ident": ctx.enter_context(nc.sbuf_tensor("ident", [P, P], F32)),
                "siluc": ctx.enter_context(nc.sbuf_tensor("siluc", [P, KT], F32))}
        with ExitStack() as early:
            keep["hTh"] = early.enter_context(nc.sbuf_tensor("hTh", [P, KT, S], F32R))
            keep["hTl"] = early.enter_context(nc.sbuf_tensor("hTl", [P, KT, S], F32R))
            condition_and_norm(nc, io, keep)
            project(nc, io, keep, dram)
        keep["yT"] = ctx.enter_context(nc.sbuf_tensor("yT", [P, KT, S], F32))
        attend(nc, io, keep, dram)
        merge(nc, io, keep, dram)
        output(nc, io, keep, dram, out)

_INS = ["x", "c", "w_ada", "b_ada", "norm_g", "w_in", "b_forget", "fox_q_g", "fox_k_g", "w_o_fox",
        "swa_q_g", "swa_k_g", "swa_sinks", "w_o_swa", "w_out"]

def kernel(**inputs):
    import numpy as _np
    import concourse.bacc as _bacc
    from concourse import mybir as _mybir
    from concourse.bass_utils import run_bass_kernel_spmd as _run

    nc = _bacc.Bacc("TRN2", target_bir_lowering=False, num_devices=1)
    arrays, io = {}, {}
    for name in _INS:
        a = _np.ascontiguousarray(inputs[name])
        arrays[f"in_{name}"] = a
        io[name] = nc.dram_tensor(f"in_{name}", a.shape, _mybir.dt.from_np(a.dtype), kind="ExternalInput").ap()
    out = nc.dram_tensor("out", (1, S, D), F32, kind="ExternalOutput").ap()
    build(nc, io, out)
    return _run(nc, [arrays], core_ids=[0]).results[0]["out"]
```

```python
from contextlib import ExitStack

import numpy as np
import concourse.bass as bass
from concourse import mybir
from concourse.alu_op_type import AluOpType as ALU

F32 = mybir.dt.float32
F32R = mybir.dt.float32r
ACT = mybir.ActivationFunctionType
AX = mybir.AxisListType

P = 128
D = 1024
S = 2048
KT = D // P
TT = S // P
HD = 64
FOX_H, SWA_H, KV_H = 8, 8, 2
FW, SW, KW = FOX_H * HD, SWA_H * HD, KV_H * HD
CHUNK = 64
COLS = 512
EPS = 1e-6
NEG = -1e30
QK_SCALE = HD ** -0.5

C_Q, C_K, C_V, C_F = 0, FW, 2 * FW, 3 * FW
C_ZA = C_F + FOX_H
C_QB = C_ZA + FW
C_KB = C_QB + SW
C_VB = C_KB + KW
C_ZB = C_VB + KW
C_GA = C_ZB + SW
C_GB = C_GA + D
D_IN = C_GB + D

R_Q, R_K, R_QB, R_KB = 0, FW, 2 * FW, 2 * FW + SW

class Steps:

    def __init__(self, eng, sem):
        self.eng, self.sem, self.n, self.local = eng, sem, 0, 0

    def did(self, ins):
        ins.then_inc(self.sem, 1)
        self.n = self.n + 1
        self.local += 1
        return ins

    def settle(self, ins):
        self.did(ins)
        self.eng.wait_ge(self.sem, self.n)

    def loop(self, i, per_iteration):
        self.base, self.per, self.local = self.n, per_iteration, 0
        self.n = self.n + i * per_iteration

    def end(self, iterations):
        assert self.local == self.per, (self.local, self.per)
        self.n = self.base + iterations * self.per

def identity(pool, tile, done):
    pool.memset(tile, 0.0).then_inc(done, 1)
    pool.wait_ge(done, 1)
    pool.affine_select(out=tile, in_=tile, compare_op=ALU.not_equal, fill=1.0, base=0,
                       pattern=[[-1, P]], channel_multiplier=1).then_inc(done, 1)

def condition_and_norm(nc, io, keep):
    ctx = ExitStack()
    sb = lambda name, shape, dt=F32: ctx.enter_context(nc.sbuf_tensor(name, shape, dt))
    sem = lambda name: ctx.enter_context(nc.semaphore(name))
    NADA = 2 * KT
    WR, XR = 3, 4
    with ctx:
        wada = [sb(f"wada{k}", [P, 2 * D]) for k in range(WR)]
        xin = [sb(f"xin{k}", [P, D]) for k in range(XR)]
        xn = [sb(f"xn{k}", [P, D]) for k in range(2)]
        hf = [sb(f"hf{k}", [P, KT, P]) for k in range(2)]
        c_raw, bias, ng = sb("c_raw", [P, KT]), sb("bias", [P, NADA]), sb("ng", [P, KT])
        acc, mulA = sb("acc", [P, NADA]), sb("mulA", [P, KT])
        ss, sd, rstd = sb("ss", [P, 2]), sb("sd", [P, 2]), sb("rstd", [P, 2])
        ps_ada = [ctx.enter_context(nc.psum_tensor(f"ps_ada{k}", [P, 512], F32)) for k in range(2)]
        ps_x = [ctx.enter_context(nc.psum_tensor(f"ps_x{k}", [P, KT, P], F32)) for k in range(2)]
        small_in, id_done, siluc_done = sem("p_small"), sem("p_id"), sem("p_siluc")
        wada_in = [sem(f"p_wada{k}") for k in range(WR)]
        x_in = [sem(f"p_x{k}") for k in range(XR)]
        ada_mm, ada_acc = sem("p_ada_mm"), sem("p_ada_acc")
        ab_ready = sem("p_ab")
        ss_done, var_done, sd_done, rstd_done, xn_done = (sem("p_" + n) for n in ("ss", "var", "sd", "rstd", "xn"))
        xt_done, mul_done, full_done, hi_done, lo_done = (sem("p_" + n) for n in ("xt", "mul", "full", "hi", "lo"))
        dve_steps = sem("p_dve")
        block = ctx.enter_context(nc.Block())

        @block.sync
        def _(sp):
            with nc.allow_non_contiguous_dma(reason="columns of small vectors"):
                sp.dma_start(c_raw[:], io["c"].rearrange("a (k p) -> p (a k)", p=P)).then_inc(small_in, 16)
                sp.dma_start(bias[:], io["b_ada"][:, 0:2 * D].rearrange("a (k p) -> p (a k)", p=P)).then_inc(small_in, 16)
                sp.dma_start(ng[:], io["norm_g"].rearrange("a (k p) -> p (a k)", p=P)).then_inc(small_in, 16)
            for k in range(KT):
                if k >= WR:
                    sp.wait_ge(ada_mm, k - WR + 1)
                sp.dma_start(wada[k % WR][:], io["w_ada"][0, k * P:(k + 1) * P, 0:2 * D]).then_inc(wada_in[k % WR], 16)
            for t in range(TT):
                if t >= XR:
                    sp.wait_ge(xn_done, t - XR + 1)
                sp.dma_start(xin[t % XR][:], io["x"][0, t * P:(t + 1) * P, :]).then_inc(x_in[t % XR], 16)

        @block.gpsimd
        def _(pool):
            identity(pool, keep["ident"][:], id_done)
            pool.wait_ge(ab_ready, 1)
            for t in range(TT):
                pool.wait_ge(mul_done, t + 1)
                pool.tensor_tensor(hf[t % 2][:], hf[t % 2][:], acc[:, 0:KT].unsqueeze(2).to_broadcast([P, KT, P]),
                                   ALU.add).then_inc(full_done, 1)

        @block.tensor
        def _(pe):
            pe.wait_ge(siluc_done, 1)
            for k in range(KT):
                pe.wait_ge(wada_in[k % WR], 16 * (k // WR + 1))
                if k >= 2:
                    pe.wait_ge(ada_acc, k - 1)
                for m in range(NADA):
                    mm = nc.tensor.matmul(ps_ada[k % 2][:, m:m + 1], wada[k % WR][:, m * P:(m + 1) * P],
                                          keep["siluc"][:, k:k + 1], start=True, stop=True)
                mm.then_inc(ada_mm, 1)
            pe.wait_ge(id_done, 2)
            for t in range(TT):
                pe.wait_ge(xn_done, t + 1)
                if t >= 2:
                    pe.wait_ge(mul_done, t - 1)
                for k in range(KT):
                    mm = nc.tensor.transpose(ps_x[t % 2][:, k, :], xn[t % 2][:, k * P:(k + 1) * P], keep["ident"][:])
                mm.then_inc(xt_done, 1)

        @block.scalar
        def _(act):
            act.wait_ge(small_in, 48)
            nc.scalar.activation(keep["siluc"][:], c_raw[:], ACT.Silu).then_inc(siluc_done, 1)

            def high(t):
                act.wait_ge(full_done, t + 1)
                nc.scalar.activation(keep["hTh"][:, :, t * P:(t + 1) * P], hf[t % 2][:], ACT.Copy).then_inc(hi_done, 1)

            for t in range(TT):
                act.wait_ge(x_in[t % XR], 16 * (t // XR + 1))
                if t >= 2:
                    act.wait_ge(xt_done, t - 1)
                    act.wait_ge(var_done, t - 1)
                nc.scalar.activation(xn[t % 2][:], xin[t % XR][:], ACT.Square,
                                     accum_out=ss[:, t % 2:t % 2 + 1]).then_inc(ss_done, 1)
                act.wait_ge(var_done, t + 1)
                nc.scalar.activation(sd[:, t % 2:t % 2 + 1], rstd[:, t % 2:t % 2 + 1], ACT.Sqrt).then_inc(sd_done, 1)
                act.wait_ge(rstd_done, t + 1)
                nc.scalar.activation(xn[t % 2][:], xin[t % XR][:], ACT.Copy,
                                     scale=rstd[:, t % 2:t % 2 + 1]).then_inc(xn_done, 1)
                if t >= 1:
                    high(t - 1)
            high(TT - 1)

        @block.vector
        def _(dve):
            st = Steps(dve, dve_steps)
            for k in range(KT):
                dve.wait_ge(ada_mm, k + 1)
                if k == 0:
                    nc.vector.tensor_tensor(acc[:], ps_ada[0][:, 0:NADA], bias[:], ALU.add).then_inc(ada_acc, 1)
                else:
                    dve.wait_ge(ada_acc, k)
                    nc.vector.tensor_tensor(acc[:], ps_ada[k % 2][:, 0:NADA], acc[:], ALU.add).then_inc(ada_acc, 1)
            dve.wait_ge(ada_acc, KT)
            st.settle(nc.vector.tensor_scalar(mulA[:], acc[:, KT:NADA], 1.0, None, ALU.add))
            st.settle(nc.vector.tensor_tensor(mulA[:], mulA[:], ng[:], ALU.mult))
            nc.vector.engine_nop().then_inc(ab_ready, 1)

            def low(t):
                dve.wait_ge(hi_done, t + 1)
                high = keep["hTh"][:, :, t * P:(t + 1) * P]
                nc.vector.tensor_tensor(keep["hTl"][:, :, t * P:(t + 1) * P], hf[t % 2][:], high.bitcast(F32),
                                        ALU.subtract).then_inc(lo_done, 1)

            for t in range(TT):
                v = rstd[:, t % 2:t % 2 + 1]
                dve.wait_ge(ss_done, t + 1)
                if t >= 2:
                    dve.wait_ge(xn_done, t - 1)
                nc.vector.tensor_scalar(v, ss[:, t % 2:t % 2 + 1], 1.0 / D, EPS, ALU.mult, ALU.add).then_inc(var_done, 1)
                dve.wait_ge(sd_done, t + 1)
                nc.vector.reciprocal(v, sd[:, t % 2:t % 2 + 1]).then_inc(rstd_done, 1)
                dve.wait_ge(xt_done, t + 1)
                if t >= 2:
                    dve.wait_ge(lo_done, t - 1)
                nc.vector.tensor_tensor(hf[t % 2][:], ps_x[t % 2][:], mulA[:].unsqueeze(2).to_broadcast([P, KT, P]),
                                        ALU.mult).then_inc(mul_done, 1)
                if t >= 1:
                    low(t - 1)
            low(TT - 1)

def project(nc, io, keep, dram):
    ctx = ExitStack()
    sb = lambda name, shape, dt=F32: ctx.enter_context(nc.sbuf_tensor(name, shape, dt))
    sem = lambda name: ctx.enter_context(nc.semaphore(name))
    hTh, hTl = keep["hTh"], keep["hTl"]
    RAW, BANKS, ST = 4, 4, 4
    NT = S // COLS
    N_NORM, N_Z, N_G = 3, 2, 2 * D // COLS
    G_NORM = 0
    G_KV = G_NORM + N_NORM
    G_V = G_KV + 1
    G_Z = G_V + 1
    G_G = G_Z + N_Z
    G_F = G_G + N_G
    DVE_TILES = TT * G_G
    with ctx:
        wraw = [sb(f"wraw{k}", [P, COLS]) for k in range(RAW)]
        Wh, Wl = sb("Wh", [P, KT, COLS], F32R), sb("Wl", [P, KT, COLS], F32R)
        st = [sb(f"st{k}", [P, COLS]) for k in range(ST)]
        qn = [sb(f"qn{k}", [P, COLS]) for k in range(2)]
        qT = [sb(f"qT{k}", [P, COLS]) for k in range(2)]
        sq = sb("sq", [P, COLS])
        var, sd, rs = sb("var", [P, 2, FOX_H]), sb("nsd", [P, 2, FOX_H]), sb("nrs", [P, 2, FOX_H])
        gains = sb("gains", [P, 4, HD])
        bf, one = sb("bf", [FOX_H, 1]), sb("one", [FOX_H, 1])
        fu, fl = sb("fu", [FOX_H, COLS]), sb("fl", [FOX_H, COLS])
        fc = [t[0:FOX_H, :] for t in (*qn, *qT)]
        wg = [sb(f"wg{k}", [P, D]) for k in range(4)]
        bg, gacc = sb("bg", [P, KT]), sb("gacc", [P, KT])
        bank = [ctx.enter_context(nc.psum_tensor(f"pj{k}", [P, COLS], F32)) for k in range(BANKS)]
        tbank = [ctx.enter_context(nc.psum_tensor(f"pt{k}", [P, 4, P], F32)) for k in range(2)]
        gbank = [ctx.enter_context(nc.psum_tensor(f"pg{k}", [P, 512], F32)) for k in range(2)]
        small_in, credits = sem("j_small"), sem("j_credits")
        w_in = [sem(f"j_w{k}") for k in range(RAW)]
        w_hi, w_split, w_free = sem("j_whi"), sem("j_wsplit"), sem("j_wfree")
        mm_done, dve_free, act_free = sem("j_mm"), sem("j_dfree"), sem("j_afree")
        sq_done, var_done, sd_done, qn_done = sem("j_sq"), sem("j_var"), sem("j_sd"), sem("j_qn")
        qt_done, qT_done = sem("j_qt"), sem("j_qTd")
        qT_stored = [sem(f"j_qs{k}") for k in range(2)]
        st_dve, st_act = sem("j_std"), sem("j_sta")
        stored = [sem(f"j_st{k}") for k in range(ST)]
        sig_done, ln_done, f_done, f_stored = sem("j_sig"), sem("j_ln"), sem("j_f"), sem("j_fs")
        wg_in = [sem(f"j_wg{k}") for k in range(4)]
        g_mm, g_acc, g_stored = sem("j_gmm"), sem("j_gacc"), sem("j_gs")
        gains_ready = sem("j_gains")
        act_steps, dve_steps = sem("j_act"), sem("j_dve")
        block = ctx.enter_context(nc.Block())

        def norm_loop(eng, body):
            with eng.Fori(0, N_NORM) as i:
                body(i)

        @block.gpsimd
        def _(pool):
            pool.sem_inc(w_split, RAW)

            def load(g, col0):
                for k in range(KT):
                    n = g * KT + k
                    pool.wait_ge(w_split, n + 1)
                    pool.dma_start(wraw[k % RAW][:], io["w_in"][0, k * P:(k + 1) * P, bass.ds(col0, COLS)]
                                   ).then_inc(w_in[k % RAW], 16)

            with pool.Fori(0, N_NORM) as i:
                load(i + G_NORM, i * COLS + i // 2 * (C_QB - 2 * COLS))
            load(G_KV, C_KB)
            load(G_V, C_V)
            with pool.Fori(0, N_Z) as i:
                load(i + G_Z, i * (C_ZB - C_ZA) + C_ZA)
            with pool.Fori(0, N_G) as i:
                load(i + G_G, i * COLS + C_GA)
            load(G_F, C_F)

        @block.sync
        def _(sp):
            for n, name in enumerate(("fox_q_g", "fox_k_g", "swa_q_g", "swa_k_g")):
                sp.dma_start(gains[:, n, :], io[name].to_broadcast([P, HD])).then_inc(small_in, 16)
            with nc.allow_non_contiguous_dma(reason="columns of small vectors"):
                sp.dma_start(bf[:], io["b_forget"].rearrange("a h -> h a")).then_inc(small_in, 16)
                sp.dma_start(bg[:], io["b_ada"][:, 2 * D:3 * D].rearrange("a (k p) -> p (a k)", p=P)).then_inc(small_in, 16)

            def store_norm(g, row0, heads):
                for t in range(TT):
                    sp.wait_ge(qT_done, g * TT + t + 2 + 1)
                    sp.dma_start(dram["qk"][bass.ds(row0, heads * HD), t * P:(t + 1) * P]
                                 .rearrange("(b p) n -> p b n", p=P),
                                 qT[t % 2][:, 0:heads * HD].rearrange("p (b n) -> p b n", n=P)
                                 ).then_inc(qT_stored[t % 2], 16)
            with sp.Fori(0, N_NORM) as i:
                store_norm(i, i * COLS + R_Q, FOX_H)
            for t in range(TT):
                sp.wait_ge(qT_done, N_NORM * TT + t + 2 + 1)
                sp.dma_start(dram["qk"][R_KB:R_KB + KW, t * P:(t + 1) * P], qT[t % 2][:, 0:P]).then_inc(qT_stored[t % 2], 16)
                sp.wait_ge(st_dve, t + 1)
                sp.dma_start(dram["v"][t * P:(t + 1) * P, FW:FW + KW], st[t % ST][:, 0:KW]).then_inc(stored[t % ST], 16)
            for t in range(TT):
                sp.wait_ge(st_dve, TT + t + 1)
                sp.dma_start(dram["v"][t * P:(t + 1) * P, 0:FW], st[t % ST][:]).then_inc(stored[t % ST], 16)
            with sp.Fori(0, N_Z) as i:
                for t in range(TT):
                    sp.wait_ge(st_dve, i * TT + (2 * TT + t + 1))
                    sp.dma_start(dram["z"][t * P:(t + 1) * P, bass.ds(i * COLS, COLS)], st[t % ST][:]).then_inc(stored[t % ST], 16)
            with sp.Fori(0, N_G) as i:
                for t in range(TT):
                    m, b = t // NT, t % NT
                    sp.wait_ge(st_act, i * TT + (t + 1))
                    sp.dma_start(dram["g"][bass.ds(i * COLS + m * P, P), b * COLS:(b + 1) * COLS], st[t % ST][:]).then_inc(stored[t % ST], 16)
            for k in range(KT):
                if k >= 4:
                    sp.wait_ge(g_mm, k - 3)
                sp.dma_start(wg[k % 4][:], io["w_ada"][0, k * P:(k + 1) * P, 2 * D:3 * D]).then_inc(wg_in[k % 4], 16)
                if k == 3:
                    for b in range(NT):
                        sp.wait_ge(f_done, b + 1)
                        sp.dma_start(dram["f"][:, b * COLS:(b + 1) * COLS], fc[b]).then_inc(f_stored, 16)
            sp.wait_ge(g_acc, KT)
            with nc.allow_non_contiguous_dma(reason="column to row of a small vector"):
                sp.dma_start(dram["gate"].rearrange("a (k p) -> p (a k)", p=P), gacc[:]).then_inc(g_stored, 16)
            sp.wait_ge(g_stored, 16)
            sp.wait_ge(f_stored, 16 * NT)
            for k in range(2):
                sp.wait_ge(qT_stored[k], 16 * (N_NORM + 1) * TT // 2 + 16)
            for k in range(ST):
                sp.wait_ge(stored[k], 16 * (2 + N_Z + N_G) * TT // ST)

        @block.tensor
        def _(pe):
            pe.sem_inc(w_free, KT - 1)
            pe.sem_inc(qt_done, 2)

            def three(out, a_hi, a_lo, b_hi, b_lo, first, last):
                nc.tensor.matmul(out, a_hi, b_hi, start=first, stop=False)
                nc.tensor.matmul(out, a_hi, b_lo, start=False, stop=False)
                return nc.tensor.matmul(out, a_lo, b_hi, start=False, stop=last)

            def tile(g, t, tiles, free_sem, free_at, operands, width):
                pe.wait_ge(free_sem, free_at)
                for k in range(KT):
                    if t == 0:
                        pe.wait_ge(w_split, g * KT + k + 1 + RAW)
                    mm = three(bank[t % BANKS][:, 0:width], *operands(k), k == 0, k == KT - 1)
                    if t == tiles - 1 and k < KT - 1:
                        mm.then_inc(w_free, 1)
                mm.then_inc(mm_done, 1)

            def tokens_by_cols(t, width):
                tok = slice(t * P, (t + 1) * P)
                return lambda k: (hTh[:, k, tok], hTl[:, k, tok], Wh[:, k, 0:width], Wl[:, k, 0:width])

            def cols_by_tokens(m, b):
                c, tok = slice(m * P, (m + 1) * P), slice(b * COLS, (b + 1) * COLS)
                return lambda k: (Wh[:, k, c], Wl[:, k, c], hTh[:, k, tok], hTl[:, k, tok])

            def flip(g, t, heads):
                pe.wait_ge(qn_done, g * TT + t + 1)
                pe.wait_ge(qT_done, g * TT + t + 1)
                for b in range(heads * HD // P):
                    mm = nc.tensor.transpose(tbank[t % 2][:, b, :], qn[t % 2][:, b * P:(b + 1) * P], keep["ident"][:])
                mm.then_inc(qt_done, 1)

            def norm_group(g, heads):
                for t in range(TT):
                    tile(g, t, TT, dve_free, g * TT + t + 1, tokens_by_cols(t, heads * HD if heads == FOX_H else 2 * KW),
                         heads * HD if heads == FOX_H else 2 * KW)
                    if t >= 2:
                        flip(g, t - 2, heads)
                flip(g, TT - 2, heads)
                flip(g, TT - 1, heads)

            def plain_group(g):
                for t in range(TT):
                    tile(g, t, TT, dve_free, g * TT + t + 1, tokens_by_cols(t, COLS), COLS)

            with pe.Fori(0, N_NORM) as i:
                norm_group(i, FOX_H)
            norm_group(G_KV, KV_H)
            plain_group(G_V)
            with pe.Fori(0, N_Z) as i:
                plain_group(i + G_Z)
            pe.wait_ge(dve_free, DVE_TILES + BANKS)
            with pe.Fori(0, N_G) as i:
                for t in range(TT):
                    tile(i + G_G, t, TT, act_free, i * TT + (t + 1), cols_by_tokens(t // NT, t % NT), COLS)
            for t in range(NT):
                tile(G_F, t, NT, act_free, N_G * TT + t + 1, cols_by_tokens(0, t), COLS)
            for k in range(KT):
                pe.wait_ge(wg_in[k % 4], 16 * (k // 4 + 1))
                if k >= 2:
                    pe.wait_ge(g_acc, k - 1)
                for m in range(KT):
                    mm = nc.tensor.matmul(gbank[k % 2][:, m:m + 1], wg[k % 4][:, m * P:(m + 1) * P],
                                          keep["siluc"][:, k:k + 1], start=True, stop=True)
                mm.then_inc(g_mm, 1)

        @block.scalar
        def _(act):
            act.sem_inc(qT_done, 2)
            act.sem_inc(act_free, BANKS)
            act.sem_inc(qT_stored[0], 16)
            act.sem_inc(qT_stored[1], 16)

            def split_high(g, first=False):
                for k in range(KT):
                    act.wait_ge(w_in[k % RAW], g * (16 * KT // RAW) + 16 * (k // RAW + 1))
                    if k < KT - 1:
                        act.wait_ge(w_free, g * (KT - 1) + (k + 1))
                    elif not first:
                        act.wait_ge(mm_done, g * TT)
                    nc.scalar.activation(Wh[:, k, :], wraw[k % RAW][:], ACT.Copy).then_inc(w_hi, 1)

            def squares(g, t, heads):
                w = heads * HD
                n = g * TT + t
                act.wait_ge(mm_done, n + 1)
                act.wait_ge(var_done, n + 1)
                nc.scalar.activation(sq[:, 0:w], bank[t % BANKS][:, 0:w], ACT.Square).then_inc(sq_done, 1)
                act.wait_ge(var_done, n + 2)
                nc.scalar.activation(sd[:, t % 2, 0:heads], var[:, t % 2, 0:heads], ACT.Sqrt).then_inc(sd_done, 1)

            def copy_out(g, t, heads):
                w = heads * HD
                act.wait_ge(qt_done, g * TT + t + 2 + 1)
                act.wait_ge(qT_stored[t % 2], g * (8 * TT) + 16 * (t // 2 + 1))
                nc.scalar.activation(qT[t % 2][:, 0:w], tbank[t % 2][:, 0:w // P, :].rearrange("p b n -> p (b n)"),
                                     ACT.Copy).then_inc(qT_done, 1)

            def norm_group(g, heads):
                for t in range(TT):
                    if t == TT - 1:
                        split_high(g + 1)
                    squares(g, t, heads)
                    if t >= 2:
                        copy_out(g, t - 2, heads)
                copy_out(g, TT - 2, heads)
                copy_out(g, TT - 1, heads)

            split_high(0, first=True)
            with act.Fori(0, N_NORM) as i:
                norm_group(i, FOX_H)
            norm_group(G_KV, KV_H)
            split_high(G_Z)
            with act.Fori(0, N_Z) as i:
                for t in range(TT):
                    if t == TT - 1:
                        split_high(i + (G_Z + 1))
                    act.wait_ge(mm_done, i * TT + (G_Z * TT + t + 1))
                    act.wait_ge(stored[t % ST], i * (16 * TT // ST) + 16 * (2 * TT // ST + t // ST))
                    nc.scalar.activation(st[t % ST][:], bank[t % BANKS][:], ACT.Sigmoid).then_inc(sig_done, 1)
            with act.Fori(0, N_G) as i:
                for t in range(TT):
                    if t == TT - 1:
                        split_high(i + (G_G + 1))
                    act.wait_ge(mm_done, i * TT + (G_G * TT + t + 1))
                    act.wait_ge(stored[t % ST], i * (16 * TT // ST) + 16 * ((2 + N_Z) * TT // ST + t // ST))
                    nc.scalar.activation(st[t % ST][:], bank[t % BANKS][:], ACT.Sigmoid).then_inc(st_act, 1)
                    act.wait_ge(st_act, i * TT + (t + 1))
                    act.sem_inc(act_free, 1)
            steps = Steps(act, act_steps)
            act.wait_ge(small_in, 96)
            for b in range(NT):
                act.wait_ge(mm_done, (G_F * TT) + b + 1)
                if b >= 1:
                    act.wait_ge(f_done, b)
                steps.did(nc.scalar.activation(fu[:], bank[b % BANKS][0:FOX_H, :], ACT.Identity, bias=bf[:, 0:1]))
                steps.settle(nc.scalar.activation(fl[:], bank[b % BANKS][0:FOX_H, :], ACT.Abs, bias=bf[:, 0:1]))
                act.sem_inc(act_free, 1)
                steps.settle(nc.scalar.activation(fl[:], fl[:], ACT.Exp, scale=-1.0))
                nc.scalar.activation(fl[:], fl[:], ACT.Ln, bias=1.0).then_inc(ln_done, 1)

        @block.vector
        def _(dve):
            dve.sem_inc(dve_free, BANKS)
            dve.sem_inc(var_done, 1)
            steps = Steps(dve, dve_steps)

            def split_low(g):
                for k in range(KT):
                    n = g * KT + k
                    dve.wait_ge(w_hi, n + 1)
                    nc.vector.tensor_tensor(Wl[:, k, :], wraw[k % RAW][:], Wh[:, k, :].bitcast(F32),
                                            ALU.subtract).then_inc(w_split, 1)

            def normalise(g, t, heads, gain, copy_v):
                w, u = heads * HD, t % 2
                n = g * TT + t
                by_head = lambda ap: ap[:, 0:w].rearrange("p (h d) -> p h d", d=HD)
                dve.wait_ge(sq_done, n + 1)
                steps.settle(nc.vector.tensor_reduce(var[:, u, 0:heads], by_head(sq), AX.X, ALU.add))
                nc.vector.tensor_scalar(var[:, u, 0:heads], var[:, u, 0:heads], 1.0 / HD, EPS, ALU.mult, ALU.add
                                        ).then_inc(var_done, 1)
                if copy_v:
                    if t >= ST:
                        dve.wait_ge(stored[t % ST], 16 * (t // ST))
                    nc.vector.tensor_copy(st[t % ST][:, 0:KW], bank[t % BANKS][:, KW:2 * KW]).then_inc(st_dve, 1)
                dve.wait_ge(sd_done, n + 1)
                steps.settle(nc.vector.reciprocal(rs[:, u, 0:heads], sd[:, u, 0:heads]))
                dve.wait_ge(qt_done, n + 1)
                nc.vector.tensor_tensor(by_head(qn[u]), by_head(bank[t % BANKS]),
                                        rs[:, u, 0:heads].unsqueeze(2).to_broadcast([P, heads, HD]), ALU.mult
                                        ).then_inc(dve_free, 1)
                dve.wait_ge(dve_free, n + 1 + BANKS)
                nc.vector.tensor_tensor(by_head(qn[u]), by_head(qn[u]),
                                        gains[:, bass.ds(gain, 1), :].to_broadcast([P, heads, HD]), ALU.mult
                                        ).then_inc(qn_done, 1)

            split_low(0)
            dve.wait_ge(small_in, 96)
            for n in (0, 2):
                nc.vector.tensor_scalar(gains[:, n, :], gains[:, n, :], QK_SCALE, None, ALU.mult).then_inc(gains_ready, 1)
            dve.wait_ge(gains_ready, 2)
            with dve.Fori(0, N_NORM) as i:
                steps.loop(i, 2 * TT)
                for t in range(TT):
                    if t == TT - 1:
                        split_low(i + 1)
                    normalise(i, t, FOX_H, i, False)
            steps.end(N_NORM)
            for t in range(TT):
                if t == TT - 1:
                    split_low(G_V)
                normalise(G_KV, t, KV_H, 3, True)
            for t in range(TT):
                if t == TT - 1:
                    split_low(G_Z)
                dve.wait_ge(mm_done, G_V * TT + t + 1)
                dve.wait_ge(stored[t % ST], 16 * (TT // ST + t // ST))
                nc.vector.tensor_copy(st[t % ST][:], bank[t % BANKS][:]).then_inc(dve_free, 1)
                dve.wait_ge(dve_free, G_V * TT + t + 1 + BANKS)
                dve.sem_inc(st_dve, 1)
            with dve.Fori(0, N_Z) as i:
                for t in range(TT):
                    if t == TT - 1:
                        split_low(i + (G_Z + 1))
                    dve.wait_ge(sig_done, i * TT + (t + 1))
                    nc.vector.tensor_tensor(st[t % ST][:], st[t % ST][:], bank[t % BANKS][:], ALU.mult).then_inc(dve_free, 1)
                    dve.wait_ge(dve_free, i * TT + (G_Z * TT + t + 1 + BANKS))
                    dve.sem_inc(st_dve, 1)
            with dve.Fori(0, N_G) as i:
                split_low(i + (G_G + 1))
            steps.settle(nc.vector.memset(one[:], 1.0))
            dve.wait_ge(qt_done, G_V * TT + 2)
            for k in range(2):
                dve.wait_ge(qT_stored[k], 16 * (G_V * TT // 2) + 16)
            for b in range(NT):
                dve.wait_ge(ln_done, b + 1)
                steps.settle(nc.vector.tensor_scalar(fu[:], fu[:], 0.0, None, ALU.min))
                steps.settle(nc.vector.tensor_tensor(fu[:], fl[:], fu[:], ALU.subtract))
                nc.vector.tensor_tensor_scan(fc[b], one[:].to_broadcast([FOX_H, COLS]), fu[:],
                                             fc[b - 1][:, COLS - 1:COLS] if b else 0.0,
                                             ALU.mult, ALU.add).then_inc(f_done, 1)
                dve.wait_ge(f_done, b + 1)
            for k in range(KT):
                dve.wait_ge(g_mm, k + 1)
                if k >= 1:
                    dve.wait_ge(g_acc, k)
                nc.vector.tensor_tensor(gacc[:], gbank[k % 2][:, 0:KT], gacc[:] if k else bg[:], ALU.add).then_inc(g_acc, 1)

def attend(nc, io, keep, dram):
    ctx = ExitStack()
    sb = lambda name, shape, dt=F32: ctx.enter_context(nc.sbuf_tensor(name, shape, dt))
    sem = lambda name: ctx.enter_context(nc.semaphore(name))
    yT = keep["yT"]
    QUAD = 4
    HALF = 1024
    with ctx:
        raw = {"q": sb("raw_q", [P, S]), "k": sb("raw_k", [P, S])}
        Q = [sb(f"Q{k}", [P, S], F32R) for k in range(2)]
        Kh = [sb(f"Kh{k}", [P, S], F32R) for k in range(2)]
        Kl = [sb(f"Kl{k}", [P, S], F32R) for k in range(2)]
        V = [sb(f"V{k}", [P, TT, 2 * HD]) for k in range(2)]
        ZY = [sb(f"ZY{k}", [P, TT, 2 * HD]) for k in range(2)]
        Sn = [sb(f"Sn{k}", [P, S]) for k in range(3)]
        PT = [sb(f"PT{k}", [P, 4 * P]) for k in range(3)]
        nF = [sb(f"nF{k}", [P, S]) for k in range(2)]
        identr, maskr = sb("identr", [P, P], F32R), sb("maskr", [P, P], F32R)
        mask0 = Sn[0][:, 0:P]
        nmax, rsum, rinv = sb("nmax", [P, 4]), sb("rsum", [P, 4]), sb("rinv", [P, 2])
        sinks = sb("sinks", [P, SWA_H])
        alibi = [nF[0][:, 0:QUAD * 2 * P].rearrange("p (h n) -> p h n", h=QUAD),
                 nF[1][:, 0:2 * P]]
        logits = [ctx.enter_context(nc.psum_tensor(f"lg{k}", [P, HALF], F32)) for k in range(2)]
        flips = [ctx.enter_context(nc.psum_tensor(f"fl{k}", [P, 4 * P], F32)) for k in range(2)]
        outs = [ctx.enter_context(nc.psum_tensor(f"ot{k}", [P, 512], F32)) for k in range(2)]

        def part(tag, swa):
            s = lambda name: sem(f"{tag}_{name}")
            raw_in, split_done = {x: s("raw" + x) for x in "qk"}, {x: s("split" + x) for x in "qk"}
            hi_done = s("hi")
            bias_in, vz_in = [s("bias0"), s("bias1")], [s("vz0"), s("vz1")]
            chunk_ready, chunk_read = s("cready"), s("cread")
            exp_done, flip_done, copy_act, copy_dve = s("exp"), s("flip"), s("cact"), s("cdve")
            pv_group, y_done, yt_done = s("pvg"), s("y"), s("yt")
            bias_used, init = s("bused"), s("init")
            dve_steps = s("dve")
            ITER = (SWA_H if swa else FOX_H) // QUAD

            LAG = 2 if swa else 1
            rows = [(hh, qb, max(0, qb - 1) if swa else 0) for hh in range(QUAD) for qb in range(TT)]
            NR = len(rows)
            row_chunks, row_groups, NCH, n_pt = [], [], 0, 0
            for hh, qb, first in rows:
                width = (qb + 1 - first) * P
                row_chunks.append([(NCH + j, c, min(HALF, width - c)) for j, c in enumerate(range(0, width, HALF))])
                NCH += len(row_chunks[-1])
                blocks = list(range(first, qb + 1))
                row_groups.append([(n_pt + j, blocks[b:b + 4]) for j, b in enumerate(range(0, len(blocks), 4))])
                n_pt += len(row_groups[-1])
            on_dve = lambda pt: pt % 2 == 1 if swa else pt % 3 == 2
            copies, work, yt_rows = {}, [], []
            n_of = {True: 0, False: 0}
            for r in range(-2, NR + LAG + 1):
                mine = []
                score = row_chunks[r + 2] if r + 2 < NR else []
                flip = row_groups[r] if 0 <= r < NR else []
                gather = row_groups[r - LAG] if 0 <= r - LAG < NR else []
                mine += [("score", r + 2, c) for c in score[:1]]
                for j in range(4):
                    mine += [("gather", r - LAG, g) for g in gather[j:j + 1]]
                    mine += [("flip", r, g) for g in flip[j:j + 1]]
                    if j == 1:
                        mine += [("score", r + 2, c) for c in score[1:]]
                y = r - LAG - 1
                if 0 <= y < NR and rows[y][0] % 2:
                    mine.append(("flip_y", y, None))
                    yt_rows.append(y)
                work.append((r, mine))
                for kind, row, g in mine:
                    if kind in ("flip", "flip_y"):
                        dve = kind == "flip" and on_dve(g[0])
                        copies[kind, row, g and g[0]] = (len(copies), dve, n_of[dve])
                        n_of[dve] += 1
            flips_in_order = list(copies.values())
            NG, NYT, n_dve, n_act = len(copies), len(yt_rows), n_of[True], n_of[False]
            assert NCH % 2 == 0 and NG % 2 == 0

            def before(n, ring, total):
                if n >= ring:
                    return n - ring + 1
                return max(m for m in range(total) if m % ring == n % ring) + 1 - total

            def until(eng, sm, i, per, count):
                assert count > -per
                eng.wait_ge(sm, i * per + (per + count))

            def flip_bank_free(pe, i, order):
                _, dve, n = flips_in_order[order - 2]
                sm, per = (copy_dve, n_dve) if dve else (copy_act, n_act)
                until(pe, sm, i, per, n + 1 - (per if order < 2 else 0))

            def last_flip(r):
                return copies["flip", r, row_groups[r][-1][0]][0] + 1

            block = ctx2.enter_context(nc.Block())

            @block.sync
            def _(sp):
                if swa:
                    sp.dma_start(sinks[:], io["swa_sinks"].to_broadcast([P, SWA_H])).then_inc(bias_in[0], 16)
                for i in range(ITER):
                    for hh in range(QUAD):
                        pair = hh // 2
                        for x in "qk":
                            if x == "k" and swa and hh:
                                continue
                            per = QUAD if x == "q" or not swa else 1
                            until(sp, split_done[x], i, per, hh)
                            row0 = (i * (QUAD * HD) + (hh * HD + (R_QB if swa else R_Q)) if x == "q" else
                                    i * HD + R_KB if swa else i * (QUAD * HD) + (hh * HD + R_K))
                            for half in range(2):
                                sp.dma_start(raw[x][half * HD:(half + 1) * HD, :], dram["qk"][bass.ds(row0, HD), :]
                                             ).then_inc(raw_in[x], 16)
                        if not swa:
                            until(sp, bias_used, i, QUAD, hh - 1)
                            sp.dma_start(nF[hh % 2][:], dram["f"][bass.ds(i * QUAD + hh, 1), :].to_broadcast([P, S])
                                         ).then_inc(bias_in[hh % 2], 16)
                        if hh % 2 == 0:
                            vcol = i * HD + FW if swa else i * (QUAD * HD) + pair * 2 * HD
                            zcol = i * (QUAD * HD) + ((FW if swa else 0) + pair * 2 * HD)
                            until(sp, pv_group, i, n_pt, (pair - 1) * n_pt // 2 if not swa or pair else 0)
                            until(sp, yt_done, i, NYT, (pair - 1) * NYT // 2)
                            if swa:
                                if hh == 0:
                                    sp.dma_start(V[0][:, :, 0:HD], dram["v"][:, bass.ds(vcol, HD)]
                                                 .rearrange("(t p) n -> p t n", p=P)).then_inc(vz_in[0], 16)
                            else:
                                sp.dma_start(V[pair][:], dram["v"][:, bass.ds(vcol, 2 * HD)]
                                             .rearrange("(t p) n -> p t n", p=P)).then_inc(vz_in[pair], 16)
                            sp.dma_start(ZY[pair][:], dram["z"][:, bass.ds(zcol, 2 * HD)]
                                         .rearrange("(t p) n -> p t n", p=P)).then_inc(vz_in[pair], 16)

            @block.gpsimd
            def _(pool):
                pool.sem_inc(split_done["q"], QUAD)
                pool.sem_inc(split_done["k"], 1 if swa else QUAD)
                if not swa:
                    pool.memset(mask0, 0.0).then_inc(init, 1)
                    pool.wait_ge(init, 1)
                    pool.affine_select(out=mask0, in_=mask0, compare_op=ALU.is_ge, fill=NEG, base=0,
                                       pattern=[[-1, P]], channel_multiplier=1).then_inc(init, 1)
                else:
                    dist = alibi[1]
                    pool.iota(dist.bitcast(mybir.dt.int32), pattern=[[-1, 2 * P]], base=P, channel_multiplier=1).then_inc(init, 1)
                    pool.wait_ge(init, 1)
                with pool.Fori(0, ITER) as i:
                    for hh in range(QUAD):
                        u = hh % 2
                        pool.wait_ge(hi_done, i * (QUAD + (1 if swa else QUAD)) + (hh + (1 if swa else hh) + 1 if hh or not swa else 1))
                        pool.tensor_tensor(Q[u][HD:P, :], raw["q"][HD:P, :], Q[u][HD:P, :].bitcast(F32), ALU.subtract
                                           ).then_inc(split_done["q"], 1)
                        until(pool, split_done["q"], i, QUAD, hh + 1)
                        if swa and hh:
                            continue
                        pool.wait_ge(hi_done, i * (QUAD + (1 if swa else QUAD)) + (2 * hh + 2))
                        pool.tensor_tensor(Kl[u][:], raw["k"][:], Kh[u][:].bitcast(F32), ALU.subtract
                                           ).then_inc(split_done["k"], 1)
                        until(pool, split_done["k"], i, *((1, 1) if swa else (QUAD, hh + 1)))

            @block.scalar
            def _(act):
                act.sem_inc(copy_act, n_act)
                act.sem_inc(yt_done, NYT)
                if not swa:
                    act.wait_ge(init, 2)
                    nc.scalar.activation(maskr[:], mask0, ACT.Copy).then_inc(init, 1)
                    nc.scalar.activation(identr[:], keep["ident"][:], ACT.Copy).then_inc(init, 1)

                def high(i, hh):
                    u = hh % 2
                    NH = NCH // QUAD
                    until(act, chunk_ready, i, NCH, (hh - 1) * NH)
                    act.wait_ge(raw_in["q"], i * (32 * QUAD) + 32 * (hh + 1))
                    nc.scalar.activation(Q[u][:], raw["q"][:], ACT.Copy).then_inc(hi_done, 1)
                    if swa and hh:
                        return
                    if swa:
                        until(act, chunk_ready, i, NCH, 0)
                    act.wait_ge(raw_in["k"], i * (32 * (1 if swa else QUAD)) + 32 * (hh + 1))
                    nc.scalar.activation(Kh[u][:], raw["k"][:], ACT.Copy).then_inc(hi_done, 1)

                def exps(i, r):
                    last = row_chunks[r][-1]
                    width = last[1] + last[2] + (1 if swa else 0)
                    until(act, chunk_read, i, NCH, last[0] + 1)
                    until(act, y_done, i, NR, r - 3)
                    nc.scalar.activation(Sn[r % 3][:, 0:width], Sn[r % 3][:, 0:width], ACT.Exp, scale=-1.0,
                                         bias=nmax[:, r % 4:r % 4 + 1], accum_out=rsum[:, r % 4:r % 4 + 1]).then_inc(exp_done, 1)

                def copy(i, r, g):
                    pt, blocks = g
                    order, dve, n = copies["flip", r, pt]
                    if dve:
                        return
                    until(act, flip_done, i, NG, order + 1)
                    until(act, pv_group, i, n_pt, before(pt, 3, n_pt))
                    nc.scalar.activation(PT[pt % 3][:, 0:len(blocks) * P], flips[order % 2][:, 0:len(blocks) * P], ACT.Copy
                                         ).then_inc(copy_act, 1)

                def keep_yt(i, r):
                    order, _, n = copies["flip_y", r, None]
                    hh, qb, _ = rows[r]
                    until(act, flip_done, i, NG, order + 1)
                    tile = i * 2 + ((4 if swa else 0) + hh // 2)
                    nc.scalar.activation(yT[:, bass.ds(tile, 1), qb * P:(qb + 1) * P].rearrange("p a n -> p (a n)"),
                                         flips[order % 2][:, 0:P], ACT.Copy).then_inc(copy_act, 1)
                    until(act, copy_act, i, n_act, n + 1)
                    act.sem_inc(yt_done, 1)

                with act.Fori(0, ITER) as i:
                    high(i, 0)
                    for r, mine in work:
                        fl = [(row, g) for kind, row, g in mine if kind == "flip"]
                        half = (len(fl) + 1) // 2
                        for row, g in fl[:half]:
                            copy(i, row, g)
                        if 0 <= r + 1 < NR:
                            exps(i, r + 1)
                        for row, g in fl[half:]:
                            copy(i, row, g)
                        for kind, row, g in mine:
                            if kind == "flip_y":
                                keep_yt(i, row)
                        if 0 <= r < NR and rows[r][1] == 6 and rows[r][0] + 1 < QUAD:
                            high(i, rows[r][0] + 1)

            @block.tensor
            def _(pe):
                pe.sem_inc(pv_group, n_pt)
                pe.sem_inc(chunk_ready, NCH)
                pe.sem_inc(flip_done, NG)
                if not swa:
                    pe.wait_ge(init, 4)

                def score(i, r, chunk):
                    hh, qb, first = rows[r]
                    u, ku = hh % 2, 0 if swa else hh % 2
                    n, c0, width = chunk
                    if qb == 0:
                        until(pe, split_done["q"], i, QUAD, hh + 1)
                        until(pe, split_done["k"], i, *((1, 1) if swa else (QUAD, hh + 1)))
                    q = Q[u][:, qb * P:(qb + 1) * P]
                    until(pe, chunk_read, i, NCH, n - 1)
                    for c in range(c0, c0 + width, 512):
                        w = min(512, c0 + width - c)
                        diagonal = not swa and c + w == (qb + 1) * P
                        out = logits[n % 2][:, c - c0:c - c0 + w]
                        k = slice(first * P + c, first * P + c + w)
                        nc.tensor.matmul(out, q, Kh[ku][:, k], start=True, stop=False)
                        mm = nc.tensor.matmul(out, q, Kl[ku][:, k], start=False, stop=not diagonal)
                        if diagonal:
                            mm = nc.tensor.matmul(logits[n % 2][:, c - c0 + w - P:c - c0 + w], identr[:], maskr[:],
                                                  start=False, stop=True)
                    mm.then_inc(chunk_ready, 1)

                def flip(i, r, g):
                    pt, blocks = g
                    order, _, _ = copies["flip", r, pt]
                    hh, qb, first = rows[r]
                    if blocks[0] == first:
                        pe.wait_ge(exp_done, i * NR + (r + 1))
                    flip_bank_free(pe, i, order)
                    for j, b in enumerate(blocks):
                        mm = nc.tensor.transpose(flips[order % 2][:, j * P:(j + 1) * P],
                                                 Sn[r % 3][:, (b - first) * P:(b - first + 1) * P], keep["ident"][:])
                    mm.then_inc(flip_done, 1)

                def gather(i, r, g):
                    pt, blocks = g
                    order, dve, n = copies["flip", r, pt]
                    hh, qb, first = rows[r]
                    vslot, vcol = (0, 0) if swa else (hh // 2, hh % 2 * HD)
                    if qb == 0 and (hh == 0 if swa else hh % 2 == 0):
                        pe.wait_ge(vz_in[vslot], i * 32 + 32)
                    if blocks[0] == first:
                        until(pe, y_done, i, NR, r - 1)
                    if dve:
                        until(pe, copy_dve, i, n_dve, n + 1)
                    else:
                        until(pe, copy_act, i, n_act, n + 1)
                    for j, b in enumerate(blocks):
                        mm = nc.tensor.matmul(outs[r % 2][:, 0:HD], PT[pt % 3][:, j * P:(j + 1) * P],
                                              V[vslot][:, b, vcol:vcol + HD], start=b == first, stop=b == qb)
                    mm.then_inc(pv_group, 1)

                def flip_y(i, r, _):
                    order = copies["flip_y", r, None][0]
                    hh, qb, first = rows[r]
                    flip_bank_free(pe, i, order)
                    until(pe, y_done, i, NR, r + 1)
                    nc.tensor.transpose(flips[order % 2][:, 0:P], ZY[hh // 2][:, qb, :], keep["ident"][:]).then_inc(flip_done, 1)

                step = {"score": score, "flip": flip, "gather": gather, "flip_y": flip_y}
                with pe.Fori(0, ITER) as i:
                    for _, mine in work:
                        for kind, row, what in mine:
                            step[kind](i, row, what)

            @block.vector
            def _(dve):
                for sm, credits in ((copy_dve, n_dve), (chunk_read, NCH), (y_done, NR), (bias_used, QUAD)):
                    dve.sem_inc(sm, credits)
                steps = Steps(dve, dve_steps)
                if swa:
                    dist, bias = alibi[1], alibi[0]
                    dve.wait_ge(init, 1)
                    dve.wait_ge(bias_in[0], 16)
                    steps.settle(nc.vector.tensor_copy(dist, dist.bitcast(mybir.dt.int32)))
                    steps.settle(nc.vector.tensor_scalar(Sn[0][:, 0:2 * P], dist, -1.0, None, ALU.mult))
                    steps.settle(nc.vector.tensor_tensor(dist, dist, Sn[0][:, 0:2 * P], ALU.max))
                    for hh in range(QUAD):
                        steps.settle(nc.vector.tensor_scalar(bias[:, hh, :], dist, -(2.0 ** -(8.0 * (hh + 1) / SWA_H)), None, ALU.mult))
                        steps.settle(nc.vector.memset(bias[0:HD, hh, 0:CHUNK], NEG))
                        steps.settle(nc.vector.memset(bias[0:HD, hh, 3 * CHUNK:4 * CHUNK], NEG))
                        steps.settle(nc.vector.memset(bias[HD:P, hh, 0:2 * CHUNK], NEG))
                    steps.settle(nc.vector.tensor_scalar(sinks[:], sinks[:], -1.0, None, ALU.mult))

                def bias_of(hh, qb, first, c, w):
                    if swa:
                        off = 2 * P - w
                        return alibi[0][:, hh, off:off + w]
                    return nF[hh % 2][:, c:c + w]

                def take(i, r):
                    hh, qb, first = rows[r]
                    if qb == 0 and not swa:
                        dve.wait_ge(bias_in[hh % 2], i * 32 + 16 * (hh // 2 + 1))
                    p = before(r, 3, NR)
                    until(dve, flip_done, i, NG, last_flip(p - 1) if p > 0 else last_flip(p - 1 + NR) - NG)
                    start = snk[:, hh:hh + 1] if swa else -NEG
                    if swa:
                        w = row_chunks[r][-1][2]
                        steps.did(nc.vector.tensor_copy(Sn[r % 3][:, w:w + 1], start))
                    for n, c, w in row_chunks[r]:
                        until(dve, chunk_ready, i, NCH, n + 1)
                        m = nmax[:, r % 4:r % 4 + 1]
                        if c:
                            until(dve, chunk_read, i, NCH, n)
                            start = m
                        nc.vector.tensor_tensor_reduce(out=Sn[r % 3][:, c:c + w], in0=logits[n % 2][:, 0:w],
                                                       in1=bias_of(hh, qb, first, c, w), scale=-1.0, scalar=start,
                                                       op0=ALU.add, op1=ALU.min, accum_out=m).then_inc(chunk_read, 1)
                    if qb == TT - 1:
                        until(dve, chunk_read, i, NCH, row_chunks[r][-1][0] + 1)
                        dve.sem_inc(bias_used, 1)

                def copy(i, r, g):
                    pt, blocks = g
                    order, mine, n = copies["flip", r, pt]
                    if not mine:
                        return
                    until(dve, flip_done, i, NG, order + 1)
                    until(dve, pv_group, i, n_pt, before(pt, 3, n_pt))
                    nc.vector.tensor_copy(PT[pt % 3][:, 0:len(blocks) * P], flips[order % 2][:, 0:len(blocks) * P]
                                          ).then_inc(copy_dve, 1)

                def finish(i, r):
                    hh, qb, first = rows[r]
                    dve.wait_ge(exp_done, i * NR + (r + 1))
                    steps.settle(nc.vector.reciprocal(rinv[:, r % 2:r % 2 + 1], rsum[:, r % 4:r % 4 + 1]))
                    if qb == 0 and hh % 2 == 0:
                        dve.wait_ge(vz_in[hh // 2], (i * 32 + 32) if not (swa and hh == 2) else (i * 16 + 16))
                    until(dve, pv_group, i, n_pt, row_groups[r][-1][0] + 1)
                    y = ZY[hh // 2][:, qb, hh % 2 * HD:(hh % 2 + 1) * HD]
                    nc.vector.scalar_tensor_tensor(out=y, in0=outs[r % 2][:, 0:HD], scalar=rinv[:, r % 2:r % 2 + 1],
                                                   in1=y, op0=ALU.mult, op1=ALU.mult).then_inc(y_done, 1)

                snk = sinks[:, 0:QUAD]
                for i in range(ITER):
                    for r, mine in work:
                        fl = [(row, g) for kind, row, g in mine if kind == "flip"]
                        half = (len(fl) + 1) // 2
                        for row, g in fl[:half]:
                            copy(i, row, g)
                        if r + 2 < NR:
                            take(i, r + 2)
                        for row, g in fl[half:]:
                            copy(i, row, g)
                        if 0 <= r - LAG < NR:
                            finish(i, r - LAG)
                    if swa:
                        for hh in range(QUAD):
                            steps.settle(nc.vector.tensor_scalar(alibi[0][:, hh, :], alibi[0][:, hh, :],
                                                                 2.0 ** -(8.0 * QUAD / SWA_H), None, ALU.mult))
                        steps.settle(nc.vector.tensor_copy(sinks[:, 0:QUAD], sinks[:, QUAD:2 * QUAD]))

            return bias_in

        for tag, swa in (("a", False), ("b", True)):
            with ExitStack() as ctx2:
                part(tag, swa)

def split_rows(nc, ctx, tag, sources, Wh, Wl):
    RING = 2
    ring = [ctx.enter_context(nc.sbuf_tensor(f"{tag}_raw{k}", [P, D], F32)) for k in range(RING)]
    w_in = [ctx.enter_context(nc.semaphore(f"{tag}_win{k}")) for k in range(RING)]
    w_hi, w_split = (ctx.enter_context(nc.semaphore(f"{tag}_{n}")) for n in ("whi", "wsplit"))

    def load(sp):
        for k, src in enumerate(sources):
            if k >= RING:
                sp.wait_ge(w_split, k - RING + 1)
            sp.dma_start(ring[k % RING][:], src).then_inc(w_in[k % RING], 16)

    def high(act, k):
        act.wait_ge(w_in[k % RING], 16 * (k // RING + 1))
        nc.scalar.activation(Wh[:, k, :], ring[k % RING][:], ACT.Copy).then_inc(w_hi, 1)

    def low(dve, k):
        dve.wait_ge(w_hi, k + 1)
        nc.vector.tensor_tensor(Wl[:, k, :], ring[k % RING][:], Wh[:, k, :].bitcast(F32), ALU.subtract).then_inc(w_split, 1)

    return load, high, low, w_split

def merge(nc, io, keep, dram):
    ctx = ExitStack()
    sb = lambda name, shape, dt=F32: ctx.enter_context(nc.sbuf_tensor(name, shape, dt))
    sem = lambda name: ctx.enter_context(nc.semaphore(name))
    yT = keep["yT"]
    TB = 256
    NB, BK = S // TB, FW // P
    with ctx:
        Wh, Wl = sb("woh", [P, KT, D], F32R), sb("wol", [P, KT, D], F32R)
        yh, yl = ([sb(f"{n}{k}", [P, KT, TB], F32R) for k in range(2)] for n in ("yh", "yl"))
        gates = [sb(f"gt{k}", [P, 2, KT, TB]) for k in range(2)]
        ta, tb_ = [sb(f"ta{k}", [P, TB]) for k in range(2)], [sb(f"tb{k}", [P, TB]) for k in range(2)]
        pa = [ctx.enter_context(nc.psum_tensor(f"pa{k}", [P, 512], F32)) for k in range(4)]
        pb = [ctx.enter_context(nc.psum_tensor(f"pb{k}", [P, 512], F32)) for k in range(4)]
        sources = [io["w_o_fox"][0, k * P:(k + 1) * P, :] for k in range(BK)] + \
                  [io["w_o_swa"][0, k * P:(k + 1) * P, :] for k in range(BK)]
        load, high, low, w_split = split_rows(nc, ctx, "m", sources, Wh, Wl)
        gate_in = [sem(f"m_g{k}") for k in range(2)]
        y_hi, y_split, mm_done, gated, merged = sem("m_yhi"), sem("m_ysplit"), sem("m_mm"), sem("m_gated"), sem("m_merged")
        block = ctx.enter_context(nc.Block())

        PER = 2 * KT

        @block.sync
        def _(sp):
            load(sp)
            with sp.Fori(0, NB // 2) as i:
                for u in range(2):
                    sp.wait_ge(merged, i * PER + (u + 1) * KT)
                    for half in range(2):
                        sp.dma_start(gates[u][:, half, :, :],
                                     dram["g"][half * D:(half + 1) * D, bass.ds(i * 2 * TB + u * TB, TB)]
                                     .rearrange("(k p) n -> p k n", p=P)).then_inc(gate_in[u], 16)

        @block.gpsimd
        def _(pool):
            with pool.Fori(0, NB // 2) as i:
                for u in range(2):
                    pool.wait_ge(y_hi, i * 2 + (u + 1))
                    pool.tensor_tensor(yl[u][:], yT[:, :, bass.ds(i * 2 * TB + u * TB, TB)], yh[u][:].bitcast(F32),
                                       ALU.subtract).then_inc(y_split, 1)

        @block.tensor
        def _(pe):
            def branch(bank, u, m, k0):
                for k in range(k0, k0 + BK):
                    c = slice(m * P, (m + 1) * P)
                    nc.tensor.matmul(bank, Wh[:, k, c], yh[u][:, k, :], start=k == k0, stop=False)
                    nc.tensor.matmul(bank, Wh[:, k, c], yl[u][:, k, :], start=False, stop=False)
                    mm = nc.tensor.matmul(bank, Wl[:, k, c], yh[u][:, k, :], start=False, stop=k == k0 + BK - 1)
                return mm

            pe.wait_ge(w_split, KT)
            with pe.Fori(0, NB // 2) as i:
                for u in range(2):
                    pe.wait_ge(y_split, i * 2 + (u + 1))
                    for m in range(KT):
                        n = u * KT + m
                        pe.wait_ge(merged, i * PER + (PER + n - 3))
                        branch(pa[n % 4][:, 0:TB], u, m, 0)
                        branch(pb[n % 4][:, 0:TB], u, m, BK).then_inc(mm_done, 1)

        @block.scalar
        def _(act):
            for k in range(KT):
                high(act, k)
            with act.Fori(0, NB // 2) as i:
                for u in range(2):
                    act.wait_ge(merged, i * PER + (u + 1) * KT)
                    nc.scalar.activation(yh[u][:], yT[:, :, bass.ds(i * 2 * TB + u * TB, TB)], ACT.Copy).then_inc(y_hi, 1)

        @block.vector
        def _(dve):
            dve.sem_inc(merged, PER)
            for k in range(KT):
                low(dve, k)
            with dve.Fori(0, NB // 2) as i:
                for u in range(2):
                    dve.wait_ge(gate_in[u], i * 32 + 32)
                    for m in range(KT):
                        n = u * KT + m
                        dve.wait_ge(mm_done, i * 2 * KT + (n + 1))
                        dve.wait_ge(merged, i * PER + (PER + n - 1))
                        nc.vector.tensor_tensor(ta[n % 2][:], pa[n % 4][:, 0:TB], gates[u][:, 0, m, :], ALU.mult)
                        nc.vector.tensor_tensor(tb_[n % 2][:], pb[n % 4][:, 0:TB], gates[u][:, 1, m, :], ALU.mult).then_inc(gated, 1)
                        dve.wait_ge(gated, i * PER + (n + 1))
                        nc.vector.tensor_tensor(yT[:, m, bass.ds(i * 2 * TB + u * TB, TB)], ta[n % 2][:], tb_[n % 2][:],
                                                ALU.add).then_inc(merged, 1)

def output(nc, io, keep, dram, out):
    ctx = ExitStack()
    sb = lambda name, shape, dt=F32: ctx.enter_context(nc.sbuf_tensor(name, shape, dt))
    sem = lambda name: ctx.enter_context(nc.semaphore(name))
    yT = keep["yT"]
    N = 512
    with ctx:
        Wh, Wl = sb("wuh", [P, KT, D], F32R), sb("wul", [P, KT, D], F32R)
        mh, ml = ([sb(f"{n}{k}", [P, KT, P], F32R) for k in range(2)] for n in ("mh", "ml"))
        x_in = [sb(f"xo{k}", [P, D]) for k in range(3)]
        o = [sb(f"o{k}", [P, D]) for k in range(2)]
        gate = sb("gate", [P, D])
        po = [ctx.enter_context(nc.psum_tensor(f"po{k}", [P, D], F32)) for k in range(2)]
        load, high, low, w_split = split_rows(nc, ctx, "o", [io["w_out"][0, k * P:(k + 1) * P, :] for k in range(KT)], Wh, Wl)
        gate_in, x_sem = sem("o_gate"), [sem(f"o_x{k}") for k in range(3)]
        m_hi, m_split, mm_done, scaled, added = sem("o_mhi"), sem("o_msplit"), sem("o_mm"), sem("o_scaled"), sem("o_added")
        stored = [sem(f"o_st{k}") for k in range(2)]
        block = ctx.enter_context(nc.Block())

        @block.sync
        def _(sp):
            sp.dma_start(gate[:], dram["gate"].to_broadcast([P, D])).then_inc(gate_in, 16)
            load(sp)
            for t in range(TT):
                sp.wait_ge(added, t + 1)
                sp.dma_start(out[0, t * P:(t + 1) * P, :], o[t % 2][:]).then_inc(stored[t % 2], 16)
            for k in range(2):
                sp.wait_ge(stored[k], 16 * TT // 2)

        @block.gpsimd
        def _(pool):
            for t in range(TT):
                if t >= 3:
                    pool.wait_ge(added, t - 2)
                pool.dma_start(x_in[t % 3][:], io["x"][0, t * P:(t + 1) * P, :]).then_inc(x_sem[t % 3], 16)

        @block.tensor
        def _(pe):
            for t in range(TT):
                pe.wait_ge(m_split, t + 1)
                if t >= 2:
                    pe.wait_ge(scaled, t - 1)
                u = t % 2
                for h in range(D // N):
                    bank = po[u][:, h * N:(h + 1) * N]
                    for k in range(KT):
                        if t == 0 and h == 0:
                            pe.wait_ge(w_split, k + 1)
                        c = slice(h * N, (h + 1) * N)
                        nc.tensor.matmul(bank, mh[u][:, k, :], Wh[:, k, c], start=k == 0, stop=False)
                        nc.tensor.matmul(bank, mh[u][:, k, :], Wl[:, k, c], start=False, stop=False)
                        mm = nc.tensor.matmul(bank, ml[u][:, k, :], Wh[:, k, c], start=False, stop=k == KT - 1)
                mm.then_inc(mm_done, 1)

        def tile_of(t):
            return yT[:, :, t * P:(t + 1) * P]

        @block.scalar
        def _(act):
            def high_m(t):
                if t >= 2:
                    act.wait_ge(mm_done, t - 1)
                nc.scalar.activation(mh[t % 2][:], tile_of(t), ACT.Copy).then_inc(m_hi, 1)

            high_m(0)
            high_m(1)
            for k in range(KT):
                high(act, k)
            for t in range(2, TT):
                high_m(t)

        @block.vector
        def _(dve):
            def low_m(t):
                dve.wait_ge(m_hi, t + 1)
                nc.vector.tensor_tensor(ml[t % 2][:], tile_of(t), mh[t % 2][:].bitcast(F32), ALU.subtract).then_inc(m_split, 1)

            low_m(0)
            low_m(1)
            for k in range(KT):
                low(dve, k)
            dve.wait_ge(gate_in, 16)
            for t in range(TT):
                dve.wait_ge(mm_done, t + 1)
                if t >= 2:
                    dve.wait_ge(stored[t % 2], 16 * (t // 2))
                nc.vector.tensor_tensor(o[t % 2][:], po[t % 2][:], gate[:], ALU.mult).then_inc(scaled, 1)
                if t + 2 < TT:
                    low_m(t + 2)
                dve.wait_ge(scaled, t + 1)
                dve.wait_ge(x_sem[t % 3], 16 * (t // 3 + 1))
                nc.vector.tensor_tensor(o[t % 2][:], o[t % 2][:], x_in[t % 3][:], ALU.add).then_inc(added, 1)

def build(nc, io, out):
    scratch = lambda name, shape: nc.dram_tensor(name, shape, F32).ap()
    dram = {
        "qk": scratch("qk_scratch", [2 * FW + SW + KW, S]),
        "v": scratch("v_scratch", [S, FW + KW]),
        "z": scratch("z_scratch", [S, FW + SW]),
        "g": scratch("g_scratch", [2 * D, S]),
        "f": scratch("f_scratch", [FOX_H, S]),
        "gate": scratch("gate_scratch", [1, D]),
    }
    with ExitStack() as ctx:
        keep = {"ident": ctx.enter_context(nc.sbuf_tensor("ident", [P, P], F32)),
                "siluc": ctx.enter_context(nc.sbuf_tensor("siluc", [P, KT], F32))}
        with ExitStack() as early:
            keep["hTh"] = early.enter_context(nc.sbuf_tensor("hTh", [P, KT, S], F32R))
            keep["hTl"] = early.enter_context(nc.sbuf_tensor("hTl", [P, KT, S], F32R))
            condition_and_norm(nc, io, keep)
            project(nc, io, keep, dram)
        keep["yT"] = ctx.enter_context(nc.sbuf_tensor("yT", [P, KT, S], F32))
        attend(nc, io, keep, dram)
        merge(nc, io, keep, dram)
        output(nc, io, keep, dram, out)

_INS = ["x", "c", "w_ada", "b_ada", "norm_g", "w_in", "b_forget", "fox_q_g", "fox_k_g", "w_o_fox",
        "swa_q_g", "swa_k_g", "swa_sinks", "w_o_swa", "w_out"]

def kernel(**inputs):
    import numpy as _np
    import concourse.bacc as _bacc
    from concourse import mybir as _mybir
    from concourse.bass_utils import run_bass_kernel_spmd as _run

    nc = _bacc.Bacc("TRN2", target_bir_lowering=False, num_devices=1)
    arrays, io = {}, {}
    for name in _INS:
        a = _np.ascontiguousarray(inputs[name])
        arrays[f"in_{name}"] = a
        io[name] = nc.dram_tensor(f"in_{name}", a.shape, _mybir.dt.from_np(a.dtype), kind="ExternalInput").ap()
    out = nc.dram_tensor("out", (1, S, D), F32, kind="ExternalOutput").ap()
    build(nc, io, out)
    return _run(nc, [arrays], core_ids=[0]).results[0]["out"]
```

```python
from contextlib import ExitStack

import numpy as np
import concourse.bass as bass
from concourse import mybir
from concourse.alu_op_type import AluOpType as ALU

F32 = mybir.dt.float32
F32R = mybir.dt.float32r
ACT = mybir.ActivationFunctionType
AX = mybir.AxisListType

P = 128
D = 1024
S = 2048
KT = D // P
TT = S // P
HD = 64
FOX_H, SWA_H, KV_H = 8, 8, 2
FW, SW, KW = FOX_H * HD, SWA_H * HD, KV_H * HD
CHUNK = 64
COLS = 512
RAW = 4
EPS = 1e-6
NEG = -1e30
QK_SCALE = HD ** -0.5

C_Q, C_K, C_V, C_F = 0, FW, 2 * FW, 3 * FW
C_ZA = C_F + FOX_H
C_QB = C_ZA + FW
C_KB = C_QB + SW
C_VB = C_KB + KW
C_ZB = C_VB + KW
C_GA = C_ZB + SW
C_GB = C_GA + D

R_Q, R_K, R_QB, R_KB = 0, FW, 2 * FW, 2 * FW + SW

class Steps:

    def __init__(self, eng, sem):
        self.eng, self.sem, self.n, self.local = eng, sem, 0, 0

    def did(self, ins):
        ins.then_inc(self.sem, 1)
        self.n = self.n + 1
        self.local += 1
        return ins

    def settle(self, ins):
        self.did(ins)
        self.eng.wait_ge(self.sem, self.n)

    def loop(self, i, per_iteration):
        self.base, self.per, self.local = self.n, per_iteration, 0
        self.n = self.n + i * per_iteration

    def end(self, iterations):
        assert self.local == self.per, (self.local, self.per)
        self.n = self.base + iterations * self.per

def identity(pool, tile, done):
    pool.memset(tile, 0.0).then_inc(done, 1)
    pool.wait_ge(done, 1)
    pool.affine_select(out=tile, in_=tile, compare_op=ALU.not_equal, fill=1.0, base=0,
                       pattern=[[-1, P]], channel_multiplier=1).then_inc(done, 1)

def condition_and_norm(nc, io, keep):
    ctx = ExitStack()
    sb = lambda name, shape, dt=F32: ctx.enter_context(nc.sbuf_tensor(name, shape, dt))
    sem = lambda name: ctx.enter_context(nc.semaphore(name))
    NADA = 2 * KT
    WR, XR = 3, 6
    PAIR = 2 * P
    NPAIR = S // PAIR
    k_dve = lambda b: 0 if b < NPAIR // 2 else 3 if b < NPAIR - 1 else 5
    KA = 6
    with ctx:
        wada = [sb(f"wada{k}", [P, 2 * D]) for k in range(WR)]
        xin = [sb(f"xin{k}", [P, D]) for k in range(XR)]
        squares = sb("squares", [P, D])
        hf = [sb(f"hf{k}", [P, KT, PAIR]) for k in range(2)]
        c_raw, bias, ng = sb("c_raw", [P, KT]), sb("bias", [P, NADA]), sb("ng", [P, KT])
        acc, mulA = sb("acc", [P, NADA]), sb("mulA", [P, KT])
        ss, sd, rstd = sb("ss", [P, TT]), sb("sd", [P, TT]), sb("rstd", [P, TT])
        ps_x = [ctx.enter_context(nc.psum_tensor(f"ps_x{k}", [P, KT, PAIR], F32)) for k in range(2)]
        ada_row = ps_x[1].rearrange("p k n -> p (k n)")[0:1, :]
        ada_cols = ps_x[1][:, 0, 0:NADA]
        row = wada[0][0:1, :]
        one = sb("one_p", [1, 1])
        small_in, id_done, siluc_done = sem("p_small"), sem("p_id"), sem("p_siluc")
        wada_in = [sem(f"p_wada{k}") for k in range(WR)]
        x_in = [sem(f"p_x{k}") for k in range(XR)]
        ada_mm, row_act, row_dve, cols_done, cols_read, ab_ready = (sem("p_" + n) for n in ("ada", "rowa", "rowd", "cols", "colsr", "ab"))
        var_done, sd_done, rstd_done, xn_done = (sem("p_" + n) for n in ("var", "sd", "rstd", "xn"))
        xt_done, full_act, full_dve, hi_done, lo_done = (sem("p_" + n) for n in ("xt", "fa", "fd", "hi", "lo"))
        lo_dve, dve_steps = sem("p_lod"), sem("p_dve")
        block = ctx.enter_context(nc.Block())

        @block.sync
        def _(sp):
            with nc.allow_non_contiguous_dma(reason="columns of small vectors"):
                sp.dma_start(c_raw[:], io["c"].rearrange("a (k p) -> p (a k)", p=P)).then_inc(small_in, 16)
                sp.dma_start(bias[:], io["b_ada"][:, 0:2 * D].rearrange("a (k p) -> p (a k)", p=P)).then_inc(small_in, 16)
                sp.dma_start(ng[:], io["norm_g"].rearrange("a (k p) -> p (a k)", p=P)).then_inc(small_in, 16)
            for k in range(KT):
                if k >= WR:
                    sp.wait_ge(ada_mm, k - WR + 1)
                sp.dma_start(wada[k % WR][:], io["w_ada"][0, k * P:(k + 1) * P, 0:2 * D]).then_inc(wada_in[k % WR], 16)

        @block.gpsimd
        def _(pool):
            def load(t):
                if t >= XR:
                    pool.wait_ge(xt_done, t - XR + 1)
                if t < TT:
                    pool.dma_start(xin[t % XR][:], io["x"][0, t * P:(t + 1) * P, :]).then_inc(x_in[t % XR], 16)

            for t in range(XR):
                if t == 2:
                    identity(pool, keep["ident"][:], id_done)
                    pool.wait_ge(wada_in[WR - 1], 16)
                load(t)
            for t in range(XR, XR + 4):
                load(t)
            for b in range(NPAIR):
                pool.wait_ge(hi_done, b + 1)
                tok = slice(b * PAIR, (b + 1) * PAIR)
                ks = slice(k_dve(b), KT)
                nc.gpsimd.tensor_tensor(keep["hTl"][:, ks, tok], hf[b % 2][:, ks, :], keep["hTh"][:, ks, tok].bitcast(F32),
                                        ALU.subtract).then_inc(lo_done, 1)
                for t in (XR + 2 * b + 4, XR + 2 * b + 5):
                    if t < TT:
                        load(t)
                if b == NPAIR - 4:
                    for k in range(RAW):
                        pool.dma_start(keep["wraw"][k][:], io["w_in"][0, k * P:(k + 1) * P, C_Q:C_Q + COLS]
                                       ).then_inc(keep["w_in"][k], 16)

        @block.tensor
        def _(pe):
            def flip(t):
                b = t // 2
                pe.wait_ge(xn_done, t + 1)
                if b >= 2 and t % 2 == 0:
                    pe.wait_ge(full_act, KA * (b - 1))
                    pe.wait_ge(full_dve, (KT - KA) * (b - 1))
                for k in range(KT):
                    mm = nc.tensor.transpose(ps_x[b % 2][:, k, t % 2 * P:(t % 2 + 1) * P],
                                             xin[t % XR][:, k * P:(k + 1) * P], keep["ident"][:])
                mm.then_inc(xt_done, 1)

            pe.wait_ge(siluc_done, 1)
            for k in range(KT):
                pe.wait_ge(wada_in[k % WR], 16 * (k // WR + 1))
                for n in range(0, 2 * D, 512):
                    mm = nc.tensor.matmul(ada_row[:, n:n + 512], keep["siluc"][:, k:k + 1], wada[k % WR][:, n:n + 512],
                                          start=k == 0, stop=k == KT - 1)
                mm.then_inc(ada_mm, 1)
                if k == KT // 2:
                    pe.wait_ge(id_done, 2)
                    flip(0)
                    flip(1)
            pe.wait_ge(row_act, 1)
            pe.wait_ge(row_dve, 2)
            for m in range(NADA):
                mm = nc.tensor.matmul(ada_cols[:, m:m + 1], row[:, m * P:(m + 1) * P], one[:], start=True, stop=True)
            mm.then_inc(cols_done, 1)
            pe.wait_ge(cols_read, 1)
            for t in range(2, TT):
                flip(t)

        @block.scalar
        def _(act):
            act.wait_ge(small_in, 48)
            nc.scalar.activation(keep["siluc"][:], c_raw[:], ACT.Silu).then_inc(siluc_done, 1)

            def root(t):
                act.wait_ge(var_done, t + 1)
                nc.scalar.activation(sd[:, t:t + 1], ss[:, t:t + 1], ACT.Sqrt).then_inc(sd_done, 1)

            def normalise(t):
                if t + 1 < TT:
                    root(t + 1)
                act.wait_ge(rstd_done, t + 1)
                nc.scalar.activation(xin[t % XR][:], xin[t % XR][:], ACT.Copy, scale=rstd[:, t:t + 1]).then_inc(xn_done, 1)

            root(0)
            for t in range(XR - 2):
                normalise(t)
            act.wait_ge(ada_mm, KT)
            nc.scalar.activation(row[:, 0:D], ada_row[:, 0:D], ACT.Copy).then_inc(row_act, 1)
            normalise(XR - 2)
            act.wait_ge(ab_ready, 1)
            for b in range(NPAIR):
                act.wait_ge(xt_done, 2 * b + 2)
                if b >= 2:
                    act.wait_ge(lo_done, b - 1)
                if b >= 2 + NPAIR // 2:
                    act.wait_ge(lo_dve, b - 1 - NPAIR // 2)
                for k in range(KA):
                    nc.scalar.activation(hf[b % 2][:, k, :], ps_x[b % 2][:, k, :], ACT.Identity,
                                         scale=mulA[:, k:k + 1], bias=acc[:, k:k + 1]).then_inc(full_act, 1)
                for t in (XR - 1 + 2 * b, XR + 2 * b):
                    if t < TT:
                        normalise(t)

        @block.vector
        def _(dve):
            st = Steps(dve, dve_steps)

            def stats(t):
                dve.wait_ge(x_in[t % XR], 16 * (t // XR + 1))
                st.settle(nc.vector.tensor_tensor_reduce(squares[:], xin[t % XR][:], xin[t % XR][:], 1.0, 0.0,
                                                         ALU.mult, ALU.add, ss[:, t:t + 1]))
                nc.vector.tensor_scalar(ss[:, t:t + 1], ss[:, t:t + 1], 1.0 / D, EPS, ALU.mult, ALU.add).then_inc(var_done, 1)

            def inverse(t):
                dve.wait_ge(sd_done, t + 1)
                nc.vector.reciprocal(rstd[:, t:t + 1], sd[:, t:t + 1]).then_inc(rstd_done, 1)

            def step(t):
                if t < TT:
                    stats(t)
                if t <= TT:
                    inverse(t - 1)

            stats(0)
            for t in (1, 2):
                step(t)
            for t in range(3, XR):
                step(t)
            nc.vector.memset(one[:], 1.0).then_inc(row_dve, 1)
            dve.wait_ge(ada_mm, KT)
            nc.vector.tensor_copy(row[:, D:2 * D], ada_row[:, D:2 * D]).then_inc(row_dve, 1)
            dve.wait_ge(cols_done, 1)
            nc.vector.tensor_tensor(acc[:], ada_cols, bias[:], ALU.add).then_inc(cols_read, 1)
            dve.wait_ge(cols_read, 1)
            st.settle(nc.vector.tensor_scalar(mulA[:], acc[:, KT:NADA], 1.0, None, ALU.add))
            nc.vector.tensor_tensor(mulA[:], mulA[:], ng[:], ALU.mult).then_inc(ab_ready, 1)
            dve.wait_ge(ab_ready, 1)
            for b in range(NPAIR):
                tok = slice(b * PAIR, (b + 1) * PAIR)
                dve.wait_ge(xt_done, 2 * b + 2)
                if b >= 2:
                    dve.wait_ge(lo_done, b - 1)
                if b >= 2 + NPAIR // 2:
                    dve.wait_ge(lo_dve, b - 1 - NPAIR // 2)
                for k in range(KA, KT):
                    nc.vector.tensor_scalar(hf[b % 2][:, k, :], ps_x[b % 2][:, k, :], mulA[:, k:k + 1], acc[:, k:k + 1],
                                            ALU.mult, ALU.add).then_inc(full_dve, 1)
                step(XR + 2 * b)
                step(XR + 2 * b + 1)
                dve.wait_ge(full_act, KA * (b + 1))
                dve.wait_ge(full_dve, (KT - KA) * (b + 1))
                nc.vector.tensor_copy(keep["hTh"][:, :, tok], hf[b % 2][:]).then_inc(hi_done, 1)
                if k_dve(b):
                    ks = slice(0, k_dve(b))
                    dve.wait_ge(hi_done, b + 1)
                    nc.vector.tensor_tensor(keep["hTl"][:, ks, tok], hf[b % 2][:, ks, :],
                                            keep["hTh"][:, ks, tok].bitcast(F32), ALU.subtract).then_inc(lo_dve, 1)

def project(nc, io, keep, dram):
    ctx = ExitStack()
    sb = lambda name, shape, dt=F32: ctx.enter_context(nc.sbuf_tensor(name, shape, dt))
    sem = lambda name: ctx.enter_context(nc.semaphore(name))
    hTh, hTl = keep["hTh"], keep["hTl"]
    BANKS, ST, WG = 4, 4, 2
    NT = S // COLS
    N_NORM, N_Z, N_G = 3, 2, 2 * D // COLS
    G_NORM = 0
    G_KV = G_NORM + N_NORM
    G_V = G_KV + 1
    G_Z = G_V + 1
    G_G = G_Z + N_Z
    T_F = TT * G_G
    T_G = T_F + NT
    with ctx:
        wraw = keep["wraw"]
        Wh, Wl = sb("Wh", [P, KT, COLS], F32R), sb("Wl", [P, KT, COLS], F32R)
        st = [sb(f"st{k}", [P, COLS]) for k in range(ST)]
        qn = [sb(f"qn{k}", [P, COLS]) for k in range(2)]
        qT = [sb(f"qT{k}", [P, COLS]) for k in range(2)]
        sq = sb("sq", [P, COLS])
        var, sd, rs = sb("var", [P, 2, FOX_H]), sb("nsd", [P, 2, FOX_H]), sb("nrs", [P, 2, FOX_H])
        gains = sb("gains", [P, 4, HD])
        bf, one = sb("bf", [FOX_H, 1]), sb("one", [FOX_H, 1])
        wf, wfh, wfl = sb("wf", [P, KT, FOX_H]), sb("wfh", [P, KT, FOX_H], F32R), sb("wfl", [P, KT, FOX_H], F32R)
        f_tok = sb("f_tok", [P, TT, FOX_H])
        fl = sb("fl", [FOX_H, S])
        fu = [t[0:FOX_H, :] for t in (*qn, *qT)]
        wg = [sb(f"wg{k}", [P, D]) for k in range(WG)]
        gacc = wg[0][0:1, :]
        bank = [ctx.enter_context(nc.psum_tensor(f"pj{k}", [P, COLS], F32)) for k in range(BANKS)]
        tbank = [ctx.enter_context(nc.psum_tensor(f"pt{k}", [P, 4, P], F32)) for k in range(2)]
        gbank = [ctx.enter_context(nc.psum_tensor(f"pg{k}", [P, 512], F32)) for k in range(2)]
        small_in, credits = sem("j_small"), sem("j_credits")
        w_in = keep["w_in"]
        w_hi, w_split, w_free = sem("j_whi"), sem("j_wsplit"), sem("j_wfree")
        mm_done, dve_free, act_free = sem("j_mm"), sem("j_dfree"), sem("j_afree")
        sq_done, var_done, sd_done, qn_done = sem("j_sq"), sem("j_var"), sem("j_sd"), sem("j_qn")
        qt_done, qT_done = sem("j_qt"), sem("j_qTd")
        qT_stored = [sem(f"j_qs{k}") for k in range(2)]
        st_dve, st_act = sem("j_std"), sem("j_sta")
        stored = [sem(f"j_st{k}") for k in range(ST)]
        sig_done, ln_done, f_done, f_stored = sem("j_sig"), sem("j_ln"), sem("j_f"), sem("j_fs")
        wg_in = [sem(f"j_wg{k}") for k in range(WG)]
        g_mm, g_acc, g_stored, gb_in = sem("j_gmm"), sem("j_gacc"), sem("j_gs"), sem("j_gb")
        gains_ready = sem("j_gains")
        wf_hi, wf_split, wf_placed, f_tok_done = sem("j_wfh"), sem("j_wfs"), sem("j_wfp"), sem("j_ftok")
        act_steps, dve_steps = sem("j_act"), sem("j_dve")
        block = ctx.enter_context(nc.Block())

        @block.gpsimd
        def _(pool):
            pool.sem_inc(w_split, RAW)

            def load(g, col0, k0=0):
                for k in range(k0, KT):
                    n = g * KT + k
                    pool.wait_ge(w_split, n + 1)
                    pool.dma_start(wraw[k % RAW][:], io["w_in"][0, k * P:(k + 1) * P, bass.ds(col0, COLS)]
                                   ).then_inc(w_in[k % RAW], 16)

            load(0, C_Q, RAW)
            load(1, C_K)
            load(2, C_QB)
            load(G_KV, C_KB)
            load(G_V, C_V)
            with pool.Fori(0, N_Z) as i:
                load(i + G_Z, i * (C_ZB - C_ZA) + C_ZA)
            with pool.Fori(0, N_G) as i:
                load(i + G_G, i * COLS + C_GA)

        @block.sync
        def _(sp):
            for n, name in enumerate(("fox_q_g", "fox_k_g", "swa_q_g", "swa_k_g")):
                sp.dma_start(gains[:, n, :], io[name].to_broadcast([P, HD])).then_inc(small_in, 16)
            with nc.allow_non_contiguous_dma(reason="columns of small vectors"):
                sp.dma_start(bf[:], io["b_forget"].rearrange("a h -> h a")).then_inc(small_in, 16)
                sp.dma_start(wf[:], io["w_in"][0, :, C_F:C_F + FOX_H].rearrange("(k p) n -> p k n", p=P)).then_inc(small_in, 16)

            def store_norm(g, row0, heads):
                for t in range(TT):
                    sp.wait_ge(qT_done, g * TT + t + 2 + 1)
                    sp.dma_start(dram["qk"][bass.ds(row0, heads * HD), t * P:(t + 1) * P]
                                 .rearrange("(b p) n -> p b n", p=P),
                                 qT[t % 2][:, 0:heads * HD].rearrange("p (b n) -> p b n", n=P)
                                 ).then_inc(qT_stored[t % 2], 16)
            def load_gate(k0):
                for k in (k0, k0 + 1):
                    if k >= WG:
                        sp.wait_ge(g_mm, k - WG + 1)
                    sp.dma_start(wg[k % WG][:], io["w_ada"][0, k * P:(k + 1) * P, 2 * D:3 * D]).then_inc(wg_in[k % WG], 16)

            load_gate(0)
            with sp.Fori(0, N_NORM) as i:
                store_norm(i, i * COLS + R_Q, FOX_H)
            load_gate(2)
            for t in range(TT):
                sp.wait_ge(qT_done, N_NORM * TT + t + 2 + 1)
                sp.dma_start(dram["qk"][R_KB:R_KB + KW, t * P:(t + 1) * P], qT[t % 2][:, 0:P]).then_inc(qT_stored[t % 2], 16)
                sp.wait_ge(st_dve, t + 1)
                sp.dma_start(dram["v"][t * P:(t + 1) * P, FW:FW + KW], st[t % ST][:, 0:KW]).then_inc(stored[t % ST], 16)
            load_gate(4)
            for t in range(TT):
                sp.wait_ge(st_dve, TT + t + 1)
                sp.dma_start(dram["v"][t * P:(t + 1) * P, 0:FW], st[t % ST][:]).then_inc(stored[t % ST], 16)
            load_gate(6)
            with sp.Fori(0, N_Z) as i:
                for t in range(TT):
                    sp.wait_ge(st_dve, i * TT + (2 * TT + t + 1))
                    sp.dma_start(dram["z"][t * P:(t + 1) * P, bass.ds(i * COLS, COLS)], st[t % ST][:]).then_inc(stored[t % ST], 16)
            sp.wait_ge(g_mm, KT)
            sp.dma_start(gacc, io["b_ada"][:, 2 * D:3 * D]).then_inc(gb_in, 16)
            for b in range(NT):
                sp.wait_ge(f_done, b + 1)
                sp.dma_start(dram["f"][:, b * COLS:(b + 1) * COLS], fl[:, b * COLS:(b + 1) * COLS]).then_inc(f_stored, 16)
            sp.wait_ge(g_acc, D // 512)
            sp.dma_start(dram["gate"], gacc).then_inc(g_stored, 16)
            with sp.Fori(0, N_G) as i:
                for t in range(TT):
                    m, b = t // NT, t % NT
                    sp.wait_ge(st_act, i * TT + (t + 1))
                    sp.dma_start(dram["g"][bass.ds(i * COLS + m * P, P), b * COLS:(b + 1) * COLS], st[t % ST][:]).then_inc(stored[t % ST], 16)
            sp.wait_ge(g_stored, 16)
            sp.wait_ge(f_stored, 16 * NT)
            for k in range(2):
                sp.wait_ge(qT_stored[k], 16 * (N_NORM + 1) * TT // 2 + 16)
            for k in range(ST):
                sp.wait_ge(stored[k], 16 * (2 + N_Z + N_G) * TT // ST)

        @block.tensor
        def _(pe):
            pe.sem_inc(w_free, KT - 1)
            pe.sem_inc(qt_done, 2)

            def three(out, a_hi, a_lo, b_hi, b_lo, first, last):
                nc.tensor.matmul(out, a_hi, b_hi, start=first, stop=False)
                nc.tensor.matmul(out, a_hi, b_lo, start=False, stop=False)
                return nc.tensor.matmul(out, a_lo, b_hi, start=False, stop=last)

            def tile(g, t, tiles, free_sem, free_at, operands, width):
                pe.wait_ge(free_sem, free_at)
                for k in range(KT):
                    if t == 0:
                        pe.wait_ge(w_split, g * KT + k + 1 + RAW)
                    mm = three(bank[t % BANKS][:, 0:width], *operands(k), k == 0, k == KT - 1)
                    if t == tiles - 1 and k < KT - 1:
                        mm.then_inc(w_free, 1)
                mm.then_inc(mm_done, 1)

            def tokens_by_cols(t, width):
                tok = slice(t * P, (t + 1) * P)
                return lambda k: (hTh[:, k, tok], hTl[:, k, tok], Wh[:, k, 0:width], Wl[:, k, 0:width])

            def cols_by_tokens(m, b):
                c, tok = slice(m * P, (m + 1) * P), slice(b * COLS, (b + 1) * COLS)
                return lambda k: (Wh[:, k, c], Wl[:, k, c], hTh[:, k, tok], hTl[:, k, tok])

            def flip(g, t, heads):
                pe.wait_ge(qn_done, g * TT + t + 1)
                pe.wait_ge(qT_done, g * TT + t + 1)
                for b in range(heads * HD // P):
                    mm = nc.tensor.transpose(tbank[t % 2][:, b, :], qn[t % 2][:, b * P:(b + 1) * P], keep["ident"][:])
                mm.then_inc(qt_done, 1)

            def token_tile(g, t, width=COLS):
                tile(g, t, TT, dve_free, g * TT + t + 1, tokens_by_cols(t, width), width)

            def gate_tiles(k0):
                for k in (k0, k0 + 1):
                    pe.wait_ge(wg_in[k % WG], 16 * (k // WG + 1))
                    for n in range(D // 512):
                        mm = nc.tensor.matmul(gbank[n][0:1, :], keep["siluc"][:, k:k + 1], wg[k % WG][:, n * 512:(n + 1) * 512],
                                              start=k == 0, stop=k == KT - 1)
                    mm.then_inc(g_mm, 1)

            token_tile(0, 0)
            token_tile(0, 1)
            with pe.Fori(0, N_NORM) as i:
                for t in range(2, TT + 2):
                    token_tile(i + t // TT, t % TT)
                    flip(i, t - 2, FOX_H)
            gate_tiles(0)
            pe.wait_ge(wf_placed, 2)
            for t in range(2, TT):
                token_tile(G_KV, t, 2 * KW + FOX_H)
                flip(G_KV, t - 2, KV_H)
            gate_tiles(2)
            for t in range(TT):
                token_tile(G_V, t)
                if t < 2:
                    flip(G_KV, TT - 2 + t, KV_H)
            gate_tiles(4)
            with pe.Fori(0, N_Z) as i:
                for t in range(TT):
                    token_tile(i + G_Z, t)
            gate_tiles(6)
            pe.wait_ge(dve_free, T_F + BANKS)
            pe.wait_ge(f_tok_done, TT - 2)
            for t in range(NT):
                pe.wait_ge(act_free, t + 1)
                if t == 0:
                    tok = slice(0, 2 * P)
                    for k in range(KT):
                        three(bank[0][0:FOX_H, tok], wfh[:, k, :], wfl[:, k, :], hTh[:, k, tok], hTl[:, k, tok],
                              k == 0, k == KT - 1)
                for j in range(2 if t == 0 else 0, NT):
                    mm = nc.tensor.transpose(bank[t % BANKS][0:FOX_H, j * P:(j + 1) * P], f_tok[:, t * NT + j, :],
                                             keep["ident"][:])
                mm.then_inc(mm_done, 1)
            with pe.Fori(0, N_G) as i:
                for t in range(TT):
                    tile(i + G_G, t, TT, act_free, i * TT + (NT + t + 1), cols_by_tokens(t // NT, t % NT), COLS)

        @block.scalar
        def _(act):
            act.sem_inc(qT_done, 2)
            act.sem_inc(act_free, BANKS)
            act.sem_inc(qT_stored[0], 16)
            act.sem_inc(qT_stored[1], 16)

            def split_high(g, tiles_before, first=False):
                for k in range(KT):
                    act.wait_ge(w_in[k % RAW], g * (16 * KT // RAW) + 16 * (k // RAW + 1))
                    if k < KT - 1:
                        act.wait_ge(w_free, g * (KT - 1) + (k + 1))
                    elif not first:
                        act.wait_ge(mm_done, tiles_before)
                    nc.scalar.activation(Wh[:, k, :], wraw[k % RAW][:], ACT.Copy).then_inc(w_hi, 1)

            def squares(g, t, heads):
                w = heads * HD
                n = g * TT + t
                act.wait_ge(mm_done, n + 1)
                act.wait_ge(var_done, n + 1)
                nc.scalar.activation(sq[:, 0:w], bank[t % BANKS][:, 0:w], ACT.Square).then_inc(sq_done, 1)
                act.wait_ge(var_done, n + 2)
                nc.scalar.activation(sd[:, t % 2, 0:heads], var[:, t % 2, 0:heads], ACT.Sqrt).then_inc(sd_done, 1)

            def copy_out(g, t, heads):
                w = heads * HD
                act.wait_ge(qt_done, g * TT + t + 2 + 1)
                act.wait_ge(qT_stored[t % 2], g * (8 * TT) + 16 * (t // 2 + 1))
                nc.scalar.activation(qT[t % 2][:, 0:w], tbank[t % 2][:, 0:w // P, :].rearrange("p b n -> p (b n)"),
                                     ACT.Copy).then_inc(qT_done, 1)

            split_high(0, 0, first=True)
            act.wait_ge(small_in, 96)
            nc.scalar.activation(wfh[:], wf[:], ACT.Copy).then_inc(wf_hi, 1)
            squares(0, 0, FOX_H)
            squares(0, 1, FOX_H)
            with act.Fori(0, N_NORM) as i:
                for t in range(2, TT + 2):
                    if t == TT - 1:
                        split_high(i + 1, i * TT + TT)
                    squares(i + t // TT, t % TT, FOX_H)
                    copy_out(i, t - 2, FOX_H)
            act.wait_ge(mm_done, G_KV * TT + 2)
            act.wait_ge(wf_split, 1)
            nc.scalar.activation(Wh[:, :, 2 * KW:2 * KW + FOX_H], wfh[:].bitcast(F32), ACT.Copy).then_inc(wf_placed, 1)
            nc.scalar.activation(Wl[:, :, 2 * KW:2 * KW + FOX_H], wfl[:].bitcast(F32), ACT.Copy).then_inc(wf_placed, 1)
            for t in range(2, TT):
                if t == TT - 1:
                    split_high(G_V, G_V * TT)
                squares(G_KV, t, KV_H)
                copy_out(G_KV, t - 2, KV_H)
            copy_out(G_KV, TT - 2, KV_H)
            copy_out(G_KV, TT - 1, KV_H)
            split_high(G_Z, G_Z * TT)
            with act.Fori(0, N_Z) as i:
                for t in range(TT):
                    if t == TT - 1:
                        split_high(i + (G_Z + 1), i * TT + (G_Z + 1) * TT)
                    act.wait_ge(mm_done, i * TT + (G_Z * TT + t + 1))
                    act.wait_ge(stored[t % ST], i * (16 * TT // ST) + 16 * (2 * TT // ST + t // ST))
                    nc.scalar.activation(st[t % ST][:], bank[t % BANKS][:], ACT.Sigmoid).then_inc(sig_done, 1)
            steps = Steps(act, act_steps)
            act.wait_ge(small_in, 96)
            act.wait_ge(qt_done, G_V * TT + 2)
            for k in range(2):
                act.wait_ge(qT_stored[k], 16 * (G_V * TT // 2) + 16)
            for b in range(NT):
                cols = slice(b * COLS, (b + 1) * COLS)
                act.wait_ge(mm_done, T_F + b + 1)
                steps.did(nc.scalar.activation(fu[b], bank[b % BANKS][0:FOX_H, :], ACT.Identity, bias=bf[:, 0:1]))
                steps.settle(nc.scalar.activation(fl[:, cols], bank[b % BANKS][0:FOX_H, :], ACT.Abs, bias=bf[:, 0:1]))
                act.sem_inc(act_free, 1)
            steps.settle(nc.scalar.activation(fl[:], fl[:], ACT.Exp, scale=-1.0))
            nc.scalar.activation(fl[:], fl[:], ACT.Ln, bias=1.0).then_inc(ln_done, 1)

            def gate_group(i, another):
                for t in range(TT):
                    if another and t == TT - 1:
                        split_high(i + (G_G + 1), i * TT + (T_G + TT))
                    act.wait_ge(mm_done, i * TT + (T_G + t + 1))
                    act.wait_ge(stored[t % ST], i * (16 * TT // ST) + 16 * ((2 + N_Z) * TT // ST + t // ST))
                    nc.scalar.activation(st[t % ST][:], bank[t % BANKS][:], ACT.Sigmoid).then_inc(st_act, 1)
                    act.wait_ge(st_act, i * TT + (t + 1))
                    act.sem_inc(act_free, 1)

            with act.Fori(0, N_G - 1) as i:
                gate_group(i, True)
            gate_group(N_G - 1, False)

        @block.vector
        def _(dve):
            dve.sem_inc(dve_free, BANKS)
            dve.sem_inc(var_done, 1)
            steps = Steps(dve, dve_steps)

            def split_low(g):
                for k in range(KT):
                    n = g * KT + k
                    dve.wait_ge(w_hi, n + 1)
                    nc.vector.tensor_tensor(Wl[:, k, :], wraw[k % RAW][:], Wh[:, k, :].bitcast(F32),
                                            ALU.subtract).then_inc(w_split, 1)

            def normalise(g, t, heads, gain, copy_v):
                w, u = heads * HD, t % 2
                n = g * TT + t
                by_head = lambda ap: ap[:, 0:w].rearrange("p (h d) -> p h d", d=HD)
                dve.wait_ge(sq_done, n + 1)
                steps.settle(nc.vector.tensor_reduce(var[:, u, 0:heads], by_head(sq), AX.X, ALU.add))
                nc.vector.tensor_scalar(var[:, u, 0:heads], var[:, u, 0:heads], 1.0 / HD, EPS, ALU.mult, ALU.add
                                        ).then_inc(var_done, 1)
                if copy_v:
                    if t >= ST:
                        dve.wait_ge(stored[t % ST], 16 * (t // ST))
                    nc.vector.tensor_copy(st[t % ST][:, 0:KW], bank[t % BANKS][:, KW:2 * KW]).then_inc(st_dve, 1)
                    nc.vector.tensor_copy(f_tok[:, t, :], bank[t % BANKS][:, 2 * KW:2 * KW + FOX_H]).then_inc(f_tok_done, 1)
                dve.wait_ge(sd_done, n + 1)
                steps.settle(nc.vector.reciprocal(rs[:, u, 0:heads], sd[:, u, 0:heads]))
                dve.wait_ge(qt_done, n + 1)
                nc.vector.tensor_tensor(by_head(qn[u]), by_head(bank[t % BANKS]),
                                        rs[:, u, 0:heads].unsqueeze(2).to_broadcast([P, heads, HD]), ALU.mult
                                        ).then_inc(dve_free, 1)
                dve.wait_ge(dve_free, n + 1 + BANKS)
                nc.vector.tensor_tensor(by_head(qn[u]), by_head(qn[u]),
                                        gains[:, bass.ds(gain, 1), :].to_broadcast([P, heads, HD]), ALU.mult
                                        ).then_inc(qn_done, 1)

            split_low(0)
            dve.wait_ge(small_in, 96)
            for n in (0, 2):
                nc.vector.tensor_scalar(gains[:, n, :], gains[:, n, :], QK_SCALE, None, ALU.mult).then_inc(gains_ready, 1)
            dve.wait_ge(gains_ready, 2)
            dve.wait_ge(wf_hi, 1)
            nc.vector.tensor_tensor(wfl[:], wf[:], wfh[:].bitcast(F32), ALU.subtract).then_inc(wf_split, 1)
            normalise(0, 0, FOX_H, 0, False)
            normalise(0, 1, FOX_H, 0, False)
            with dve.Fori(0, N_NORM) as i:
                steps.loop(i, 2 * TT + 2)
                for t in range(2, TT + 2):
                    if t == TT - 1:
                        split_low(i + 1)
                    if t >= TT:
                        dve.wait_ge(sq_done, i * TT + (t + 1))
                        steps.settle(nc.vector.tensor_copy(st[t % TT][:, 0:KW], bank[t % BANKS][:, KW:2 * KW]))
                    normalise(i + t // TT, t % TT, FOX_H, i + t // TT, False)
            steps.end(N_NORM)
            dve.sem_inc(st_dve, 2)
            for t in range(2, TT):
                if t == TT - 1:
                    split_low(G_V)
                normalise(G_KV, t, KV_H, 3, True)
            for t in range(TT):
                if t == TT - 1:
                    split_low(G_Z)
                dve.wait_ge(mm_done, G_V * TT + t + 1)
                dve.wait_ge(stored[t % ST], 16 * (TT // ST + t // ST))
                nc.vector.tensor_copy(st[t % ST][:], bank[t % BANKS][:]).then_inc(dve_free, 1)
                dve.wait_ge(dve_free, G_V * TT + t + 1 + BANKS)
                dve.sem_inc(st_dve, 1)
            with dve.Fori(0, N_Z) as i:
                for t in range(TT):
                    if t == TT - 1:
                        split_low(i + (G_Z + 1))
                    dve.wait_ge(sig_done, i * TT + (t + 1))
                    nc.vector.tensor_tensor(st[t % ST][:], st[t % ST][:], bank[t % BANKS][:], ALU.mult).then_inc(dve_free, 1)
                    dve.wait_ge(dve_free, i * TT + (G_Z * TT + t + 1 + BANKS))
                    dve.sem_inc(st_dve, 1)
            steps.settle(nc.vector.memset(one[:], 1.0))
            dve.wait_ge(g_mm, KT)
            dve.wait_ge(gb_in, 16)
            for n in range(D // 512):
                nc.vector.tensor_tensor(gacc[:, n * 512:(n + 1) * 512], gbank[n][0:1, :], gacc[:, n * 512:(n + 1) * 512],
                                        ALU.add).then_inc(g_acc, 1)
            dve.wait_ge(ln_done, 1)
            for b in range(NT):
                part = fl[:, b * COLS:(b + 1) * COLS]
                steps.settle(nc.vector.tensor_scalar(fu[b], fu[b], 0.0, None, ALU.min))
                steps.settle(nc.vector.tensor_tensor(fu[b], part, fu[b], ALU.subtract))
                nc.vector.tensor_tensor_scan(part, one[:].to_broadcast([FOX_H, COLS]), fu[b],
                                             fl[:, b * COLS - 1:b * COLS] if b else 0.0,
                                             ALU.mult, ALU.add).then_inc(f_done, 1)
                dve.wait_ge(f_done, b + 1)
            with dve.Fori(0, N_G - 1) as i:
                split_low(i + (G_G + 1))

def attend(nc, io, keep, dram):
    ctx = ExitStack()
    sb = lambda name, shape, dt=F32: ctx.enter_context(nc.sbuf_tensor(name, shape, dt))
    sem = lambda name: ctx.enter_context(nc.semaphore(name))
    yT = keep["yT"]
    QUAD = 4
    HALF = 1024
    with ctx:
        raw = {"q": sb("raw_q", [P, S]), "k": sb("raw_k", [P, S])}
        Q = [sb(f"Q{k}", [P, S], F32R) for k in range(2)]
        Kh, Kl = sb("Kh", [P, 2, S], F32R), sb("Kl", [P, 2, S], F32R)
        V = [sb(f"V{k}", [P, TT, 2 * HD]) for k in range(2)]
        ZY = [sb(f"ZY{k}", [P, TT, 2 * HD]) for k in range(2)]
        PT = [sb(f"PT{k}", [P, 4 * P]) for k in range(3)]
        identr, maskr = sb("identr", [P, P], F32R), sb("maskr", [P, P], F32R)
        nmax, rsum, rinv = sb("nmax", [P, 4, 2]), sb("rsum", [P, 4, 2]), sb("rinv", [P, 2, 2])
        sinks = sb("sinks", [P, SWA_H])
        WIN = 2 * P
        SPAN = WIN + 1
        logits = [ctx.enter_context(nc.psum_tensor(f"lg{k}", [P, HALF], F32)) for k in range(2)]
        flips = [ctx.enter_context(nc.psum_tensor(f"fl{k}", [P, 4 * P], F32)) for k in range(2)]
        outs = [ctx.enter_context(nc.psum_tensor(f"ot{k}", [P, 512], F32)) for k in range(2)]

        def part(tag, swa):
            s = lambda name: sem(f"{tag}_{name}")
            own = lambda name, shape, dt=F32: ctx2.enter_context(nc.sbuf_tensor(name, shape, dt))
            if swa:
                bias_b = own("bias_b", [P, SWA_H, WIN])
                dist, dist_neg = own("dist", [P, WIN])[:], own("dist_neg", [P, WIN])[:]
                ring_b = [own(f"Snb{k}", [P, 2 * SPAN]) for k in range(3)]
                Q_b = [t[:] for t in (*Q, own("Q2", [P, S], F32R), own("Q3", [P, S], F32R))]
            else:
                nF = [own(f"nF{k}", [P, S]) for k in range(2)]
                Sn = [own(f"Sn{k}", [P, S]) for k in range(3)]
                mask0 = Sn[0][:, 0:P]
                Q_b = [t[:] for t in Q]
            raw_in, split_done = {x: s("raw" + x) for x in "qk"}, {x: s("split" + x) for x in "qk"}
            hi_done = {x: s("hi" + x) for x in "qk"}
            bias_in, vz_in, v_in = [s("bias0"), s("bias1")], [s("vz0"), s("vz1")], s("vin")
            chunk_ready, chunk_read = s("cready"), s("cread")
            exp_done, flip_done, copy_act, copy_dve = s("exp"), s("flip"), s("cact"), s("cdve")
            pv_group, y_done, yt_done = s("pvg"), s("y"), s("yt")
            bias_used, init = s("bused"), s("init")
            dve_steps = s("dve")
            ITER = (SWA_H if swa else FOX_H) // QUAD

            LAG = 1
            if swa:
                rows = [[(hh + g, qb, max(0, qb - 1), g * SPAN) for g in range(2)] for hh in range(0, QUAD, 2) for qb in range(TT)]
            else:
                of_head = [(q, q + 1) for q in range(0, TT // 2, 2)] + [(q,) for q in range(TT // 2, TT)]
                rows = [[(hh, q, 0, g * (qs[0] + 1) * P) for g, q in enumerate(qs)] for hh in range(QUAD) for qs in of_head]
            NR = len(rows)
            PER_HEADS = NR // (2 if swa else QUAD)
            row_chunks, row_groups, NCH, n_pt = [], [], 0, 0
            for row in rows:
                widths = [(qb + 1 - first) * P for _, qb, first, _ in row]
                step_g = WIN if swa else 512
                if len(row) == 2 and max(widths) <= step_g:
                    chunks = [[(g, 0, w, g * step_g) for g, w in enumerate(widths)]]
                else:
                    chunks = [[(g, c, min(HALF, w - c), 0)] for g, w in enumerate(widths) for c in range(0, w, HALF)]
                row_chunks.append([(NCH + j, pieces) for j, pieces in enumerate(chunks)])
                NCH += len(chunks)
                blocks = [(g, b) for g, (_, qb, first, _) in enumerate(row) for b in range(first, qb + 1)]
                row_groups.append([(n_pt + j, blocks[b:b + 4]) for j, b in enumerate(range(0, len(blocks), 4))])
                n_pt += len(row_groups[-1])
            on_dve = lambda j: swa or j == 2
            copies, work, yt_rows = {}, [], []
            n_of = {True: 0, False: 0}
            for r in range(-2, NR + LAG + 1):
                mine = []
                score = row_chunks[r + 2] if r + 2 < NR else []
                flip = row_groups[r] if 0 <= r < NR else []
                gather = row_groups[r - LAG] if 0 <= r - LAG < NR else []
                mine += [("score", r + 2, c) for c in score[:1]]
                for j in range(4):
                    mine += [("gather", r - LAG, g) for g in gather[j:j + 1]]
                    mine += [("flip", r, g) for g in flip[j:j + 1]]
                    if j == 1:
                        mine += [("score", r + 2, c) for c in score[1:]]
                y = r - LAG - 1
                if 0 <= y < NR and (swa or rows[y][0][0] % 2):
                    mine.append(("flip_y", y, None))
                    yt_rows.append(y)
                work.append((r, mine))
                for kind, row, g in mine:
                    if kind in ("flip", "flip_y"):
                        dve = kind == "flip" and on_dve(g[0] - row_groups[row][0][0])
                        copies[kind, row, g and g[0]] = (len(copies), dve, n_of[dve])
                        n_of[dve] += 1
            flips_in_order = list(copies.values())
            NG, NYT, n_dve, n_act = len(copies), len(yt_rows), n_of[True], n_of[False]
            assert NCH % 2 == 0 and NG % 2 == 0

            def before(n, ring, total):
                if n >= ring:
                    return n - ring + 1
                return max(m for m in range(total) if m % ring == n % ring) + 1 - total

            def until(eng, sm, i, per, count):
                assert count > -per
                eng.wait_ge(sm, i * per + (per + count))

            def flip_bank_free(pe, i, order):
                _, dve, n = flips_in_order[order - 2]
                sm, per = (copy_dve, n_dve) if dve else (copy_act, n_act)
                until(pe, sm, i, per, n + 1 - (per if order < 2 else 0))

            def last_flip(r):
                return copies["flip", r, row_groups[r][-1][0]][0] + 1

            def probs(r, g, c, w):
                off = rows[r][g][3] + c
                return (ring_b if swa else Sn)[r % 3][:, off:off + w]

            def head_of(n):
                return n % QUAD // 2 * (SWA_H // KV_H) + n // QUAD * 2 + n % 2 if swa else n

            q_slot = lambda hh: Q_b[hh % len(Q_b)]
            LEAD = 2 if swa else 1
            AHEAD_ROW = 4
            ahead = {}
            for hh in range(QUAD):
                row = hh // 2 * TT + (2 + hh % 2 * 6) if swa else hh * PER_HEADS + AHEAD_ROW
                ahead[row] = hh + LEAD

            def exp_pieces(r):
                sizes = [(qb + 1 - first) * P + (1 if swa else 0) for _, qb, first, _ in rows[r]]
                if len(sizes) == 1:
                    return [(0, c, min(HALF, sizes[0] - c)) for c in range(0, sizes[0], HALF)]
                return [(g, 0, w) for g, w in enumerate(sizes)]

            def woven(flips_, others):
                half = (len(flips_) + 1) // 2
                out = list(flips_[:half])
                rest = list(flips_[half:])
                for o in others:
                    out.append(o)
                    out += rest[:1]
                    rest = rest[1:]
                return out + rest

            block = ctx2.enter_context(nc.Block())

            @block.sync
            def _(sp):
                if swa:
                    sp.dma_start(sinks[:], io["swa_sinks"].to_broadcast([P, SWA_H])).then_inc(bias_in[0], 16)
                def load_raw(x, n, total):
                    if n:
                        sp.wait_ge(split_done[x], n)
                    row0 = {"q": R_QB, "k": R_KB}[x] if swa else {"q": R_Q, "k": R_K}[x]
                    if not swa and n >= total:
                        row0, n = {"q": R_QB, "k": R_KB}[x], n - total
                    row0 += (head_of(min(n, total - 1)) if x == "q" else n) * HD
                    for half in range(2):
                        sp.dma_start(raw[x][half * HD:(half + 1) * HD, :], dram["qk"][row0:row0 + HD, :]
                                     ).then_inc(raw_in[x], 16)

                def load_z(i, pair):
                    zcol = (FW if swa else 0) + head_of(i * QUAD + pair * 2) * HD
                    sp.dma_start(ZY[pair][:], dram["z"][:, zcol:zcol + 2 * HD]
                                 .rearrange("(t p) n -> p t n", p=P)).then_inc(vz_in[pair], 16)

                if swa:
                    for x in "qk":
                        sp.sem_inc(raw_in[x], 64)
                    sp.dma_start(V[0][:], dram["v"][:, FW:FW + KW].rearrange("(t p) n -> p t n", p=P)).then_inc(v_in, 16)
                    load_z(0, 0)
                    load_z(0, 1)
                    for n in range(2, SWA_H + LEAD):
                        load_raw("q", n, SWA_H)
                        if n >= QUAD and n % 2 == 1 and n // 2 < SWA_H // 2:
                            i, pair = n // QUAD, n % QUAD // 2
                            until(sp, yt_done, i, NYT, (pair - 1) * NYT // 2)
                            load_z(i, pair)
                else:
                    for n in range(FOX_H + 2):
                        for x in "qk":
                            load_raw(x, n, FOX_H)
                        if n >= FOX_H:
                            continue
                        i, hh = n // QUAD, n % QUAD
                        until(sp, bias_used, i, QUAD, hh - 1)
                        sp.dma_start(nF[hh % 2][:], dram["f"][n:n + 1, :].to_broadcast([P, S])
                                     ).then_inc(bias_in[hh % 2], 16)
                        if hh % 2 == 0:
                            pair = hh // 2
                            until(sp, pv_group, i, n_pt, (pair - 1) * n_pt // 2)
                            until(sp, yt_done, i, NYT, (pair - 1) * NYT // 2)
                            sp.dma_start(V[pair][:], dram["v"][:, n * HD:(n + 2) * HD]
                                         .rearrange("(t p) n -> p t n", p=P)).then_inc(vz_in[pair], 16)
                            load_z(i, pair)
                    for x in "qk":
                        sp.wait_ge(raw_in[x], 32 * (FOX_H + 2))

            @block.gpsimd
            def _(pool):
                if not swa:
                    pool.memset(mask0, 0.0).then_inc(init, 1)
                    pool.wait_ge(init, 1)
                    pool.affine_select(out=mask0, in_=mask0, compare_op=ALU.is_ge, fill=NEG, base=0,
                                       pattern=[[-1, P]], channel_multiplier=1).then_inc(init, 1)
                else:
                    pool.iota(dist.bitcast(mybir.dt.int32), pattern=[[-1, WIN]], base=P, channel_multiplier=1).then_inc(init, 1)
                    pool.wait_ge(init, 1)

                def low_q(n, hh):
                    pool.wait_ge(hi_done["q"], n + 1)
                    low = q_slot(hh)[HD:P, :]
                    pool.tensor_tensor(low, raw["q"][HD:P, :], low.bitcast(F32), ALU.subtract).then_inc(split_done["q"], 1)
                    pool.wait_ge(split_done["q"], n + 1)

                def low_k(n, u):
                    pool.wait_ge(hi_done["k"], n + 1)
                    pool.tensor_tensor(Kl[:, u, :], raw["k"][:], Kh[:, u, :].bitcast(F32), ALU.subtract
                                       ).then_inc(split_done["k"], 1)
                    pool.wait_ge(split_done["k"], n + 1)

                if swa:
                    for x in "qk":
                        pool.sem_inc(split_done[x], 1)
                    low_k(1, 1)
                with pool.Fori(0, ITER) as i:
                    for hh in ahead.values():
                        low_q(i * QUAD + hh, hh % QUAD)
                        if not swa:
                            low_k(i * QUAD + hh, hh % 2)

            @block.scalar
            def _(act):
                act.sem_inc(copy_act, n_act)
                act.sem_inc(yt_done, NYT)
                def high_q(n, hh):
                    act.wait_ge(raw_in["q"], n * 32 + 32)
                    nc.scalar.activation(q_slot(hh), raw["q"][:], ACT.Copy).then_inc(hi_done["q"], 1)

                def high_k(n, u):
                    act.wait_ge(raw_in["k"], n * 32 + 32)
                    nc.scalar.activation(Kh[:, u, :], raw["k"][:], ACT.Copy).then_inc(hi_done["k"], 1)

                def high(i, hh):
                    part = NCH // (NR // PER_HEADS)
                    if swa:
                        until(act, chunk_ready, i, NCH, (hh // 2 + 1) * part - NCH)
                    else:
                        until(act, chunk_ready, i, NCH, (hh - 1) * part)
                    high_q(i * QUAD + hh, hh % QUAD)

                def exp(i, r, j):
                    if j == 0:
                        until(act, chunk_read, i, NCH, row_chunks[r][-1][0] + 1)
                        until(act, y_done, i, NR, r - 3)
                    g, c, w = exp_pieces(r)[j]
                    p = probs(r, g, c, w)
                    e = nc.scalar.activation(p, p, ACT.Exp, scale=-1.0,
                                             bias=nmax[:, r % 4, g:g + 1], accum_out=rsum[:, r % 4, j:j + 1])
                    if j == len(exp_pieces(r)) - 1:
                        e.then_inc(exp_done, 1)

                def copy(i, r, g):
                    pt, blocks = g
                    order, dve, n = copies["flip", r, pt]
                    if dve:
                        return
                    until(act, flip_done, i, NG, order + 1)
                    until(act, pv_group, i, n_pt, before(pt, 3, n_pt))
                    nc.scalar.activation(PT[pt % 3][:, 0:len(blocks) * P], flips[order % 2][:, 0:len(blocks) * P], ACT.Copy
                                         ).then_inc(copy_act, 1)

                def keep_yt(i, r):
                    order, _, n = copies["flip_y", r, None]
                    hh, qb = rows[r][0][:2]
                    until(act, flip_done, i, NG, order + 1)
                    tile = i + (4 + hh // 2 * 2) if swa else i * 2 + hh // 2
                    w = P if swa else len(rows[r]) * P
                    nc.scalar.activation(yT[:, bass.ds(tile, 1), qb * P:qb * P + w].rearrange("p a n -> p (a n)"),
                                         flips[order % 2][:, 0:w], ACT.Copy).then_inc(copy_act, 1)
                    until(act, copy_act, i, n_act, n + 1)
                    act.sem_inc(yt_done, 1)

                if swa:
                    for x in "qk":
                        act.sem_inc(hi_done[x], 1)
                high_q(LEAD - 1, LEAD - 1)
                high_k(LEAD - 1, LEAD - 1)
                if not swa:
                    act.wait_ge(init, 2)
                    nc.scalar.activation(maskr[:], mask0, ACT.Copy).then_inc(init, 1)
                    nc.scalar.activation(identr[:], keep["ident"][:], ACT.Copy).then_inc(init, 1)
                with act.Fori(0, ITER) as i:
                    for r, mine in work:
                        steps_ = [(copy, row, g) for kind, row, g in mine if kind == "flip"]
                        exps = [(exp, r + 1, j) for j in range(len(exp_pieces(r + 1)))] if 0 <= r + 1 < NR else []
                        for do, row, what in woven(steps_, exps):
                            do(i, row, what)
                        for kind, row, g in mine:
                            if kind == "flip_y":
                                keep_yt(i, row)
                        if r in ahead:
                            high(i + ahead[r] // QUAD, ahead[r] % QUAD)
                        if not swa and r - 1 in ahead:
                            high_k(i * QUAD + ahead[r - 1], ahead[r - 1] % 2)

            @block.tensor
            def _(pe):
                pe.sem_inc(pv_group, n_pt)
                pe.sem_inc(chunk_ready, NCH)
                pe.sem_inc(flip_done, NG)
                if not swa:
                    pe.wait_ge(init, 4)

                def score(i, r, chunk):
                    hh = rows[r][0][0]
                    n, pieces = chunk
                    if r % PER_HEADS == 0:
                        pe.wait_ge(split_done["q"], i * QUAD + (hh + LEAD))
                        pe.wait_ge(split_done["k"], hh // 2 + 1 if swa else i * QUAD + (hh + 1))
                    until(pe, chunk_read, i, NCH, n - 1)
                    for g, c0, width, col in pieces:
                        hh, qb, first, _ = rows[r][g]
                        q = q_slot(hh)[:, qb * P:(qb + 1) * P]
                        u = hh // 2 if swa else hh % 2
                        for c in range(c0, c0 + width, 512):
                            w = min(512, c0 + width - c)
                            diagonal = not swa and c + w == (qb + 1) * P
                            at = col + c - c0
                            out = logits[n % 2][:, at:at + w]
                            k = slice(first * P + c, first * P + c + w)
                            nc.tensor.matmul(out, q, Kh[:, u, k], start=True, stop=False)
                            mm = nc.tensor.matmul(out, q, Kl[:, u, k], start=False, stop=not diagonal)
                            if diagonal:
                                mm = nc.tensor.matmul(logits[n % 2][:, at + w - P:at + w], identr[:], maskr[:],
                                                      start=False, stop=True)
                    mm.then_inc(chunk_ready, 1)

                def flip(i, r, g):
                    pt, blocks = g
                    order, _, _ = copies["flip", r, pt]
                    if g is row_groups[r][0]:
                        pe.wait_ge(exp_done, i * NR + (r + 1))
                    flip_bank_free(pe, i, order)
                    for j, (h, b) in enumerate(blocks):
                        mm = nc.tensor.transpose(flips[order % 2][:, j * P:(j + 1) * P],
                                                 probs(r, h, (b - rows[r][h][2]) * P, P), keep["ident"][:])
                    mm.then_inc(flip_done, 1)

                def gather(i, r, g):
                    pt, blocks = g
                    order, dve, n = copies["flip", r, pt]
                    hh = rows[r][0][0]
                    vslot = 0 if swa else hh // 2
                    vcol = hh // 2 * HD if swa else hh % 2 * HD
                    if r % PER_HEADS == 0 and hh % 2 == 0:
                        if swa:
                            pe.wait_ge(v_in, 16)
                        else:
                            pe.wait_ge(vz_in[vslot], i * 32 + 32)
                    if g is row_groups[r][0]:
                        until(pe, y_done, i, NR, r - 1)
                    if dve:
                        until(pe, copy_dve, i, n_dve, n + 1)
                    else:
                        until(pe, copy_act, i, n_act, n + 1)
                    for j, (h, b) in enumerate(blocks):
                        mm = nc.tensor.matmul(outs[r % 2][:, h * HD:(h + 1) * HD], PT[pt % 3][:, j * P:(j + 1) * P],
                                              V[vslot][:, b, vcol:vcol + HD], start=b == rows[r][h][2], stop=b == rows[r][h][1])
                    mm.then_inc(pv_group, 1)

                def flip_y(i, r, _):
                    order = copies["flip_y", r, None][0]
                    flip_bank_free(pe, i, order)
                    until(pe, y_done, i, NR, r + 1)
                    for j, (hh, qb, _, _) in enumerate(rows[r][:1] if swa else rows[r]):
                        mm = nc.tensor.transpose(flips[order % 2][:, j * P:(j + 1) * P], ZY[hh // 2][:, qb, :], keep["ident"][:])
                    mm.then_inc(flip_done, 1)

                step = {"score": score, "flip": flip, "gather": gather, "flip_y": flip_y}
                with pe.Fori(0, ITER) as i:
                    for _, mine in work:
                        for kind, row, what in mine:
                            step[kind](i, row, what)

            @block.vector
            def _(dve):
                for sm, credits in ((copy_dve, n_dve), (chunk_read, NCH), (y_done, NR), (bias_used, QUAD)):
                    dve.sem_inc(sm, credits)
                steps = Steps(dve, dve_steps)
                dve.wait_ge(hi_done["q"], LEAD)
                low = q_slot(LEAD - 1)[HD:P, :]
                nc.vector.tensor_tensor(low, raw["q"][HD:P, :], low.bitcast(F32), ALU.subtract).then_inc(split_done["q"], 1)
                if not swa:
                    dve.wait_ge(hi_done["k"], 1)
                    nc.vector.tensor_tensor(Kl[:, 0, :], raw["k"][:], Kh[:, 0, :].bitcast(F32), ALU.subtract
                                            ).then_inc(split_done["k"], 1)
                else:
                    dve.wait_ge(init, 1)
                    dve.wait_ge(bias_in[0], 16)
                    steps.settle(nc.vector.tensor_copy(dist, dist.bitcast(mybir.dt.int32)))
                    steps.settle(nc.vector.tensor_scalar(dist_neg, dist, -1.0, None, ALU.mult))
                    steps.settle(nc.vector.tensor_tensor(dist, dist, dist_neg, ALU.max))
                    for rows_, cols in (((0, HD), (0, CHUNK)), ((0, HD), (3 * CHUNK, 4 * CHUNK)), ((HD, P), (0, 2 * CHUNK))):
                        steps.did(nc.vector.memset(dist[rows_[0]:rows_[1], cols[0]:cols[1]], -NEG * 2.0 ** 8))
                    dve.wait_ge(dve_steps, steps.n)
                    for h in range(SWA_H):
                        steps.did(nc.vector.tensor_scalar(bias_b[:, h, :], dist, -(2.0 ** -(8.0 * (h + 1) / SWA_H)), None, ALU.mult))
                    steps.settle(nc.vector.tensor_scalar(sinks[:], sinks[:], -1.0, None, ALU.mult))

                def bias_of(i, hh, c, w):
                    if swa:
                        return bias_b[:, head_of(i * QUAD + hh), WIN - w:WIN]
                    return nF[hh % 2][:, c:c + w]

                def prepare(i, r):
                    hh = rows[r][0][0]
                    if r % PER_HEADS == 0 and not swa:
                        dve.wait_ge(bias_in[hh % 2], i * 32 + 16 * (hh // 2 + 1))
                    p = before(r, 3, NR)
                    until(dve, flip_done, i, NG, last_flip(p - 1) if p > 0 else last_flip(p - 1 + NR) - NG)
                    if swa:
                        w, h = (rows[r][0][1] + 1 - rows[r][0][2]) * P, head_of(i * QUAD + hh)
                        steps.did(nc.vector.tensor_copy(ring_b[r % 3].rearrange("p (g n) -> p g n", g=2)[:, :, w:w + 1],
                                                        sinks[:, h:h + 2].unsqueeze(2)))

                def take(i, r, j):
                    if j == 0:
                        prepare(i, r)
                    n, pieces = row_chunks[r][j]
                    until(dve, chunk_ready, i, NCH, n + 1)
                    for g, c, w, col in pieces:
                        m = nmax[:, r % 4, g:g + 1]
                        if c:
                            until(dve, chunk_read, i, NCH, n)
                        h = head_of(i * QUAD + rows[r][0][0]) + g
                        start = sinks[:, h:h + 1] if swa else m if c else -NEG
                        t = nc.vector.tensor_tensor_reduce(out=probs(r, g, c, w), in0=logits[n % 2][:, col:col + w],
                                                           in1=bias_of(i, rows[r][g][0], c, w), scale=-1.0, scalar=start,
                                                           op0=ALU.add, op1=ALU.min, accum_out=m)
                    t.then_inc(chunk_read, 1)
                    if j < len(row_chunks[r]) - 1:
                        return
                    if r % PER_HEADS == PER_HEADS - 1 and not swa:
                        until(dve, chunk_read, i, NCH, row_chunks[r][-1][0] + 1)
                        dve.sem_inc(bias_used, 1)

                def copy(i, r, g):
                    pt, blocks = g
                    order, mine, n = copies["flip", r, pt]
                    if not mine:
                        return
                    until(dve, flip_done, i, NG, order + 1)
                    until(dve, pv_group, i, n_pt, before(pt, 3, n_pt))
                    nc.vector.tensor_copy(PT[pt % 3][:, 0:len(blocks) * P], flips[order % 2][:, 0:len(blocks) * P]
                                          ).then_inc(copy_dve, 1)

                def finish(i, r):
                    hh, parts = rows[r][0][0], len(rows[r])
                    dve.wait_ge(exp_done, i * NR + (r + 1))
                    if len(exp_pieces(r)) > parts:
                        total = rinv[:, r % 2, 1:2]
                        steps.settle(nc.vector.tensor_tensor(total, rsum[:, r % 4, 0:1], rsum[:, r % 4, 1:2], ALU.add))
                    else:
                        total = rsum[:, r % 4, 0:parts]
                    steps.settle(nc.vector.reciprocal(rinv[:, r % 2, 0:parts], total))
                    if r % PER_HEADS == 0 and hh % 2 == 0:
                        dve.wait_ge(vz_in[hh // 2], (i + 1) * (16 if swa else 32))
                    until(dve, pv_group, i, n_pt, row_groups[r][-1][0] + 1)
                    for g, (hh, qb, _, _) in enumerate(rows[r]):
                        y = ZY[hh // 2][:, qb, hh % 2 * HD:(hh % 2 + 1) * HD]
                        o = nc.vector.scalar_tensor_tensor(out=y, in0=outs[r % 2][:, g * HD:(g + 1) * HD],
                                                           scalar=rinv[:, r % 2, g:g + 1], in1=y, op0=ALU.mult, op1=ALU.mult)
                    o.then_inc(y_done, 1)

                for i in range(ITER):
                    for r, mine in work:
                        steps_ = [(copy, row, g) for kind, row, g in mine if kind == "flip"]
                        takes = [(take, r + 2, j) for j in range(len(row_chunks[r + 2]))] if r + 2 < NR else []
                        for do, row, what in woven(steps_, takes):
                            do(i, row, what)
                        if 0 <= r - LAG < NR:
                            finish(i, r - LAG)

        for tag, swa in (("a", False), ("b", True)):
            with ExitStack() as ctx2:
                part(tag, swa)

def split_rows(nc, ctx, tag, sources, ring, Wh, Wl, early=()):
    RING = len(ring)
    EARLY = len(early)
    w_in = [*early, *(ctx.enter_context(nc.semaphore(f"{tag}_win{k}")) for k in range(EARLY, RING))]
    w_hi, w_split = (ctx.enter_context(nc.semaphore(f"{tag}_{n}")) for n in ("whi", "wsplit"))

    def load(sp):
        for k, src in enumerate(sources):
            if k < EARLY:
                continue
            if k >= RING:
                sp.wait_ge(w_split, k - RING + 1)
            sp.dma_start(ring[k % RING], src).then_inc(w_in[k % RING], 16)

    def high(act, k):
        act.wait_ge(w_in[k % RING], 16 * (k // RING + 1))
        nc.scalar.activation(Wh[:, k, :], ring[k % RING], ACT.Copy).then_inc(w_hi, 1)

    def low(dve, k):
        dve.wait_ge(w_hi, k + 1)
        nc.vector.tensor_tensor(Wl[:, k, :], ring[k % RING], Wh[:, k, :].bitcast(F32), ALU.subtract).then_inc(w_split, 1)

    return load, high, low, w_split

def merge(nc, io, keep, dram):
    ctx = ExitStack()
    sb = lambda name, shape, dt=F32: ctx.enter_context(nc.sbuf_tensor(name, shape, dt))
    sem = lambda name: ctx.enter_context(nc.semaphore(name))
    yT = keep["yT"]
    TB = 256
    NB, BK = S // TB, FW // P
    with ctx:
        Wh, Wl = sb("woh", [P, KT, D], F32R), sb("wol", [P, KT, D], F32R)
        yh, yl = ([sb(f"{n}{k}", [P, KT, TB], F32R) for k in range(2)] for n in ("yh", "yl"))
        gates = [sb(f"gt{k}", [P, 2, KT, TB]) for k in range(2)]
        ta, tb_ = [sb(f"ta{k}", [P, TB]) for k in range(2)], [sb(f"tb{k}", [P, TB]) for k in range(2)]
        pa = [ctx.enter_context(nc.psum_tensor(f"pa{k}", [P, 512], F32)) for k in range(4)]
        pb = [ctx.enter_context(nc.psum_tensor(f"pb{k}", [P, 512], F32)) for k in range(4)]
        sources = [io["w_o_fox"][0, k * P:(k + 1) * P, :] for k in range(BK)] + \
                  [io["w_o_swa"][0, k * P:(k + 1) * P, :] for k in range(BK)]
        spare = gates[1].rearrange("p a k n -> p (a k n)")
        ring = [t[:] for t in keep["w_raw"]] + [spare[:, c:c + D] for c in range(0, 2 * KT * TB, D)]
        load, high, low, w_split = split_rows(nc, ctx, "m", sources, ring, Wh, Wl)
        gate_in = [sem(f"m_g{k}") for k in range(2)]
        y_hi, y_split, mm_done, gated, merged = sem("m_yhi"), sem("m_ysplit"), sem("m_mm"), sem("m_gated"), sem("m_merged")
        block = ctx.enter_context(nc.Block())

        PER = 2 * KT

        @block.sync
        def _(sp):
            load(sp)

            def load_gates(i, u):
                sp.wait_ge(merged, i * PER + (u + 1) * KT)
                for half in range(2):
                    sp.dma_start(gates[u][:, half, :, :],
                                 dram["g"][half * D:(half + 1) * D, bass.ds(i * 2 * TB + u * TB, TB)]
                                 .rearrange("(k p) n -> p k n", p=P)).then_inc(gate_in[u], 16)

            load_gates(0, 0)
            sp.wait_ge(w_split, KT)
            load_gates(0, 1)
            with sp.Fori(0, NB // 2 - 1) as i:
                for u in range(2):
                    load_gates(i + 1, u)
            for k, (tile, loaded) in enumerate(zip(keep["w_raw"], keep["w_out_in"])):
                sp.dma_start(tile[:], io["w_out"][0, k * P:(k + 1) * P, :]).then_inc(loaded, 16)

        @block.gpsimd
        def _(pool):
            with pool.Fori(0, NB // 2) as i:
                for u in range(2):
                    pool.wait_ge(y_hi, i * 2 + (u + 1))
                    pool.tensor_tensor(yl[u][:], yT[:, :, bass.ds(i * 2 * TB + u * TB, TB)], yh[u][:].bitcast(F32),
                                       ALU.subtract).then_inc(y_split, 1)

        @block.tensor
        def _(pe):
            def three(bank, u, m, k, k0):
                c = slice(m * P, (m + 1) * P)
                nc.tensor.matmul(bank, Wh[:, k, c], yh[u][:, k, :], start=k == k0, stop=False)
                nc.tensor.matmul(bank, Wh[:, k, c], yl[u][:, k, :], start=False, stop=False)
                return nc.tensor.matmul(bank, Wl[:, k, c], yh[u][:, k, :], start=False, stop=k == k0 + BK - 1)

            def pair(i, u, m):
                n = u * KT + m
                pe.wait_ge(merged, i * PER + (PER + n - 3))
                for bank, k0 in ((pa, 0), (pb, BK)):
                    for k in range(k0, k0 + BK):
                        mm = three(bank[n % 4][:, 0:TB], u, m, k, k0)
                mm.then_inc(mm_done, 1)

            pe.wait_ge(y_split, 1)
            for k in range(KT):
                pe.wait_ge(w_split, k + 1)
                for m in range(4):
                    mm = three((pa if k < BK else pb)[m][:, 0:TB], 0, m, k, k // BK * BK)
                    if k == KT - 1:
                        mm.then_inc(mm_done, 1)
            for m in range(4, KT):
                pair(0, 0, m)
            pe.wait_ge(y_split, 2)
            for m in range(KT):
                pair(0, 1, m)
            with pe.Fori(0, NB // 2 - 1) as i:
                for u in range(2):
                    pe.wait_ge(y_split, i * 2 + (u + 3))
                    for m in range(KT):
                        pair(i + 1, u, m)

        @block.scalar
        def _(act):
            def high_y(i, u):
                act.wait_ge(merged, i * PER + (u + 1) * KT)
                nc.scalar.activation(yh[u][:], yT[:, :, bass.ds(i * 2 * TB + u * TB, TB)], ACT.Copy).then_inc(y_hi, 1)

            high_y(0, 0)
            for k in range(KT):
                high(act, k)
            high_y(0, 1)
            with act.Fori(0, NB // 2 - 1) as i:
                for u in range(2):
                    high_y(i + 1, u)

        @block.vector
        def _(dve):
            dve.sem_inc(merged, PER)
            for k in range(KT):
                low(dve, k)
            with dve.Fori(0, NB // 2) as i:
                for u in range(2):
                    dve.wait_ge(gate_in[u], i * 32 + 32)
                    for m in range(KT):
                        n = u * KT + m
                        dve.wait_ge(mm_done, i * 2 * KT + (n + 1))
                        dve.wait_ge(merged, i * PER + (PER + n - 1))
                        nc.vector.tensor_tensor(ta[n % 2][:], pa[n % 4][:, 0:TB], gates[u][:, 0, m, :], ALU.mult)
                        nc.vector.tensor_tensor(tb_[n % 2][:], pb[n % 4][:, 0:TB], gates[u][:, 1, m, :], ALU.mult).then_inc(gated, 1)
                        dve.wait_ge(gated, i * PER + (n + 1))
                        nc.vector.tensor_tensor(yT[:, m, bass.ds(i * 2 * TB + u * TB, TB)], ta[n % 2][:], tb_[n % 2][:],
                                                ALU.add).then_inc(merged, 1)

def output(nc, io, keep, dram, out):
    ctx = ExitStack()
    sb = lambda name, shape, dt=F32: ctx.enter_context(nc.sbuf_tensor(name, shape, dt))
    sem = lambda name: ctx.enter_context(nc.semaphore(name))
    yT = keep["yT"]
    N = 512
    with ctx:
        Wh, Wl = sb("wuh", [P, KT, D], F32R), sb("wul", [P, KT, D], F32R)
        mh, ml = ([sb(f"{n}{k}", [P, KT, P], F32R) for k in range(2)] for n in ("mh", "ml"))
        x_in = [sb(f"xo{k}", [P, D]) for k in range(3)]
        o = [sb(f"o{k}", [P, D]) for k in range(2)]
        gate = sb("gate", [P, D])
        po = [ctx.enter_context(nc.psum_tensor(f"po{k}", [P, D], F32)) for k in range(2)]
        ring = [t[:] for t in keep["w_raw"]] + [sb(f"o_raw{k}", [P, D])[:] for k in range(2, KT)]
        load, high, low, w_split = split_rows(nc, ctx, "o", [io["w_out"][0, k * P:(k + 1) * P, :] for k in range(KT)], ring, Wh, Wl,
                                              keep["w_out_in"])
        gate_in, x_sem = sem("o_gate"), [sem(f"o_x{k}") for k in range(3)]
        m_hi, m_split, mm_done, scaled, added = sem("o_mhi"), sem("o_msplit"), sem("o_mm"), sem("o_scaled"), sem("o_added")
        stored = [sem(f"o_st{k}") for k in range(2)]
        block = ctx.enter_context(nc.Block())

        @block.sync
        def _(sp):
            load(sp)
            sp.dma_start(gate[:], dram["gate"].to_broadcast([P, D])).then_inc(gate_in, 16)
            for t in range(TT):
                sp.wait_ge(added, t + 1)
                sp.dma_start(out[0, t * P:(t + 1) * P, :], o[t % 2][:]).then_inc(stored[t % 2], 16)
            for k in range(2):
                sp.wait_ge(stored[k], 16 * TT // 2)

        @block.gpsimd
        def _(pool):
            for t in range(TT):
                if t >= 3:
                    pool.wait_ge(added, t - 2)
                pool.dma_start(x_in[t % 3][:], io["x"][0, t * P:(t + 1) * P, :]).then_inc(x_sem[t % 3], 16)

        @block.tensor
        def _(pe):
            def three(t, h, k):
                u, c = t % 2, slice(h * N, (h + 1) * N)
                bank = po[u][:, c]
                nc.tensor.matmul(bank, mh[u][:, k, :], Wh[:, k, c], start=k == 0, stop=False)
                nc.tensor.matmul(bank, mh[u][:, k, :], Wl[:, k, c], start=False, stop=False)
                return nc.tensor.matmul(bank, ml[u][:, k, :], Wh[:, k, c], start=False, stop=k == KT - 1)

            pe.wait_ge(m_split, 2)
            for k in range(KT):
                pe.wait_ge(w_split, k + 1)
                for t in range(2):
                    for h in range(D // N):
                        mm = three(t, h, k)
                    if k == KT - 1:
                        mm.then_inc(mm_done, 1)
            for t in range(2, TT):
                pe.wait_ge(m_split, t + 1)
                pe.wait_ge(scaled, t - 1)
                for h in range(D // N):
                    for k in range(KT):
                        mm = three(t, h, k)
                mm.then_inc(mm_done, 1)

        def tile_of(t):
            return yT[:, :, t * P:(t + 1) * P]

        @block.scalar
        def _(act):
            def high_m(t):
                if t >= 2:
                    act.wait_ge(mm_done, t - 1)
                nc.scalar.activation(mh[t % 2][:], tile_of(t), ACT.Copy).then_inc(m_hi, 1)

            high_m(0)
            high_m(1)
            for k in range(KT):
                high(act, k)
            for t in range(2, TT):
                high_m(t)

        @block.vector
        def _(dve):
            def low_m(t):
                dve.wait_ge(m_hi, t + 1)
                nc.vector.tensor_tensor(ml[t % 2][:], tile_of(t), mh[t % 2][:].bitcast(F32), ALU.subtract).then_inc(m_split, 1)

            low_m(0)
            low_m(1)
            for k in range(KT):
                low(dve, k)
            dve.wait_ge(gate_in, 16)
            for t in range(TT):
                dve.wait_ge(mm_done, t + 1)
                if t >= 2:
                    dve.wait_ge(stored[t % 2], 16 * (t // 2))
                nc.vector.tensor_tensor(o[t % 2][:], po[t % 2][:], gate[:], ALU.mult).then_inc(scaled, 1)
                if t + 2 < TT:
                    low_m(t + 2)
                dve.wait_ge(scaled, t + 1)
                dve.wait_ge(x_sem[t % 3], 16 * (t // 3 + 1))
                nc.vector.tensor_tensor(o[t % 2][:], o[t % 2][:], x_in[t % 3][:], ALU.add).then_inc(added, 1)

def build(nc, io, out):
    scratch = lambda name, shape: nc.dram_tensor(name, shape, F32).ap()
    dram = {
        "qk": scratch("qk_scratch", [2 * FW + SW + KW, S]),
        "v": scratch("v_scratch", [S, FW + KW]),
        "z": scratch("z_scratch", [S, FW + SW]),
        "g": scratch("g_scratch", [2 * D, S]),
        "f": scratch("f_scratch", [FOX_H, S]),
        "gate": scratch("gate_scratch", [1, D]),
    }
    with ExitStack() as ctx:
        keep = {"ident": ctx.enter_context(nc.sbuf_tensor("ident", [P, P], F32)),
                "siluc": ctx.enter_context(nc.sbuf_tensor("siluc", [P, KT], F32))}
        with ExitStack() as early:
            keep["hTh"] = early.enter_context(nc.sbuf_tensor("hTh", [P, KT, S], F32R))
            keep["hTl"] = early.enter_context(nc.sbuf_tensor("hTl", [P, KT, S], F32R))
            keep["wraw"] = [early.enter_context(nc.sbuf_tensor(f"wraw{k}", [P, COLS], F32)) for k in range(RAW)]
            keep["w_in"] = [ctx.enter_context(nc.semaphore(f"w_in{k}")) for k in range(RAW)]
            condition_and_norm(nc, io, keep)
            project(nc, io, keep, dram)
        keep["yT"] = ctx.enter_context(nc.sbuf_tensor("yT", [P, KT, S], F32))
        attend(nc, io, keep, dram)
        keep["w_raw"] = [ctx.enter_context(nc.sbuf_tensor(f"w_raw{k}", [P, D], F32)) for k in range(2)]
        keep["w_out_in"] = [ctx.enter_context(nc.semaphore(f"w_out_in{k}")) for k in range(2)]
        merge(nc, io, keep, dram)
        output(nc, io, keep, dram, out)

_INS = ["x", "c", "w_ada", "b_ada", "norm_g", "w_in", "b_forget", "fox_q_g", "fox_k_g", "w_o_fox",
        "swa_q_g", "swa_k_g", "swa_sinks", "w_o_swa", "w_out"]

def kernel(**inputs):
    import numpy as _np
    import concourse.bacc as _bacc
    from concourse import mybir as _mybir
    from concourse.bass_utils import run_bass_kernel_spmd as _run

    nc = _bacc.Bacc("TRN2", target_bir_lowering=False, num_devices=1)
    arrays, io = {}, {}
    for name in _INS:
        a = _np.ascontiguousarray(inputs[name])
        arrays[f"in_{name}"] = a
        io[name] = nc.dram_tensor(f"in_{name}", a.shape, _mybir.dt.from_np(a.dtype), kind="ExternalInput").ap()
    out = nc.dram_tensor("out", (1, S, D), F32, kind="ExternalOutput").ap()
    build(nc, io, out)
    return _run(nc, [arrays], core_ids=[0]).results[0]["out"]
```
